# Optimizing a Trainium2 kernel written in Bass

```python
import math
import jax, jax.numpy as jnp
from jax import lax
import numpy as np

"""One inference step of a YOCO-style hybrid decoder trunk (DEPTH layers) for two request groups.

Layers 0..N_A-1: pre-RMSNorm Griffin recurrent block (GeLU gate branch x [width-4 causal depthwise conv -> RG-LRU] branch) + pre-RMSNorm gated ConvFFN.
After layer N_A-1 (incl. its ConvFFN) ONE shared K/V (GQA, QK-normed keys) is projected from the residual stream.
Layers N_A..DEPTH-1: pre-RMSNorm sliding-window (128) GQA with learned per-head sinks, per-head QK RMSNorm and a shared
T5 relative-position bias, attending to the shared K/V; + pre-RMSNorm gated ConvFFN.

Inputs: x_prompt (BATCH, SEQ, D_MODEL), x_sample (DEC_BATCH, DEC_SEQ, D_MODEL),
  state_lru_h (N_A, DEC_BATCH, D_RNN), state_lru_conv (N_A, DEC_BATCH, CONV_W-1, D_RNN),
  state_ffn_conv (DEPTH, DEC_BATCH, FFN_CONV_W-1, D_FF),
  cache_k_win / cache_v_win (DEC_BATCH, WINDOW, N_KV_HEADS, HEAD_DIM) = shared K/V of positions PAST_LEN-WINDOW..PAST_LEN-1,
  then weights.
Returns (y_prompt (BATCH,SEQ,D), y_sample (DEC_BATCH,DEC_SEQ,D),
  lru_h_p (N_A,BATCH,D_RNN), lru_conv_p (N_A,BATCH,CONV_W-1,D_RNN), ffn_conv_p (DEPTH,BATCH,FFN_CONV_W-1,D_FF),
  k_win_p (BATCH,WINDOW,N_KV_HEADS,HEAD_DIM), v_win_p (same),
  lru_h_s (N_A,DEC_BATCH,D_RNN), lru_conv_s (N_A,DEC_BATCH,CONV_W-1,D_RNN), ffn_conv_s (DEPTH,DEC_BATCH,FFN_CONV_W-1,D_FF),
  k_win_s (DEC_BATCH,WINDOW,N_KV_HEADS,HEAD_DIM), v_win_s (same)).
"""

D_MODEL = 1024
BATCH = 1
SEQ = 1024
DEPTH = 2
DEC_BATCH = 8
DEC_SEQ = 8
PAST_LEN = 2048
PAGE_SIZE = 128

N_A = DEPTH // 2
N_B = DEPTH - N_A
D_RNN = D_MODEL
N_LRU_BLOCKS = 4
LRU_BW = D_RNN // N_LRU_BLOCKS
CONV_W = 4
C_GATE = 8.0
N_HEADS = 16
N_KV_HEADS = 4
HEAD_DIM = 64
GROUP = N_HEADS // N_KV_HEADS
WINDOW = 128
ATTN_BLOCK = WINDOW
N_BUCKETS = 32
MAX_DISTANCE = 128
D_FF = 3 * D_MODEL
FFN_CONV_W = 3
EPS = 1e-6
NEG_INF = -1e30

kernel_name = "yoco_rglru_swa_sink_convffn_step"

def rmsnorm(x, g):
    xf = x.astype(jnp.float32)
    y = xf * lax.rsqrt(jnp.mean(xf * xf, axis=-1, keepdims=True) + EPS)
    return (y * g.astype(jnp.float32)).astype(x.dtype)

def causal_dwconv(x, buf, w, b):
    T = x.shape[1]
    W = w.shape[0]
    xp = jnp.concatenate([buf.astype(x.dtype), x], axis=1)
    y = b
    for k in range(W):
        y = y + w[k] * xp[:, k:k + T]
    return y, xp[:, T:]

def lru_scan(a, b, h0):
    def step(h, ab):
        a_t, b_t = ab
        h = a_t * h + b_t
        return h, h
    h_last, hs = lax.scan(step, h0, (jnp.swapaxes(a, 0, 1), jnp.swapaxes(b, 0, 1)))
    return jnp.swapaxes(hs, 0, 1), h_last

def rglru_block(xn, h0, conv_buf, w_in, conv_w, conv_b, gr_w, gr_b, gi_w, gi_b, lam, w_out):
    B, T, _ = xn.shape
    u = xn @ w_in
    gate, xb = u[..., :D_RNN], u[..., D_RNN:]
    xc, new_buf = causal_dwconv(xb, conv_buf, conv_w, conv_b)
    xblk = xc.reshape(B, T, N_LRU_BLOCKS, LRU_BW)
    r = jax.nn.sigmoid(jnp.einsum('btnc,ncd->btnd', xblk, gr_w).reshape(B, T, D_RNN) + gr_b)
    i = jax.nn.sigmoid(jnp.einsum('btnc,ncd->btnd', xblk, gi_w).reshape(B, T, D_RNN) + gi_b)
    log_a = -C_GATE * r.astype(jnp.float32) * jax.nn.softplus(-lam.astype(jnp.float32))
    a = jnp.exp(log_a)
    b = jnp.sqrt(-jnp.expm1(2.0 * log_a)) * (i * xc).astype(jnp.float32)
    hs, h_last = lru_scan(a, b, h0.astype(jnp.float32))
    y = (jax.nn.gelu(gate) * hs.astype(xn.dtype)) @ w_out
    return y, h_last.astype(h0.dtype), new_buf.astype(conv_buf.dtype)

def conv_ffn(xn, buf, w_up, conv_w, conv_b, w_down):
    u = xn @ w_up
    g, v = u[..., :D_FF], u[..., D_FF:]
    gc, new_buf = causal_dwconv(g, buf, conv_w, conv_b)
    return (jax.nn.gelu(gc) * v) @ w_down, new_buf.astype(buf.dtype)

def rel_bucket(dist):
    max_exact = N_BUCKETS // 2
    d = jnp.maximum(dist, 0)
    df = jnp.maximum(d, 1).astype(jnp.float32)
    large = max_exact + (jnp.log(df / max_exact) / math.log(MAX_DISTANCE / max_exact)
                         * (N_BUCKETS - max_exact)).astype(jnp.int32)
    large = jnp.minimum(large, N_BUCKETS - 1)
    return jnp.where(d < max_exact, d, large)

def rel_bias_heads(rel_bias, dist):
    b = rel_bias.astype(jnp.float32)[rel_bucket(dist)]
    Q, S = dist.shape
    return jnp.moveaxis(b, -1, 0).reshape(N_KV_HEADS, GROUP, Q, S)

def sink_softmax(scores, sinks):
    s = sinks.astype(jnp.float32)[:, :, None]
    m = jnp.maximum(jnp.max(scores, axis=-1), s)
    p = jnp.exp(scores - m[..., None])
    denom = jnp.sum(p, axis=-1) + jnp.exp(s - m)
    return p / denom[..., None]

def swa_prompt(q, k, v, sinks, rel_bias):
    B, S = q.shape[0], q.shape[1]
    nb = S // ATTN_BLOCK
    qb = q.reshape(B, nb, ATTN_BLOCK, N_KV_HEADS, GROUP, HEAD_DIM)
    kc = k.reshape(B, nb, ATTN_BLOCK, N_KV_HEADS, HEAD_DIM)
    vc = v.reshape(B, nb, ATTN_BLOCK, N_KV_HEADS, HEAD_DIM)
    kb = jnp.concatenate([jnp.concatenate([jnp.zeros_like(kc[:, :1]), kc[:, :-1]], axis=1), kc], axis=2)
    vb = jnp.concatenate([jnp.concatenate([jnp.zeros_like(vc[:, :1]), vc[:, :-1]], axis=1), vc], axis=2)
    scores = jnp.einsum('bnqkgd,bnskd->bnkgqs', qb, kb,
                        preferred_element_type=jnp.float32) * (HEAD_DIM ** -0.5)
    qi = jnp.arange(ATTN_BLOCK)[:, None]
    sj = jnp.arange(2 * ATTN_BLOCK)[None, :]
    dist = qi + ATTN_BLOCK - sj
    band = (dist >= 0) & (dist < WINDOW)
    has_prev = (jnp.arange(nb)[:, None, None] > 0) | (sj >= ATTN_BLOCK)[None]
    valid = band[None] & has_prev
    scores = jnp.where(valid[None, :, None, None], scores + rel_bias_heads(rel_bias, dist), NEG_INF)
    probs = sink_softmax(scores, sinks.reshape(N_KV_HEADS, GROUP))
    out = jnp.einsum('bnkgqs,bnskd->bnqkgd', probs.astype(v.dtype), vb)
    return out.reshape(B, S, N_HEADS * HEAD_DIM)

def swa_sample(q, k_all, v_all, sinks, rel_bias):
    DB, T = q.shape[0], q.shape[1]
    L = k_all.shape[1]
    W = L - T
    qg = q.reshape(DB, T, N_KV_HEADS, GROUP, HEAD_DIM)
    scores = jnp.einsum('btkgd,bskd->bkgts', qg, k_all,
                        preferred_element_type=jnp.float32) * (HEAD_DIM ** -0.5)
    dist = jnp.arange(T)[:, None] + W - jnp.arange(L)[None, :]
    valid = (dist >= 0) & (dist < WINDOW)
    scores = jnp.where(valid, scores + rel_bias_heads(rel_bias, dist), NEG_INF)
    probs = sink_softmax(scores, sinks.reshape(N_KV_HEADS, GROUP))
    out = jnp.einsum('bkgts,bskd->btkgd', probs.astype(v_all.dtype), v_all)
    return out.reshape(DB, T, N_HEADS * HEAD_DIM)

def shared_kv(x, kv_norm, w_kv, b_kv, k_norm):
    B, T, _ = x.shape
    kv = rmsnorm(x, kv_norm) @ w_kv + b_kv
    hkv = N_KV_HEADS * HEAD_DIM
    k = rmsnorm(kv[..., :hkv].reshape(B, T, N_KV_HEADS, HEAD_DIM), k_norm)
    v = kv[..., hkv:].reshape(B, T, N_KV_HEADS, HEAD_DIM)
    return k, v

def trunk(x, lru_h, lru_conv, ffn_conv, win_k, win_v, P, prompt):
    B, T, _ = x.shape
    new_h, new_c, new_f = [], [], []
    k = v = new_k = new_v = None
    for layer in range(DEPTH):
        if layer < N_A:
            i = layer
            y, h_i, c_i = rglru_block(rmsnorm(x, P['a_norm'][i]), lru_h[i], lru_conv[i],
                                      P['a_w_in'][i], P['a_conv_w'][i], P['a_conv_b'][i],
                                      P['a_gate_r_w'][i], P['a_gate_r_b'][i],
                                      P['a_gate_i_w'][i], P['a_gate_i_b'][i],
                                      P['a_lambda'][i], P['a_w_out'][i])
            new_h.append(h_i)
            new_c.append(c_i)
        else:
            j = layer - N_A
            q = rmsnorm(x, P['b_norm'][j]) @ P['w_q'][j] + P['b_q'][j]
            q = rmsnorm(q.reshape(B, T, N_HEADS, HEAD_DIM), P['q_norm'][j])
            if prompt:
                o = swa_prompt(q, k, v, P['sinks'][j], P['rel_bias'])
            else:
                o = swa_sample(q, k, v, P['sinks'][j], P['rel_bias'])
            y = o @ P['w_o'][j] + P['b_o'][j]
        x = x + y
        f, f_i = conv_ffn(rmsnorm(x, P['f_norm'][layer]), ffn_conv[layer], P['f_w_up'][layer],
                          P['f_conv_w'][layer], P['f_conv_b'][layer], P['f_w_down'][layer])
        new_f.append(f_i)
        x = x + f
        if layer == N_A - 1:
            k, v = shared_kv(x, P['kv_norm'], P['w_kv'], P['b_kv'], P['k_norm'])
            if not prompt:
                k = jnp.concatenate([win_k.astype(k.dtype), k], axis=1)
                v = jnp.concatenate([win_v.astype(v.dtype), v], axis=1)
            new_k = k[:, -WINDOW:]
            new_v = v[:, -WINDOW:]
    return x, jnp.stack(new_h), jnp.stack(new_c), jnp.stack(new_f), new_k, new_v

def setup_inputs(seed: int = 0) -> dict:
    key = jax.random.key(seed)
    ks = iter(jax.random.split(key, 48))

    def nrm(shape, scale):
        return scale * jax.random.normal(next(ks), shape, jnp.float32)

    def gain(shape):
        return 1.0 + nrm(shape, 0.05)

    HQ = N_HEADS * HEAD_DIM
    HKV = N_KV_HEADS * HEAD_DIM
    a_c = jax.random.uniform(next(ks), (N_A, D_RNN), jnp.float32, 0.9, 0.999)
    a_base = jnp.exp(jnp.log(a_c) / C_GATE)
    a_lambda = jnp.log(a_base) - jnp.log1p(-a_base)
    return {
        "x_prompt": nrm((BATCH, SEQ, D_MODEL), 1.0),
        "x_sample": nrm((DEC_BATCH, DEC_SEQ, D_MODEL), 1.0),
        "state_lru_h": nrm((N_A, DEC_BATCH, D_RNN), 0.5),
        "state_lru_conv": nrm((N_A, DEC_BATCH, CONV_W - 1, D_RNN), 0.5),
        "state_ffn_conv": nrm((DEPTH, DEC_BATCH, FFN_CONV_W - 1, D_FF), 0.5),
        "cache_k_win": nrm((DEC_BATCH, WINDOW, N_KV_HEADS, HEAD_DIM), 1.0),
        "cache_v_win": nrm((DEC_BATCH, WINDOW, N_KV_HEADS, HEAD_DIM), 1.0),
        "a_norm": gain((N_A, D_MODEL)),
        "a_w_in": nrm((N_A, D_MODEL, 2 * D_RNN), D_MODEL ** -0.5),
        "a_conv_w": nrm((N_A, CONV_W, D_RNN), CONV_W ** -0.5),
        "a_conv_b": nrm((N_A, D_RNN), 0.02),
        "a_gate_r_w": nrm((N_A, N_LRU_BLOCKS, LRU_BW, LRU_BW), LRU_BW ** -0.5),
        "a_gate_r_b": nrm((N_A, D_RNN), 0.02),
        "a_gate_i_w": nrm((N_A, N_LRU_BLOCKS, LRU_BW, LRU_BW), LRU_BW ** -0.5),
        "a_gate_i_b": nrm((N_A, D_RNN), 0.02),
        "a_lambda": a_lambda,
        "a_w_out": nrm((N_A, D_RNN, D_MODEL), D_RNN ** -0.5),
        "kv_norm": gain((D_MODEL,)),
        "w_kv": nrm((D_MODEL, 2 * HKV), D_MODEL ** -0.5),
        "b_kv": nrm((2 * HKV,), 0.02),
        "k_norm": gain((HEAD_DIM,)),
        "b_norm": gain((N_B, D_MODEL)),
        "w_q": nrm((N_B, D_MODEL, HQ), D_MODEL ** -0.5),
        "b_q": nrm((N_B, HQ), 0.02),
        "q_norm": gain((N_B, HEAD_DIM)),
        "sinks": nrm((N_B, N_HEADS), 0.5),
        "w_o": nrm((N_B, HQ, D_MODEL), HQ ** -0.5),
        "b_o": nrm((N_B, D_MODEL), 0.02),
        "rel_bias": nrm((N_BUCKETS, N_HEADS), 0.5),
        "f_norm": gain((DEPTH, D_MODEL)),
        "f_w_up": nrm((DEPTH, D_MODEL, 2 * D_FF), D_MODEL ** -0.5),
        "f_conv_w": nrm((DEPTH, FFN_CONV_W, D_FF), FFN_CONV_W ** -0.5),
        "f_conv_b": nrm((DEPTH, D_FF), 0.02),
        "f_w_down": nrm((DEPTH, D_FF, D_MODEL), D_FF ** -0.5),
    }

def reference(x_prompt, x_sample, state_lru_h, state_lru_conv, state_ffn_conv, cache_k_win, cache_v_win,
              a_norm, a_w_in, a_conv_w, a_conv_b, a_gate_r_w, a_gate_r_b, a_gate_i_w, a_gate_i_b,
              a_lambda, a_w_out, kv_norm, w_kv, b_kv, k_norm, b_norm, w_q, b_q, q_norm, sinks,
              w_o, b_o, rel_bias, f_norm, f_w_up, f_conv_w, f_conv_b, f_w_down):
    P = dict(a_norm=a_norm, a_w_in=a_w_in, a_conv_w=a_conv_w, a_conv_b=a_conv_b,
             a_gate_r_w=a_gate_r_w, a_gate_r_b=a_gate_r_b, a_gate_i_w=a_gate_i_w, a_gate_i_b=a_gate_i_b,
             a_lambda=a_lambda, a_w_out=a_w_out, kv_norm=kv_norm, w_kv=w_kv, b_kv=b_kv, k_norm=k_norm,
             b_norm=b_norm, w_q=w_q, b_q=b_q, q_norm=q_norm, sinks=sinks, w_o=w_o, b_o=b_o,
             rel_bias=rel_bias, f_norm=f_norm, f_w_up=f_w_up, f_conv_w=f_conv_w, f_conv_b=f_conv_b,
             f_w_down=f_w_down)
    B = x_prompt.shape[0]
    dt = x_prompt.dtype
    zero_h = jnp.zeros((N_A, B, D_RNN), dt)
    zero_c = jnp.zeros((N_A, B, CONV_W - 1, D_RNN), dt)
    zero_f = jnp.zeros((DEPTH, B, FFN_CONV_W - 1, D_FF), dt)
    y_prompt, h_p, c_p, f_p, k_p, v_p = trunk(x_prompt, zero_h, zero_c, zero_f, None, None, P, True)
    y_sample, h_s, c_s, f_s, k_s, v_s = trunk(x_sample, state_lru_h, state_lru_conv, state_ffn_conv,
                                              cache_k_win, cache_v_win, P, False)
    return (y_prompt, y_sample, h_p, c_p, f_p, k_p, v_p, h_s, c_s, f_s, k_s, v_s)


_drawn_inputs = setup_inputs


def setup_inputs(seed=0):
    import zlib

    import numpy as np

    out = dict(_drawn_inputs(seed))
    spreads = {}
    factors = {'a_gate_r_b': 8.0,
     'a_gate_i_b': 7.37,
     'b_kv': 2.909,
     'b_norm': 7.861,
     'b_q': 8.0,
     'q_norm': 7.646,
     'sinks': 8.0,
     'b_o': 3.522,
     'f_conv_b': 3.806}
    for name, (base, spread) in spreads.items():
        noise = np.random.default_rng([zlib.crc32(name.encode()), seed]).standard_normal(out[name].shape)
        drawn = base * np.exp(spread * noise) if base else spread * noise
        out[name] = __import__('jax').numpy.asarray(drawn.astype(out[name].dtype))
    for name, factor in factors.items():
        out[name] = (out[name] * factor).astype(out[name].dtype)
    return out
```

```python
from contextlib import ExitStack

import numpy as np

import concourse.bass as bass
from concourse import mybir

P = 128
F32 = mybir.dt.float32
F32R = mybir.dt.float32r
ACT = mybir.ActivationFunctionType
ALU = mybir.AluOpType
AX_X = mybir.AxisListType.X
ds = bass.ds

D = 1024
SEQ = 1024
DEC_B = 8
DEC_T = 8
NS = DEC_B * DEC_T
T = SEQ + NS
KD = D // P
LRU_BLOCKS = 4
CONV_W = 4
D_FF = 3 * D
FT = D_FF // P
FFN_W = 3
HEADS = 16
KV_HEADS = 4
HD = 64
WIN = 128
NB = SEQ // WIN
LS = WIN + DEC_T
BUCKETS = 32
EPS = 1e-6
NEG = -1e30
C_GATE = 8.0
SCALE = HD ** -0.5
CHUNKS = [(0, 384), (384, 384), (768, 320)]
FB = 6
NFB = FT // FB
FV = 384

N_A = 0
N_OUT = N_A + 4 * LRU_BLOCKS
N_F0 = N_OUT + KD // 2
N_KV = N_F0 + NFB * (FB + KD // 2)
N_Q = N_KV + 2
N_O = N_Q + KD // 2
N_F1 = N_O + KD // 2
N_END = N_F1 + NFB * (FB + KD // 2)

(C_ANORM, C_CONVW, C_CONVB, C_RB, C_IB, C_LAM, C_KVN, C_BN, C_FN, C_BO, C_BQ, C_BKV, C_SCONV, C_SH) = \
    (0, 1, 5, 6, 7, 8, 9, 10, 11, 13, 14, 15, 16, 40)
NPROW = 48
N_PRM = 28
NPB = 3
N_ATT_IN = 36
LROW = 36
NFROW = 40
F_W, F_B, F_S = 0, 3, 4


class Tally:

    def __init__(self, eng, sem):
        self.eng, self.sem, self.at = eng, sem, 0

    def mark(self, ins):
        ins.then_inc(self.sem, 1)
        self.at = self.at + 1

    def settle(self):
        self.eng.wait_ge(self.sem, self.at)


def wait(eng, sem, value):
    if not isinstance(value, int) or value > 0:
        eng.wait_ge(sem, value)


def build(nc, A):
    with ExitStack() as ctx:
        def sem(name):
            return ctx.enter_context(nc.semaphore(name))

        base = (nc.sbuf_base + 63) // 64 * 64
        top = [base]

        def at(name, shape, dt, offset):
            return nc.alloc_sbuf_tensor_at(name, shape, dt, offset=offset)

        def take(name, shape, dt):
            offset = top[0]
            top[0] += (int(np.prod(shape[1:])) * 4 + 31) // 32 * 32
            return at(name, shape, dt, offset)

        x = take("x", [P, KD, T], F32)
        reg_n = top[0]
        nhi = take("nhi", [P, KD, T], F32R)
        nlo = take("nlo", [P, KD, T], F32R)
        reg_h = top[0]
        hhi = take("hhi", [P, FB, T], F32R)
        hlo = take("hlo", [P, FB, T], F32R)
        raw = [take(f"raw{s}", [P, KD * P], F32) for s in range(2)]
        whi = [take(f"whi{s}", [P, KD * P], F32R) for s in range(2)]
        wlo = [take(f"wlo{s}", [P, KD * P], F32R) for s in range(2)]
        convin = take("convin", [P, 1120], F32)
        y = take("y", [P, T], F32)
        rstd = take("rstd", [P, T], F32)
        t1 = take("t1", [P, T], F32)
        t2 = take("t2", [P, T], F32)
        pcol = take("pcol", [P, KD, NPROW + 4], F32)
        lstash = pcol[:, :, C_SCONV:C_SCONV + LROW]
        fcol = take("fcol", [P, FT, NFROW], F32)
        fstash = take("fstash", [P, FT, 2 + 2 * DEC_B], F32)
        ident = take("ident", [P, P], F32)
        ones = take("ones", [P, P], F32)
        blockones = take("blockones", [P, P], F32)
        epst = take("epst", [P, 1], F32)
        qkn = take("qkn", [P, 2], F32)
        sp = take("sp", [P, 2, KD], F32)
        spt = take("spt", [P, 4, KD], F32)
        h0a = take("h0a", [P, DEC_B], F32)
        sinkb = take("sinkb", [P, HEADS], F32)
        sinks_s = take("sinks_s", [P, KV_HEADS], F32)
        stat = take("stat", [P, 8, 4 * NPB], F32)
        assert top[0] <= nc.sbuf_usable_end, top[0]

        z = at("z", [P, KD, T], F32, reg_h)
        xchi = at("xchi", [P, 2, T], F32R, reg_h + KD * T * 4)
        xclo = at("xclo", [P, 2, T], F32R, reg_h + (KD + 2) * T * 4)
        xrows = at("xrows", [P, 9, D], F32, reg_h)
        prow = at("prow", [NPROW, D], F32, reg_h + 9 * D * 4)
        frow = at("frow", [NFROW, D_FF], F32, reg_n)
        qz = at("qz", [P, KD, T], F32, reg_h)
        kf = at("kf", [P, 2, T], F32, reg_h + KD * T * 4)
        vt = at("vt", [P, NB, 256], F32, reg_h + (KD + 2) * T * 4)
        tlast = at("tlast", [P, 2, T], F32, reg_n + (2 * KD - 2) * T * 4)
        top[0] = reg_n
        bias = take("bias", [P, HEADS, 2 * WIN], F32)
        sbias = take("sbias", [P, KV_HEADS, LS], F32)
        ck = take("ck", [P, DEC_B, 256], F32)
        kct = take("kct", [P, 2, DEC_B * WIN], F32)
        cv = take("cv", [P, DEC_B, 256], F32)
        vnew = take("vnew", [DEC_T, DEC_B, 256], F32)
        pb = [take("pb0", [P, 4, 2 * WIN], F32), take("pb1", [P, 4, 2 * WIN], F32),
              y[:, 0:8 * WIN].rearrange("p (j s) -> p j s", j=4)]
        pt = take("pt", [P, 2, 512], F32)
        kvrow = take("kvrow", [P, 2, 256], F32)
        assert top[0] <= reg_h
        yrows = at("yrows", [P, 9, D], F32, reg_n)
        fout = at("fout", [18, D_FF], F32, reg_h)
        lout = at("lout", [LROW, D], F32, reg_h + D_FF * 4)

        ps = ctx.enter_context(nc.psum_tensor("ps", [P, 8, 512], F32))

        raw_ready = [sem(f"raw_ready{s}") for s in range(2)]
        hi_ready = [sem(f"hi_ready{s}") for s in range(2)]
        lo_ready = [sem(f"lo_ready{s}") for s in range(2)]
        bank_ready = [sem(f"bank_ready{b}") for b in range(6)]
        bank_free = [sem(f"bank_free{b}") for b in range(6)]
        rows_in = [sem(f"rows_in{i}") for i in range(3)]
        const_ready = sem("const_ready")
        prm_in = sem("prm_in")
        tr_ready = sem("tr_ready")
        tr_act = sem("tr_act")
        tr_dve = sem("tr_dve")
        dve_seq = sem("dve_seq")
        pool_seq = sem("pool_seq")
        sq_done = sem("sq_done")
        sq_added = sem("sq_added")
        stat_ready = sem("stat_ready")
        stat_sqrt = sem("stat_sqrt")
        xn_mult = sem("xn_mult")
        xn_hi = sem("xn_hi")
        xn_lo = sem("xn_lo")
        sp_exp = sem("sp_exp")
        sp_ready = sem("sp_ready")
        hist_ready = sem("hist_ready")
        conv_done = sem("conv_done")
        stash_done = sem("stash_done")
        gelu_done = sem("gelu_done")
        hhi_done = sem("hhi_done")
        hlo_done = sem("hlo_done")
        xc_hi = sem("xc_hi")
        xc_lo = sem("xc_lo")
        tanh_done = sem("tanh_done")
        a_ready = sem("a_ready")
        one_a2 = sem("one_a2")
        root_ready = sem("root_ready")
        scan_done = sem("scan_done")
        hlast_done = sem("hlast_done")
        z_ready = sem("z_ready")
        z_hi = sem("z_hi")
        z_lo = sem("z_lo")
        fst_tr = sem("fst_tr")
        fst_cp = sem("fst_cp")
        states_out = sem("states_out")
        win_out = sem("win_out")
        y_out = sem("y_out")
        strip_in = sem("strip_in")
        strip_one = sem("strip_one")
        strip_mm = sem("strip_mm")
        strip_cp = sem("strip_cp")
        strip_out = sem("strip_out")
        att_in = sem("att_in")
        vnew_in = sem("vnew_in")
        hsq = sem("hsq")
        hmean = sem("hmean")
        hroot = sem("hroot")
        hnorm = sem("hnorm")
        prep_tr = sem("prep_tr")
        prep_cp = sem("prep_cp")
        qs_ready = sem("qs_ready")
        sc_ready = sem("sc_ready")
        sc_read = sem("sc_read")
        max_ready = sem("max_ready")
        exp_done = sem("exp_done")
        inv_ready = sem("inv_ready")
        p_ready = sem("p_ready")
        pt_ready = sem("pt_ready")
        pt_copied = sem("pt_copied")
        o_ready = sem("o_ready")
        o_copied = sem("o_copied")
        qkv_ev = sem("qkv_ev")

        strip_dram = nc.dram_tensor("strip", [HEADS * P * FV], F32, kind="Internal").ap()
        strip_in_sb = at("strip_in_sb", [BUCKETS + 1, FV + HEADS], F32, reg_h + (KD + 2) * T * 4)
        strip_sb2 = at("strip_sb2", [HEADS, FV], F32, reg_h + (KD + 2) * T * 4 + 4 * (FV + HEADS))

        def chunk(c):
            return ds(CHUNKS[c][0], CHUNKS[c][1])

        def bank(b, c):
            return ps[:, b, 0:CHUNKS[c][1]]

        def sp_view(buf, hist):
            w = SEQ + hist
            return buf[:, 0:w], buf[:, w:w + DEC_B * (DEC_T + hist)].rearrange("p (b t) -> p b t", b=DEC_B)

        def gate_tiles(c, m):
            if m == 0:
                return t1[:, :], t2[:, :]
            if isinstance(c, int) and c == LRU_BLOCKS - 1:
                return tlast[:, 0, :], tlast[:, 1, :]
            return tuple(z[:, ds(2 * c + 2 + i, 1), :].rearrange("p o t -> p (o t)") for i in range(2))

        def requests(ap):
            return ap.rearrange("p (b t) -> p b t", b=DEC_B)

        def w_cols(w, col):
            return w.rearrange("(k p) n -> p k n", p=P)[:, :, ds(col, P)]

        setup = []
        for half in range(2):
            setup.append(("p", half))
        for q3 in range(2):
            setup.append(("f", q3))
        for tt in range(9):
            for half in range(2):
                setup.append(("x", tt, half))
        NSET = len(setup)

        def job_out(job, bank_no):
            if job[0] == "p":
                h = job[1]
                return (ps[:, bank_no, 0:4 * NPROW].rearrange("p (k c) -> p k c", k=4), pcol[:, 4 * h:4 * h + 4, 0:NPROW])
            if job[0] == "f":
                h = job[1]
                return (ps[:, bank_no, 0:12 * NFROW].rearrange("p (k c) -> p k c", k=12),
                        fcol[:, 12 * h:12 * h + 12, :])
            _, tt, h = job
            w = P if tt < 8 else NS
            return (ps[:, bank_no, 0:4 * w].rearrange("p (k c) -> p k c", k=4),
                    x[:, 4 * h:4 * h + 4, tt * P:tt * P + w])

        ends = [(tt, half) for tt in range(9) for half in range(2)]
        TR_DVE_END, TR_ACT_END = [], []
        n_set_act, n_set_dve = (NSET + 1) // 2, NSET // 2
        for g in range(3):
            m = 6 * (g + 1)
            TR_ACT_END.append(n_set_act + (m + 1) // 2)
            TR_DVE_END.append(n_set_dve + m // 2)

        def end_out(m):
            tt, h = ends[m]
            w = P if tt < 8 else NS
            return ps[0:w, m % 8, :], yrows[0:w, tt, 512 * h:512 * h + 512]

        steps = [(a, e, b) for a in range(2) for e in range(2) for b in range(NB + 1)]
        NSTEP = len(steps)

        STATE0 = [0, 8, 14]

        def state_jobs(layer):
            jobs = []
            if layer == 0:
                for m in range(2):
                    b = 6 + len(jobs) % 2
                    outs = [(ps[0:LROW, b, i * P:(i + 1) * P], lstash[:, 4 * m + i, :]) for i in range(4)]
                    jobs.append((outs, ps[0:LROW, b, :], lout[:, m * 512:(m + 1) * 512]))
            for m in range(FT // 4):
                b = 6 + len(jobs) % 2
                outs = [(ps[0:18, b, i * P:(i + 1) * P], fstash[:, 4 * m + i, :]) for i in range(4)]
                jobs.append((outs, ps[0:18, b, :], fout[:, m * 512:(m + 1) * 512]))
            return jobs

        PREP_CK0 = 6

        def prep_jobs():
            jobs = []
            for m in range(4):
                outs = []
                for q in range(4):
                    blk, a = 2 * m + q // 2, q % 2
                    src = (t1, t2)[a]
                    outs.append((ps[:, m, q * P:(q + 1) * P], src[:, blk * P:(blk + 1) * P]))
                jobs.append((outs, ps[:, m, :].rearrange("p (b c) -> p b c", b=2), vt[:, 2 * m:2 * m + 2, :]))
            outs = [(ps[:, 4, a * P:(a + 1) * P], kf[:, a, SEQ - WIN:SEQ]) for a in range(2)]
            jobs.append((outs, ps[:, 4, 0:256], kvrow[:, 0, :]))
            outs = [(ps[0:NS, 5, a * P:(a + 1) * P], kf[:, a, SEQ:T]) for a in range(2)]
            outs += [(ps[0:NS, 5, 256 + a * P:256 + (a + 1) * P], (t1, t2)[a][:, SEQ:T]) for a in range(2)]
            jobs.append((outs, ps[0:NS, 5, :].rearrange("p (b c) -> p b c", b=2), None))
            for m in range(4):
                outs = []
                for q in range(4):
                    r, a = 4 * (m % 2) + q, m // 2
                    outs.append((ps[:, (6 + m) % 8, q * P:(q + 1) * P], ck[:, r, a * P:(a + 1) * P]))
                jobs.append((outs, ps[:, (6 + m) % 8, :], kct[:, m // 2, 512 * (m % 2):512 * (m % 2) + 512]))
            return jobs

        block = ctx.enter_context(nc.Block())

        @block.sync
        def _(eng):
            for g in range(3):
                if g < 2:
                    src = A["x_prompt"][0, 384 * g:384 * g + 384, :].rearrange("(i p) d -> p i d", p=P)
                    eng.dma_start(xrows[:, 3 * g:3 * g + 3, :], src).then_inc(rows_in[g], 16)
                else:
                    src = A["x_prompt"][0, 768:1024, :].rearrange("(i p) d -> p i d", p=P)
                    eng.dma_start(xrows[:, 6:8, :], src).then_inc(rows_in[g], 16)
                    eng.dma_start(xrows[0:NS, 8, :], A["x_sample"].rearrange("b t d -> (b t) d"))\
                       .then_inc(rows_in[g], 16)

            def load(n, s, src, cols):
                if not isinstance(n, int):
                    n = eng.snap(eng.to_reg(n))
                    eng.wait_ge(rows_in[0], 16)
                wait(eng, lo_ready[s], n)
                eng.dma_start(raw[s][:, 0:cols].rearrange("p (k n) -> p k n", n=P), src).then_inc(raw_ready[s], 16)

            w_in, w_out = A["a_w_in"][0], A["a_w_out"][0]

            def gate_w(w, c, m):
                return w[0][ds(c, 1), :, m * P:(m + 1) * P].rearrange("a (k p) n -> p (a k) n", p=P)

            def lru_loads(c):
                for s in range(2):
                    load(4 * c, s, w_cols(w_in, D + c * 256 + s * P), KD * P)
                for s in range(2):
                    load(4 * c + 1, s, w_cols(w_in, c * 256 + s * P), KD * P)
                for m in range(2):
                    load(4 * c + 2 + m, 0, gate_w(A["a_gate_r_w"], c, m), 2 * P)
                    load(4 * c + 2 + m, 1, gate_w(A["a_gate_i_w"], c, m), 2 * P)

            lru_loads(0)
            with eng.Fori(1, LRU_BLOCKS) as c:
                lru_loads(c)
            with eng.Fori(0, KD // 2) as i:
                for s in range(2):
                    load(N_OUT + i, s, w_cols(w_out, i * 256 + s * P), KD * P)

            def ffn(layer, n0):
                up, down = A["f_w_up"][layer], A["f_w_down"][layer]
                with eng.Fori(0, NFB) as b:
                    with eng.Fori(0, FB) as j:
                        for s in range(2):
                            load(n0 + b * (FB + KD // 2) + j, s, w_cols(up, s * D_FF + b * (FB * P) + j * P), KD * P)
                    with eng.Fori(0, KD // 2) as i:
                        for s in range(2):
                            src = down.rearrange("(k p) n -> p k n", p=P)[:, ds(b * FB, FB), ds(i * 256 + s * P, P)]
                            load(n0 + b * (FB + KD // 2) + FB + i, s, src, FB * P)

            ffn(0, N_F0)
            for m in range(2):
                for s in range(2):
                    load(N_KV + m, s, w_cols(A["w_kv"], (2 * m + s) * P), KD * P)
            wq = A["w_q"][0].rearrange("(k p) (a e j d) -> p k a e j d", p=P, a=2, e=2, j=4)
            for t in range(KD):
                a, j, n, s = t // 4, t % 4, N_Q + t // 2, t % 2
                eng.wait_ge(lo_ready[s], n)
                for e in range(2):
                    dst = raw[s][:, :].rearrange("p (k e d) -> p k e d", k=KD, e=2)[:, :, e, :]
                    eng.dma_start(dst, wq[:, :, a, e, j, :]).then_inc(raw_ready[s], 16)
            wo = A["w_o"][0].rearrange("(a e j d) n -> d a e j n", a=2, e=2, j=4)
            for t in range(KD):
                n, s = N_O + t // 2, t % 2
                eng.wait_ge(lo_ready[s], n)
                for e in range(2):
                    for a in range(2):
                        dst = raw[s][HD * e:HD * e + HD, a * 512:a * 512 + 512].rearrange("p (j n) -> p j n", j=4)
                        eng.dma_start(dst, wo[:, a, e, :, t * P:(t + 1) * P]).then_inc(raw_ready[s], 16)
            ffn(1, N_F1)

            for g in range(3):
                eng.wait_ge(tr_dve, TR_DVE_END[g])
                eng.wait_ge(tr_act, TR_ACT_END[g])
                if g < 2:
                    dst = A["y_prompt"][0, 384 * g:384 * g + 384, :].rearrange("(i p) d -> p i d", p=P)
                    eng.dma_start(dst, yrows[:, 3 * g:3 * g + 3, :]).then_inc(y_out, 16)
                else:
                    dst = A["y_prompt"][0, 768:1024, :].rearrange("(i p) d -> p i d", p=P)
                    eng.dma_start(dst, yrows[:, 6:8, :]).then_inc(y_out, 16)
                    eng.dma_start(A["y_sample"].rearrange("b t d -> (b t) d"), yrows[0:NS, 8, :])\
                       .then_inc(y_out, 16)
            eng.wait_ge(y_out, 16 * 4)

        def raw_count_at(n, phase):
            q, o = KD // 2, KD // 2
            if phase == "q":
                return 16 * (N_Q + 2 * (n - N_Q + 1))
            if phase == "o":
                return 16 * (N_Q + 2 * q + 4 * (n - N_O + 1))
            if phase == "f1":
                return 16 * (n + 1) + 16 * (q + 3 * o)
            return 16 * (n + 1)

        @block.tensor
        def _(pe):
            pe.wait_ge(const_ready, 5)
            pe.wait_ge(prm_in, 16 * N_PRM)
            for m, job in enumerate(setup):
                if m >= 8:
                    pe.wait_ge(tr_act if m % 2 == 0 else tr_dve, (m - 8) // 2 + 1)
                if job[0] == "p":
                    for i in range(4):
                        k = 4 * job[1] + i
                        last = pe.transpose(ps[:, m % 8, i * NPROW:(i + 1) * NPROW], prow[:, k * P:(k + 1) * P],
                                            ident[0:NPROW, 0:NPROW])
                elif job[0] == "f":
                    for i in range(12):
                        k = 12 * job[1] + i
                        last = pe.transpose(ps[:, m % 8, i * NFROW:(i + 1) * NFROW], frow[:, k * P:(k + 1) * P],
                                            ident[0:NFROW, 0:NFROW])
                else:
                    _, tt, h = job
                    w = P if tt < 8 else NS
                    pe.wait_ge(rows_in[tt // 3], 32 if tt >= 6 else 16)
                    for i in range(4):
                        k = 4 * h + i
                        last = pe.transpose(ps[:, m % 8, i * w:(i + 1) * w], xrows[0:w, tt, k * P:(k + 1) * P],
                                            ident[0:w, 0:w])
                last.then_inc(tr_ready, 1)

            def unit(n, s, nk, mhi, mlo, before=None):
                pe.wait_ge(hi_ready[s], n + 1)
                pe.wait_ge(lo_ready[s], n + 1)
                for c in range(3):
                    wait(pe, bank_free[3 * s + c], n)
                    out = bank(3 * s + c, c)
                    for k in range(nk):
                        if before:
                            before(c, k)
                        w = ds(k * P, P)
                        pe.matmul(out, whi[s][:, w], mhi[:, k, chunk(c)], start=(k == 0), stop=False)
                        pe.matmul(out, whi[s][:, w], mlo[:, k, chunk(c)], start=False, stop=False)
                        last = pe.matmul(out, wlo[s][:, w], mhi[:, k, chunk(c)], start=False, stop=(k == nk - 1))
                    last.then_inc(bank_ready[3 * s + c], 1)

            def stats(v):
                for c in range(3):
                    pe.wait_ge(sq_added, 24 * v + 22 + c)
                    if c == 2:
                        pe.wait_ge(stat_sqrt, 3 * v + 1)
                    pe.matmul(bank(6 + c % 2, c), ones[:, :], t2[:, chunk(c)], start=True, stop=True)\
                      .then_inc(stat_ready, 1)

            def normed(u):
                def before(c, k):
                    if k % 2 == 0:
                        pe.wait_ge(xn_lo, 24 * u + 8 * c + k + 2)
                return before

            pe.wait_ge(tr_act, n_set_act)
            pe.wait_ge(tr_dve, n_set_dve)
            stats(0)
            def lru_block(c, first=False):
                for s in range(2):
                    unit(4 * c, s, KD, nhi, nlo, normed(0) if first and s == 0 else None)
                for s in range(2):
                    unit(4 * c + 1, s, KD, nhi, nlo)
                pe.wait_ge(xc_lo, 2 * c + 2)
                for m in range(2):
                    for s in range(2):
                        unit(4 * c + 2 + m, s, 2, xchi, xclo)

            lru_block(0, first=True)
            with pe.Fori(1, LRU_BLOCKS) as c:
                lru_block(c)

            def z_split(base_count):
                def before(c, k):
                    pe.wait_ge(z_lo, base_count + k + 1)
                return before

            for ks in (range(KD - 2), range(KD - 2, KD)):
                for s in range(2):
                    if ks[0] == 0:
                        pe.wait_ge(hi_ready[s], N_OUT + 1)
                        pe.wait_ge(lo_ready[s], N_OUT + 1)
                    for c in range(3):
                        if ks[0] == 0:
                            pe.wait_ge(bank_free[3 * s + c], N_OUT)
                        for k in ks:
                            pe.wait_ge(z_lo, k + 1)
                            w, out = ds(k * P, P), bank(3 * s + c, c)
                            pe.matmul(out, whi[s][:, w], nhi[:, k, chunk(c)], start=(k == 0), stop=False)
                            pe.matmul(out, whi[s][:, w], nlo[:, k, chunk(c)], start=False, stop=False)
                            last = pe.matmul(out, wlo[s][:, w], nhi[:, k, chunk(c)], start=False, stop=(k == KD - 1))
                        if ks[0] > 0:
                            last.then_inc(bank_ready[3 * s + c], 1)
            with pe.Fori(1, KD // 2) as i:
                for s in range(2):
                    unit(N_OUT + i, s, KD, nhi, nlo)
            stats(1)

            def ffn(layer, n0, u):
                with pe.Fori(0, NFB) as b:
                    nb = n0 + b * (FB + KD // 2)
                    f1 = layer * FT + b * FB + FB
                    with pe.Fori(0, FB) as j:
                        unit(nb + j, 0, KD, nhi, nlo, normed(u))
                        unit(nb + j, 1, KD, nhi, nlo)

                    def hidden(c, k):
                        if c == 0 and k == 0:
                            pe.wait_ge(hlo_done, 3 * f1 - 3)
                        if k == FB - 1:
                            pe.wait_ge(hlo_done, 3 * f1 - 2 + c)
                    with pe.Fori(0, KD // 2) as i:
                        for s in range(2):
                            unit(nb + FB + i, s, FB, hhi, hlo, hidden if s == 0 else None)
                pe.wait_ge(stash_done, KD + (layer + 1) * FT)
                if layer == 0:
                    pe.wait_ge(hlast_done, KD)
                for m, (outs, _, _) in enumerate(state_jobs(layer)):
                    if m >= 2:
                        pe.wait_ge(fst_cp, STATE0[layer] + m - 1)
                    for o, t in outs:
                        last = pe.transpose(o, t, ident[:, :])
                    last.then_inc(fst_tr, 1)
                pe.wait_ge(fst_cp, STATE0[layer + 1])

            ffn(0, N_F0, 1)
            stats(2)
            for m in range(2):
                for s in range(2):
                    unit(N_KV + m, s, KD, nhi, nlo, normed(2))
            def head_stats(i):
                for c in range(3):
                    pe.wait_ge(hsq, i + 1)
                    if 3 * i + c >= 2:
                        pe.wait_ge(hroot, 3 * i + c - 1)
                    pe.matmul(bank(6 + (3 * i + c) % 2, c), blockones[:, :], y[:, chunk(c)], start=True, stop=True)\
                      .then_inc(hmean, 1)

            pe.wait_ge(strip_in, 32)
            pe.wait_ge(strip_one, 1)
            head_stats(0)
            head_stats(1)
            pe.wait_ge(hroot, 6)
            pe.matmul(ps[0:HEADS, 6, 0:FV], strip_in_sb[:, FV:FV + HEADS], strip_in_sb[:, 0:FV], start=True,
                      stop=True).then_inc(strip_mm, 1)
            pe.wait_ge(strip_cp, 1)
            for t in range(KD):
                unit(N_Q + t // 2, t % 2, KD, nhi, nlo, normed(3) if t == 0 else None)
                if t >= 1:
                    head_stats(2 + t - 1)
            head_stats(2 + KD - 1)

            pe.wait_ge(hroot, 3 * (2 + KD))
            pe.wait_ge(hnorm, 2 + KD)
            for b in range(6):
                pe.wait_ge(bank_free[b], N_O)
            jobs = prep_jobs()
            for m, (outs, _, _) in enumerate(jobs):
                if m >= 8:
                    pe.wait_ge(prep_cp, m - 7)
                if m == PREP_CK0:
                    pe.wait_ge(att_in, 16 * N_ATT_IN)
                for o, i in outs:
                    last = pe.transpose(o, i, ident[0:i.shape[0], 0:i.shape[0]])
                last.then_inc(prep_tr, 1)
            pe.wait_ge(prep_cp, len(jobs))
            pe.wait_ge(att_in, 16 * N_ATT_IN)
            pe.wait_ge(vnew_in, 16 * DEC_B)
            pe.wait_ge(qs_ready, 2)

            def scores(i):
                a, e, b = steps[i]
                h0 = HD * e
                if i >= 2:
                    pe.wait_ge(sc_read, i - 1)
                if b < NB:
                    k0 = 0 if b > 0 else WIN
                    for j in range(4):
                        out = ps[:, 2 * (i % 2) + j // 2, (j % 2) * 256 + k0:(j % 2) * 256 + 256]
                        last = pe.matmul(out, qz[h0:h0 + HD, 4 * a + j, b * WIN:(b + 1) * WIN],
                                         kf[h0:h0 + HD, a, (b - 1) * WIN + k0:(b + 1) * WIN], start=True, stop=True)
                else:
                    for r in range(DEC_B):
                        new = ds(SEQ + r * DEC_T, DEC_T)
                        q = convin[h0:h0 + HD, ds(256 * a + 32 * r, 32)]
                        o0 = 32 * (r % 4)
                        c0 = LS * (r // 4)
                        pe.matmul(ps[o0:o0 + 32, 2 * (i % 2), c0:c0 + WIN], q, kct[h0:h0 + HD, a, r * WIN:(r + 1) * WIN],
                                  start=True, stop=True)
                        last = pe.matmul(ps[o0:o0 + 32, 2 * (i % 2), c0 + WIN:c0 + LS], q, kf[h0:h0 + HD, a, new],
                                         start=True, stop=True)
                last.then_inc(sc_ready, 1)

            def transposes(i):
                a, e, b = steps[i]
                pe.wait_ge(p_ready, i + 1)
                if i >= 1:
                    pe.wait_ge(pt_copied, i)
                if b < NB:
                    for h in range(0 if b > 0 else 1, 2):
                        for j in range(4):
                            last = pe.transpose(ps[:, 4 + h, j * P:(j + 1) * P], pb[i % NPB][:, j, h * P:(h + 1) * P],
                                                ident[:, :])
                else:
                    flat = pb[i % NPB][:, :, :].rearrange("p a b -> p (a b)")
                    for h in range(2):
                        pe.transpose(ps[:, 4, h * P:(h + 1) * P], flat[:, h * LS:h * LS + WIN], ident[:, :])
                        last = pe.transpose(ps[0:DEC_T, 5, h * P:(h + 1) * P], flat[:, h * LS + WIN:(h + 1) * LS],
                                            ident[:, :])
                last.then_inc(pt_ready, 1)

            def values(i):
                a, e, b = steps[i]
                h0, g = HD * e, 2 * a + e
                out = 6 + i % 2
                pe.wait_ge(pt_copied, i + 1)
                if i >= 2:
                    pe.wait_ge(o_copied, i - 1)
                col = ds(g * HD, HD)
                if b < NB:
                    for h in range(0 if b > 0 else 1, 2):
                        last = pe.matmul(ps[h0:h0 + HD, out, :], vt[:, b - 1 + h, col], pt[:, h, :],
                                         start=(h == 0 or b == 0), stop=(h == 1))
                else:
                    for r in range(DEC_B):
                        c0 = 32 * r
                        pe.matmul(ps[h0:h0 + HD, out, c0:c0 + 32], cv[:, r, col], pt[:, 0, c0:c0 + 32],
                                  start=True, stop=False)
                        last = pe.matmul(ps[h0:h0 + HD, out, c0:c0 + 32], vnew[:, r, col], pt[0:DEC_T, 1, c0:c0 + 32],
                                         start=False, stop=True)
                last.then_inc(o_ready, 1)

            scores(0)
            scores(1)
            for i in range(NSTEP):
                if i + 2 < NSTEP:
                    scores(i + 2)
                if i >= 1:
                    values(i - 1)
                transposes(i)
            values(NSTEP - 1)
            pe.wait_ge(sc_read, NSTEP)
            pe.wait_ge(pt_copied, NSTEP)
            pe.wait_ge(o_copied, NSTEP)

            unit(N_O, 0, KD, nhi, nlo, z_split(KD))
            unit(N_O, 1, KD, nhi, nlo)
            with pe.Fori(1, KD // 2) as i:
                for s in range(2):
                    unit(N_O + i, s, KD, nhi, nlo)
            stats(3)
            ffn(1, N_F1, 4)

            for b in range(6):
                pe.wait_ge(bank_free[b], N_END)
            for m, (tt, h) in enumerate(ends):
                if m >= 8:
                    pe.wait_ge(tr_act if m % 2 == 0 else tr_dve,
                               (n_set_act if m % 2 == 0 else n_set_dve) + (m - 8) // 2 + 1)
                w = P if tt < 8 else NS
                for i in range(4):
                    last = pe.transpose(ps[0:w, m % 8, i * P:(i + 1) * P], x[:, 4 * h + i, tt * P:tt * P + w],
                                        ident[:, :])
                last.then_inc(tr_ready, 1)

        @block.scalar
        def _(act):
            rows = [(0, A["a_norm"]), (1, A["a_conv_w"][0]), (5, A["a_conv_b"]), (6, A["a_gate_r_b"]),
                    (7, A["a_gate_i_b"]), (8, A["a_lambda"]), (9, A["kv_norm"].rearrange("(a d) -> a d", a=1)),
                    (10, A["b_norm"]), (11, A["f_norm"]), (13, A["b_o"]),
                    (16, A["state_lru_conv"][0].rearrange("b w d -> (b w) d")), (40, A["state_lru_h"][0])]
            count = 0
            for r, src in rows:
                act.dma_start(prow[r:r + src.shape[0], :], src).then_inc(prm_in, 16)
                count += 1
            bq = A["b_q"].rearrange("o (a e j d) -> o a e j d", a=2, e=2, j=4)
            for e in range(2):
                for a in range(2):
                    dst = prow[14:15, a * 512:a * 512 + 512].rearrange("o (j e d) -> o j e d", j=4, e=2)[:, :, e, :]
                    act.dma_start(dst, bq[:, a, e, :, :]).then_inc(prm_in, 16)
                    count += 1
            for h in range(2):
                act.dma_start(prow[15:16, 512 * h:512 * h + 512], A["b_kv"].rearrange("(a d) -> a d", a=1))\
                   .then_inc(prm_in, 16)
                count += 1
            for layer in range(2):
                o = 20 * layer
                for r, src in ((0, A["f_conv_w"][layer]), (3, A["f_conv_b"][layer:layer + 1, :]),
                               (4, A["state_ffn_conv"][layer].rearrange("b w d -> (b w) d"))):
                    act.dma_start(frow[o + r:o + r + src.shape[0], :], src).then_inc(prm_in, 16)
                    count += 1
            with nc.allow_non_contiguous_dma(reason="64 single elements each"):
                for e in range(2):
                    for i, name in enumerate(("q_norm", "k_norm")):
                        src = A[name][0, :] if name == "q_norm" else A[name]
                        act.dma_start(qkn[HD * e:HD * e + HD, i:i + 1], src.rearrange("(d o) -> d o", o=1))\
                           .then_inc(prm_in, 16)
                        count += 1
            assert count == N_PRM, count

            for m, job in enumerate(setup):
                if m % 2 == 0:
                    act.wait_ge(tr_ready, m + 1)
                    view, dst = job_out(job, m % 8)
                    act.activation(dst, view, ACT.Copy).then_inc(tr_act, 1)

            def prep(n, s, cols, phase=""):
                act.wait_ge(raw_ready[s], raw_count_at(n, phase))
                wait(act, bank_ready[3 * s + 2], n)
                act.activation(whi[s][:, 0:cols], raw[s][:, 0:cols], ACT.Copy).then_inc(hi_ready[s], 1)

            act.wait_ge(const_ready, 5)

            def apart():
                act.wait_ge(const_ready, 5)

            def square(v, k, c, first=False):
                if not first:
                    act.wait_ge(sq_added, 24 * v + 3 * k + c - 2)
                act.activation(t1[:, chunk(c)], x[:, k, chunk(c)], ACT.Square).then_inc(sq_done, 1)

            def roots(v):
                for c in range(3):
                    act.wait_ge(stat_ready, 3 * v + c + 1)
                    act.activation(rstd[:, chunk(c)], bank(6 + c % 2, c), ACT.Sqrt, bias=epst[:, 0:1])\
                       .then_inc(stat_sqrt, 1)

            def norm_hi(u):
                for c in range(3):
                    w = CHUNKS[c][1]
                    for k in range(KD):
                        act.wait_ge(xn_mult, 24 * u + 8 * c + k + 1)
                        act.activation(nhi[:, k, chunk(c)], y[:, ds((k % 2) * 384, w)], ACT.Copy).then_inc(xn_hi, 1)

            act.wait_ge(tr_dve, n_set_dve)
            act.wait_ge(tr_act, n_set_act)
            prep(0, 0, KD * P)
            prep(0, 1, KD * P)
            for k in range(KD):
                for c in range(3):
                    square(0, k, c, first=(k == 0))
            roots(0)
            norm_hi(0)
            act.wait_ge(sp_ready, 1)
            act.activation(spt[:, 1, :], spt[:, 0, :], ACT.Exp, scale=-1.0).then_inc(sp_exp, 1)

            def evac_conv(s, n, hist, convs, stashes):
                gp, gs = sp_view(convin, hist)
                wait(act, conv_done, convs)
                wait(act, stash_done, stashes)
                for c in range(3):
                    act.wait_ge(bank_ready[3 * s + c], n + 1)
                    lo, w = CHUNKS[c]
                    b = 3 * s + c
                    if c == 2:
                        act.activation(gs[:, :, hist:], requests(ps[:, b, SEQ - lo:w]), ACT.Copy)
                        w = SEQ - lo
                    act.activation(gp[:, hist + lo:hist + lo + w], ps[:, b, 0:w], ACT.Copy).then_inc(bank_free[b], 1)

            def lru_block(c, last):
                for s in range(2):
                    n, kt = 4 * c, 2 * c + s
                    evac_conv(s, n, 3, 2 * kt, kt)
                    prep(n + 1, s, KD * P)
                    act.wait_ge(conv_done, 2 * kt + 2)
                    act.activation(xchi[:, s, :], y[:, :], ACT.Copy).then_inc(xc_hi, 1)
                wait(act, scan_done, 2 * c)
                for s in range(2):
                    n = 4 * c + 1
                    for ch in range(3):
                        b = 3 * s + ch
                        act.wait_ge(bank_ready[b], n + 1)
                        apart()
                        act.activation(z[:, ds(2 * c + s, 1), chunk(ch)], bank(b, ch).rearrange("p (o t) -> p o t", o=1),
                                       ACT.Gelu_apprx_tanh).then_inc(bank_free[b], 1)
                        if ch == 1:
                            prep(n + 1, s, 2 * P)
                if last:
                    act.wait_ge(bank_ready[5], 4 * c + 2)
                    for k in range(KD - 2):
                        act.wait_ge(z_ready, k + 1)
                        act.activation(nhi[:, k, :], z[:, k, :], ACT.Copy).then_inc(z_hi, 1)
                wait(act, scan_done, 2 * c)
                for m in range(2):
                    n, kt = 4 * c + 2 + m, 2 * c + m
                    for s, t, col in zip(range(2), gate_tiles(c, m), (C_RB, C_IB)):
                        for ch in range(3):
                            b = 3 * s + ch
                            apart()
                            act.wait_ge(bank_ready[b], n + 1)
                            act.activation(t[:, chunk(ch)], bank(b, ch), ACT.Sigmoid,
                                           bias=pcol[:, ds(kt, 1), col]).then_inc(bank_free[b], 1)
                            if ch == 1:
                                prep(n + 1, s, 2 * P if m == 0 else KD * P)
                for m in range(2):
                    n, kt = 4 * c + 2 + m, 2 * c + m
                    t = gate_tiles(c, m)[0]
                    act.wait_ge(bank_free[2], n + 1)
                    apart()
                    act.activation(rstd[:, :], t, ACT.Tanh, scale=sp[:, 0, ds(kt, 1)]).then_inc(tanh_done, 1)
                    apart()
                    act.wait_ge(tanh_done, kt + 1)
                    act.activation(t, t, ACT.Exp, scale=sp[:, 1, ds(kt, 1)]).then_inc(a_ready, 1)
                    act.wait_ge(one_a2, kt + 1)
                    act.activation(y[:, :], y[:, :], ACT.Sqrt).then_inc(root_ready, 1)

            lru_block(0, False)
            with act.Fori(1, LRU_BLOCKS - 1) as c:
                lru_block(c, False)
            lru_block(LRU_BLOCKS - 1, True)
            for k in range(KD - 2, KD):
                act.wait_ge(z_ready, k + 1)
                act.activation(nhi[:, k, :], z[:, k, :], ACT.Copy).then_inc(z_hi, 1)

            def residual(n, i, v, last_cols, phase):
                for s in range(2):
                    for c in range(3):
                        act.wait_ge(bank_free[3 * s + c], n + 1)
                        act.wait_ge(sq_added, 24 * v + 6 * i + 3 * s + c - 2)
                        apart()
                        act.activation(t1[:, chunk(c)].rearrange("p (o t) -> p o t", o=1),
                                       x[:, ds(2 * i + s, 1), chunk(c)], ACT.Square).then_inc(sq_done, 1)
                    prep(n + 1, s, last_cols, phase)

            with act.Fori(0, KD // 2) as i:
                residual(N_OUT + i, i, 1, KD * P, "")
            roots(1)
            norm_hi(1)

            def ffn(layer, n0, v, phase):
                def block_(b, last):
                    nb = n0 + b * (FB + KD // 2)

                    def tile(j, next_cols):
                        n = nb + j
                        f = layer * FT + b * FB + j
                        evac_conv(0, n, 2, 2 * (KD + f), KD + f)
                        prep(n + 1, 0, next_cols, phase)
                        act.wait_ge(conv_done, 2 * (KD + f) + 2)
                        act.activation(y[:, :], y[:, :], ACT.Gelu_apprx_tanh).then_inc(gelu_done, 1)
                        for c in range(3):
                            act.wait_ge(bank_free[3 + c], n + 1)
                            apart()
                            act.activation(hhi[:, ds(j, 1), chunk(c)], y[:, chunk(c)].rearrange("p (o t) -> p o t", o=1),
                                           ACT.Copy).then_inc(hhi_done, 1)
                        prep(n + 1, 1, next_cols, phase)

                    with act.Fori(0, FB - 1) as j:
                        tile(j, KD * P)
                    tile(FB - 1, FB * P)
                    nd = nb + FB
                    if last and layer == 0:
                        with act.Fori(0, KD // 2 - 1) as i:
                            residual(nd + i, i, v, FB * P, phase)
                        i = KD // 2 - 1
                        for s in range(2):
                            for c in range(3):
                                act.wait_ge(bank_free[3 * s + c], nd + i + 1)
                                square(v, 2 * i + s, c)
                            prep(nd + i + 1, s, KD * P, "")
                    else:
                        with act.Fori(0, KD // 2 - 1) as i:
                            for s in range(2):
                                prep(nd + i + 1, s, FB * P, phase)
                        if not last:
                            for s in range(2):
                                prep(nd + KD // 2, s, KD * P, phase)

                with act.Fori(0, NFB - 1) as b:
                    block_(b, False)
                block_(NFB - 1, True)
                for m, (_, view, dst) in enumerate(state_jobs(layer)):
                    act.wait_ge(fst_tr, STATE0[layer] + m + 1)
                    act.activation(dst, view, ACT.Copy).then_inc(fst_cp, 1)
                act.wait_ge(fst_cp, STATE0[layer + 1])
                act.dma_start(A["ffn_conv_p"][layer, 0], fout[0:2, :]).then_inc(states_out, 16)
                act.dma_start(A["ffn_conv_s"][layer].rearrange("b w d -> (b w) d"), fout[2:18, :])\
                   .then_inc(states_out, 16)
                if layer == 0:
                    for dst, lo, hi in ((A["lru_conv_p"][0, 0], 32, 35),
                                        (A["lru_conv_s"][0].rearrange("b w d -> (b w) d"), 0, 24),
                                        (A["lru_h_p"][0], 35, 36), (A["lru_h_s"][0], 24, 32)):
                        act.dma_start(dst, lout[lo:hi, :]).then_inc(states_out, 16)

            ffn(0, N_F0, 2, "")

            roots(2)
            norm_hi(2)

            def head_roots(i):
                for c in range(3):
                    act.wait_ge(hmean, 3 * i + c + 1)
                    if c == 0:
                        act.wait_ge(hnorm, i)
                    act.activation(convin[:, chunk(c)], bank(6 + (3 * i + c) % 2, c), ACT.Sqrt, bias=epst[:, 0:1])\
                       .then_inc(hroot, 1)

            act.wait_ge(states_out, 16 * 6)
            for m in range(2):
                for s in range(2):
                    n = N_KV + m
                    for c in range(3):
                        b = 3 * s + c
                        dst = kf[:, s, chunk(c)] if m == 0 else (t1, t2)[s][:, chunk(c)]
                        act.wait_ge(bank_ready[b], n + 1)
                        act.activation(dst, bank(b, c), ACT.Identity, bias=pcol[:, 2 * m + s, C_BKV:C_BKV + 1])\
                           .then_inc(bank_free[b], 1)
                    prep(n + 1, s, KD * P, "q" if m == 1 else "")
            for s in range(2):
                act.wait_ge(bank_free[3 * s + 2], N_KV + 1)
                if s == 1:
                    act.wait_ge(hmean, 3)
                act.activation(y[:, :], kf[:, s, :], ACT.Square).then_inc(hsq, 1)
                head_roots(s)
            act.wait_ge(strip_mm, 1)
            act.activation(strip_sb2[:, :], ps[0:HEADS, 6, 0:FV], ACT.Copy).then_inc(strip_cp, 1)
            act.wait_ge(strip_cp, 1)
            src = strip_sb2[:, :].rearrange("h (o v) -> h o v", o=1).broadcast_to([HEADS, P, FV])
            act.dma_start(strip_dram.rearrange("(h r v) -> h r v", h=HEADS, r=P), src).then_inc(strip_out, 16)
            norm_hi(3)
            for t in range(KD):
                n, s = N_Q + t // 2, t % 2
                for c in range(3):
                    b = 3 * s + c
                    act.wait_ge(bank_ready[b], n + 1)
                    act.activation(qz[:, t, chunk(c)], bank(b, c), ACT.Identity, bias=pcol[:, t, C_BQ:C_BQ + 1])\
                       .then_inc(bank_free[b], 1)
                prep(n + 1, s, KD * P, "q" if t < KD - 2 else "o")
                act.wait_ge(bank_free[3 * s + 2], n + 1)
                act.wait_ge(hmean, 3 * (2 + t))
                act.activation(y[:, :], qz[:, t, :], ACT.Square).then_inc(hsq, 1)
                head_roots(2 + t)

            act.wait_ge(bank_ready[5], N_O)
            act.wait_ge(strip_out, 16)
            act.dma_start(ck[:, :, :], A["cache_k_win"].rearrange("r w h d -> w r (h d)")).then_inc(att_in, 16)
            act.dma_start(cv[:, :, :], A["cache_v_win"].rearrange("r w h d -> w r (h d)")).then_inc(att_in, 16)
            src = bass.AP(strip_dram.tensor, WIN - 1, [[FV - 1, P], [P * FV, HEADS], [1, 2 * WIN]])
            act.dma_start(bias[:, :, :], src).then_inc(att_in, 16)
            for r in range(4):
                for j in range(4):
                    src = bass.AP(strip_dram.tensor, WIN - 1 + j * P * FV,
                                  [[FV - 1, DEC_T], [4 * P * FV, KV_HEADS], [1, LS]])
                    p0 = 32 * r + DEC_T * j
                    act.dma_start(sbias[p0:p0 + DEC_T, :, :], src).then_inc(att_in, 16)
            with nc.allow_non_contiguous_dma(reason="a few single elements"):
                act.dma_start(sinkb[:, :], bass.AP(A["sinks"].tensor, 0, [[0, P], [1, HEADS]])).then_inc(att_in, 16)
                for r in range(4):
                    for j in range(4):
                        p0 = 32 * r + DEC_T * j
                        src = bass.AP(A["sinks"].tensor, j, [[0, DEC_T], [4, KV_HEADS], [1, 1]])
                        act.dma_start(sinks_s[p0:p0 + DEC_T, :].rearrange("p (g o) -> p g o", o=1), src).then_inc(att_in, 16)

            jobs = prep_jobs()
            for m, (_, view, dst) in enumerate(jobs):
                act.wait_ge(prep_tr, m + 1)
                if dst is None:
                    act.activation(kvrow[0:NS, 1, :], ps[0:NS, 5, 0:256], ACT.Copy)
                    act.activation(pt[0:NS, 0, 0:256], ps[0:NS, 5, 256:512], ACT.Copy).then_inc(prep_cp, 1)
                else:
                    act.activation(dst, view, ACT.Copy).then_inc(prep_cp, 1)
                if m == 5:
                    act.wait_ge(prep_cp, 6)
                    for r in range(DEC_B):
                        act.dma_start(vnew[:, r, :], pt[r * DEC_T:(r + 1) * DEC_T, 0, 0:256]).then_inc(vnew_in, 16)
                    for name, cache, rows in (("k", A["cache_k_win"], kvrow[0:NS, 1, :]),
                                              ("v", A["cache_v_win"], pt[0:NS, 0, 0:256])):
                        out = A[f"{name}_win_s"].rearrange("r w h d -> r w (h d)")
                        act.dma_start(out[:, 0:WIN - DEC_T, :], cache.rearrange("r w h d -> r w (h d)")[:, DEC_T:, :])\
                           .then_inc(win_out, 16)
                        for r in range(DEC_B):
                            act.dma_start(out[r, WIN - DEC_T:, :], rows[r * DEC_T:(r + 1) * DEC_T, :])\
                               .then_inc(win_out, 16)
                    act.dma_start(A["k_win_p"][0].rearrange("w h d -> w (h d)"), kvrow[:, 0, :]).then_inc(win_out, 16)
                    act.dma_start(A["v_win_p"][0].rearrange("w h d -> w (h d)"), vt[:, NB - 1, :])\
                       .then_inc(win_out, 16)

            def exps(i):
                a, e, b = steps[i]
                st = stat[:, :, 4 * (i % NPB):4 * (i % NPB) + 4]
                act.wait_ge(max_ready, i + 1)
                if b < NB:
                    k0 = 0 if b > 0 else WIN
                    for j in range(4):
                        w = pb[i % NPB][:, j, k0:]
                        act.activation(w, w, ACT.Exp, bias=st[:, 1, j:j + 1], accum_out=st[:, 2, j:j + 1])
                else:
                    flat = pb[i % NPB][:, :, :].rearrange("p a b -> p (a b)")
                    for h in range(2):
                        w = flat[:, h * LS:(h + 1) * LS]
                        act.activation(w, w, ACT.Exp, bias=st[:, 1, h:h + 1], accum_out=st[:, 2, h:h + 1])
                m = 4 if b < NB else 2
                act.activation(st[:, 3, 0:m], st[:, 4, 0:m], ACT.Exp).then_inc(exp_done, 1)

            act.wait_ge(vnew_in, 16 * DEC_B)
            act.wait_ge(win_out, 16 * (4 + 2 * DEC_B))
            exps(0)
            for i in range(NSTEP):
                a, e, b = steps[i]
                if i + 1 < NSTEP:
                    exps(i + 1)
                act.wait_ge(pt_ready, i + 1)
                if i >= 1:
                    act.wait_ge(o_ready, i)
                if b < NB:
                    if b > 0:
                        act.activation(pt[:, 0, :], ps[:, 4, :], ACT.Copy)
                    act.activation(pt[:, 1, :], ps[:, 5, :], ACT.Copy).then_inc(pt_copied, 1)
                else:
                    act.activation(pt[:, 0, 0:256], ps[:, 4, 0:256], ACT.Copy)
                    act.activation(pt[0:DEC_T, 1, 0:256], ps[0:DEC_T, 5, 0:256], ACT.Copy).then_inc(pt_copied, 1)
            for k in range(KD):
                act.wait_ge(o_copied, NSTEP)
                act.activation(nhi[:, k, :], qz[:, k, :], ACT.Copy).then_inc(z_hi, 1)
            with act.Fori(0, KD // 2 - 1) as i:
                residual(N_O + i, i, 3, KD * P, "o")
            residual(N_O + KD // 2 - 1, KD // 2 - 1, 3, KD * P, "f1")
            roots(3)
            norm_hi(4)
            ffn(1, N_F1, 4, "f1")

            for m in range(len(ends)):
                if m % 2 == 0:
                    act.wait_ge(tr_ready, NSET + m + 1)
                    view, dst = end_out(m)
                    act.activation(dst, view, ACT.Copy).then_inc(tr_act, 1)
            act.wait_ge(states_out, 16 * 8)

        @block.vector
        def _(dve):
            seq = Tally(dve, dve_seq)

            dve.memset(ones[:, :], 1.0 / D).then_inc(const_ready, 1)
            dve.memset(epst[:, :], EPS).then_inc(const_ready, 1)
            dve.memset(convin[:, 0:3], 0.0).then_inc(const_ready, 1)
            seq.mark(dve.memset(blockones[:, :], 0.0))
            seq.settle()
            dve.memset(blockones[0:HD, 0:HD], 1.0 / HD)
            dve.memset(blockones[HD:P, HD:P], 1.0 / HD).then_inc(const_ready, 1)
            for m, job in enumerate(setup):
                if m % 2 == 1:
                    dve.wait_ge(tr_ready, m + 1)
                    view, dst = job_out(job, m % 8)
                    dve.tensor_copy(dst, view).then_inc(tr_dve, 1)

            dve.wait_ge(tr_act, n_set_act)
            dve.wait_ge(tr_dve, n_set_dve)

            def prep(n, s, cols):
                dve.wait_ge(hi_ready[s], n + 1)
                dve.tensor_tensor(wlo[s][:, 0:cols], raw[s][:, 0:cols], whi[s][:, 0:cols].bitcast(F32), ALU.subtract)\
                   .then_inc(lo_ready[s], 1)

            def recips(v):
                for c in range(3):
                    dve.wait_ge(stat_sqrt, 3 * v + c + 1)
                    seq.mark(dve.reciprocal(rstd[:, chunk(c)], rstd[:, chunk(c)]))

            def norm(u, gain):
                seq.settle()
                order = [(c, k) for c in range(3) for k in range(KD)]
                for i in range(len(order) + 1):
                    if i < len(order):
                        c, k = order[i]
                        if i >= 2:
                            dve.wait_ge(xn_lo, 24 * u + i - 1)
                        dve.scalar_tensor_tensor(y[:, ds((k % 2) * 384, CHUNKS[c][1])], x[:, k, chunk(c)],
                                                 pcol[:, k, gain:gain + 1], rstd[:, chunk(c)], ALU.mult, ALU.mult)\
                           .then_inc(xn_mult, 1)
                    if i >= 1:
                        c, k = order[i - 1]
                        dve.wait_ge(xn_mult, 24 * u + i)
                        dve.wait_ge(xn_hi, 24 * u + i)
                        dve.tensor_tensor(nlo[:, k, chunk(c)], y[:, ds((k % 2) * 384, CHUNKS[c][1])],
                                          nhi[:, k, chunk(c)].bitcast(F32), ALU.subtract).then_inc(xn_lo, 1)

            prep(0, 0, KD * P)
            prep(0, 1, KD * P)
            recips(0)
            norm(0, C_ANORM)

            lam = pcol[:, :, C_LAM]
            seq.mark(dve.tensor_scalar(spt[:, 2, :], lam, -1.0, 0.0, ALU.mult, ALU.max))
            seq.mark(dve.tensor_scalar(spt[:, 3, :], lam, 0.0, None, ALU.max))
            seq.settle()
            dve.tensor_tensor(spt[:, 0, :], spt[:, 2, :], spt[:, 3, :], ALU.add).then_inc(sp_ready, 1)
            dve.wait_ge(sp_exp, 1)
            seq.mark(dve.tensor_scalar(spt[:, 0, :], spt[:, 1, :], 2.0, None, ALU.add))
            seq.settle()
            seq.mark(dve.reciprocal(spt[:, 0, :], spt[:, 0, :]))
            seq.settle()
            seq.mark(dve.tensor_tensor(spt[:, 0, :], spt[:, 0, :], spt[:, 1, :], ALU.mult))
            seq.settle()
            seq.mark(dve.tensor_tensor(spt[:, 1, :], spt[:, 0, :], spt[:, 0, :], ALU.mult))
            seq.settle()
            terms = 9
            seq.mark(dve.tensor_scalar(spt[:, 3, :], spt[:, 1, :], 1.0 / (2 * terms + 1), 1.0 / (2 * terms - 1),
                                       ALU.mult, ALU.add))
            seq.settle()
            for i in range(terms - 2, -1, -1):
                seq.mark(dve.tensor_tensor(spt[:, 3, :], spt[:, 3, :], spt[:, 1, :], ALU.mult))
                seq.settle()
                seq.mark(dve.tensor_scalar(spt[:, 3, :], spt[:, 3, :], 1.0 / (2 * i + 1), None, ALU.add))
                seq.settle()
            seq.mark(dve.tensor_tensor(spt[:, 3, :], spt[:, 3, :], spt[:, 0, :], ALU.mult))
            seq.settle()
            seq.mark(dve.scalar_tensor_tensor(spt[:, 3, :], spt[:, 3, :], 2.0, spt[:, 2, :], ALU.mult, ALU.add))
            seq.settle()
            seq.mark(dve.tensor_scalar(sp[:, 0, :], spt[:, 3, :], C_GATE, None, ALU.mult))
            seq.mark(dve.tensor_scalar(sp[:, 1, :], spt[:, 3, :], -C_GATE, None, ALU.mult))
            seq.settle()


            def conv(taps, hist, w, b, hists, free_banks, n):
                gp, gs = sp_view(convin, hist)
                for bk in free_banks:
                    dve.wait_ge(bank_free[bk], n + 1)
                dve.wait_ge(hist_ready, hists)
                yp, ys = y[:, 0:SEQ], requests(y[:, SEQ:T])
                for i in range(taps):
                    t = taps - 1 - i
                    for o, g, m in ((yp, gp[:, t:t + SEQ], "p"), (ys, gs[:, :, t:t + DEC_T], "s")):
                        if i == 0:
                            ins = dve.tensor_scalar(o, g, w(t), b, ALU.mult, ALU.add)
                        else:
                            ins = dve.scalar_tensor_tensor(o, g, w(t), o, ALU.mult, ALU.add)
                        if i < taps - 1:
                            seq.mark(ins)
                        else:
                            ins.then_inc(conv_done, 1)
                    if i < taps - 1:
                        seq.settle()

            def lru_block(c, last, start):
                seq.at = start
                for s in range(2):
                    n, kt = 4 * c, 2 * c + s
                    wait(dve, hlast_done, 2 * c)
                    wait(dve, xc_lo, kt)
                    wait(dve, z_ready, 2 * c)
                    prep(n + 1, s, KD * P)
                    conv(CONV_W, 3, lambda t: pcol[:, ds(kt, 1), C_CONVW + t], pcol[:, ds(kt, 1), C_CONVB], kt + 1,
                         (3 * s, 3 * s + 1, 3 * s + 2), n)
                    dve.wait_ge(xc_hi, kt + 1)
                    dve.tensor_tensor(xclo[:, s, :], y[:, :], xchi[:, s, :].bitcast(F32), ALU.subtract)\
                       .then_inc(xc_lo, 1)
                for s in range(2):
                    prep(4 * c + 2, s, 2 * P)
                if last:
                    for k in range(KD - 2):
                        dve.wait_ge(z_hi, k + 1)
                        dve.tensor_tensor(nlo[:, k, :], z[:, k, :], nhi[:, k, :].bitcast(F32), ALU.subtract)\
                           .then_inc(z_lo, 1)
                for m in range(2):
                    for s in range(2):
                        prep(4 * c + 3 + m, s, 2 * P if m == 0 else KD * P)
                for m in range(2):
                    n, kt = 4 * c + 2 + m, 2 * c + m
                    ta, tb = gate_tiles(c, m)
                    dve.wait_ge(xc_lo, 2 * c + 2)
                    wait(dve, hlast_done, kt)
                    wait(dve, z_ready, kt)
                    seq.mark(dve.tensor_tensor(y[:, :], xchi[:, m, :].bitcast(F32), xclo[:, m, :].bitcast(F32), ALU.add))
                    seq.settle()
                    dve.wait_ge(bank_free[5], n + 1)
                    seq.mark(dve.tensor_tensor(tb, tb, y[:, :], ALU.mult))
                    seq.settle()
                    dve.wait_ge(a_ready, kt + 1)
                    seq.mark(dve.tensor_tensor(y[:, :], ta, ta, ALU.mult))
                    seq.settle()
                    dve.scalar_tensor_tensor(y[:, :], y[:, :], 1.0, rstd[:, :], ALU.add, ALU.mult).then_inc(one_a2, 1)
                    first1, first2 = (requests(t[:, SEQ:T])[:, :, 0] for t in (ta, tb))
                    h0 = pcol[:, ds(kt, 1), C_SH:C_SH + DEC_B].rearrange("p o b -> p (o b)")
                    seq.mark(dve.tensor_tensor(h0a[:, :], first1, h0, ALU.mult))
                    seq.settle()
                    seq.mark(dve.tensor_scalar(first1, first1, 0.0, None, ALU.mult))
                    dve.wait_ge(root_ready, kt + 1)
                    seq.mark(dve.tensor_tensor(tb, tb, y[:, :], ALU.mult))
                    seq.settle()
                    seq.mark(dve.tensor_tensor(first2, first2, h0a[:, :], ALU.add))
                    seq.settle()
                    dve.tensor_tensor_scan(y[:, :], ta, tb, 0.0, ALU.mult, ALU.add).then_inc(scan_done, 1)
                    dve.wait_ge(scan_done, kt + 1)
                    zt = z[:, ds(kt, 1), :].rearrange("p o t -> p (o t)")
                    dve.tensor_tensor(zt, zt, y[:, :], ALU.mult).then_inc(z_ready, 1)

            start = seq.at
            per = 2 * 2 * (CONV_W - 1) + 2 * 7
            lru_block(0, False, start)
            with dve.Fori(1, LRU_BLOCKS - 1) as c:
                lru_block(c, False, start + c * per)
            lru_block(LRU_BLOCKS - 1, True, start + (LRU_BLOCKS - 1) * per)
            assert seq.at == start + LRU_BLOCKS * per, (seq.at, start, per)
            for k in range(KD - 2, KD):
                dve.wait_ge(z_ready, k + 1)
                dve.wait_ge(z_hi, k + 1)
                dve.tensor_tensor(nlo[:, k, :], z[:, k, :], nhi[:, k, :].bitcast(F32), ALU.subtract).then_inc(z_lo, 1)

            def residual(n, i, next_cols, bias_col=None, last=False):
                for s in range(2):
                    for c in range(3):
                        b = 3 * s + c
                        dve.wait_ge(bank_ready[b], n + 1)
                        xt = x[:, ds(2 * i + s, 1), chunk(c)].rearrange("p o t -> p (o t)")
                        if bias_col is None:
                            ins = dve.tensor_tensor(xt, bank(b, c), xt, ALU.add)
                        else:
                            ins = dve.scalar_tensor_tensor(xt, bank(b, c), pcol[:, ds(2 * i + s, 1), bias_col], xt,
                                                           ALU.add, ALU.add)
                        ins.then_inc(bank_free[b], 1)
                    if not last:
                        prep(n + 1, s, next_cols)

            with dve.Fori(0, KD // 2) as i:
                residual(N_OUT + i, i, KD * P)
            recips(1)
            norm(1, C_FN)

            FT_MARKS = 2 * (FFN_W - 1)

            def ffn(layer, n0):
                start = seq.at

                def block_(b):
                    nb = n0 + b * (FB + KD // 2)

                    def tile(j, next_cols):
                        n = nb + j
                        f = b * FB + j
                        g = layer * FT + f
                        seq.at = start + f * FT_MARKS
                        col = 20 * layer
                        conv(FFN_W, 2, lambda t: fcol[:, ds(f, 1), col + F_W + t], fcol[:, ds(f, 1), col + F_B],
                             KD + g + 1, (0, 1, 2), n)
                        prep(n + 1, 0, next_cols)
                        dve.wait_ge(gelu_done, g + 1)
                        for c in range(3):
                            dve.wait_ge(bank_ready[3 + c], n + 1)
                            dve.tensor_tensor(y[:, chunk(c)], bank(3 + c, c), y[:, chunk(c)], ALU.mult)\
                               .then_inc(bank_free[3 + c], 1)
                        for c in range(3):
                            dve.wait_ge(bank_free[3 + c], n + 1)
                            dve.wait_ge(hhi_done, 3 * g + c + 1)
                            ht = hhi[:, ds(j, 1), chunk(c)].rearrange("p o t -> p (o t)").bitcast(F32)
                            lt = hlo[:, ds(j, 1), chunk(c)].rearrange("p o t -> p (o t)")
                            dve.tensor_tensor(lt, y[:, chunk(c)], ht, ALU.subtract).then_inc(hlo_done, 1)
                        prep(n + 1, 1, next_cols)
                        dve.wait_ge(const_ready, 5)
                        dve.wait_ge(hlo_done, 3 * g + 3)

                    with dve.Fori(0, FB - 1) as j:
                        tile(j, KD * P)
                    tile(FB - 1, FB * P)
                    nd = nb + FB
                    with dve.Fori(0, KD // 2 - 1) as i:
                        residual(nd + i, i, FB * P)
                    return nd + KD // 2 - 1

                with dve.Fori(0, NFB - 1) as b:
                    residual(block_(b), KD // 2 - 1, KD * P)
                residual(block_(NFB - 1), KD // 2 - 1, KD * P, last=(layer == 1))
                seq.at = start + FT * FT_MARKS

            ffn(0, N_F0)
            dve.memset(strip_in_sb[BUCKETS:BUCKETS + 1, FV:FV + HEADS], 1.0).then_inc(strip_one, 1)
            recips(2)
            norm(2, C_KVN)

            def head_norm(i, tile_, gain):
                for c in range(3):
                    dve.wait_ge(hroot, 3 * i + c + 1)
                    seq.mark(dve.reciprocal(convin[:, chunk(c)], convin[:, chunk(c)]))
                seq.settle()
                dve.scalar_tensor_tensor(tile_, tile_, qkn[:, gain:gain + 1], convin[:, 0:T], ALU.mult, ALU.mult)\
                   .then_inc(hnorm, 1)

            for m in range(2):
                for s in range(2):
                    prep(N_KV + m + 1, s, KD * P)
            for s in range(2):
                head_norm(s, kf[:, s, :], 1)
            dve.wait_ge(bank_ready[5], N_Q)
            dve.wait_ge(hmean, 6)
            norm(3, C_BN)
            for t in range(KD):
                prep(N_Q + t // 2 + 1, t % 2, KD * P)
                head_norm(2 + t, qz[:, t, :], 0)

            def before_exp(i):
                a, e, b = steps[i]
                g = 2 * a + e
                st = stat[:, :, 4 * (i % NPB):4 * (i % NPB) + 4]
                dve.wait_ge(sc_ready, i + 1)
                if i >= NPB:
                    dve.wait_ge(pt_ready, i - NPB + 1)
                if b < NB:
                    m, k0 = 4, (0 if b > 0 else WIN)
                    sc = ps[:, 2 * (i % 2):2 * (i % 2) + 2, :].rearrange("p a (j s) -> p (a j) s", j=2)[:, :, k0:]
                    w = pb[i % NPB][:, :, k0:]
                    bs = bias[:, 4 * g:4 * g + 4, k0:]
                    sk = sinkb[:, 4 * g:4 * g + 4]
                    dve.scalar_tensor_tensor(w, sc, SCALE, bs, ALU.mult, ALU.add).then_inc(sc_read, 1)
                else:
                    m = 2
                    w = pb[i % NPB][:, :, :].rearrange("p a b -> p (a b)")[:, 0:2 * LS].rearrange("p (h s) -> p h s", h=2)
                    for h in range(2):
                        ins = dve.scalar_tensor_tensor(w[:, h, :], ps[:, 2 * (i % 2), h * LS:(h + 1) * LS], SCALE,
                                                       sbias[:, g, :], ALU.mult, ALU.add)
                    ins.then_inc(sc_read, 1)
                dve.wait_ge(sc_read, i + 1)
                seq.mark(dve.tensor_reduce(st[:, 0, 0:m], w, AX_X, ALU.max))
                seq.settle()
                if b < NB:
                    seq.mark(dve.tensor_tensor(st[:, 0, 0:m], st[:, 0, 0:m], sk, ALU.max))
                    seq.settle()
                    seq.mark(dve.tensor_tensor(st[:, 4, 0:m], sk, st[:, 0, 0:m], ALU.subtract))
                else:
                    seq.mark(dve.tensor_scalar(st[:, 0, 0:m], st[:, 0, 0:m], sinks_s[:, g:g + 1], None, ALU.max))
                    seq.settle()
                    seq.mark(dve.tensor_scalar(st[:, 4, 0:m], st[:, 0, 0:m], -1.0, sinks_s[:, g:g + 1], ALU.mult,
                                               ALU.add))
                dve.tensor_scalar(st[:, 1, 0:m], st[:, 0, 0:m], -1.0, None, ALU.mult).then_inc(max_ready, 1)

            def after_exp(i):
                a, e, b = steps[i]
                st = stat[:, :, 4 * (i % NPB):4 * (i % NPB) + 4]
                m = 4 if b < NB else 2
                dve.wait_ge(exp_done, i + 1)
                seq.mark(dve.tensor_tensor(st[:, 5, 0:m], st[:, 2, 0:m], st[:, 3, 0:m], ALU.add))
                seq.settle()
                dve.reciprocal(st[:, 6, 0:m], st[:, 5, 0:m]).then_inc(inv_ready, 1)

            def take_out(i):
                a, e, b = steps[i]
                h0 = HD * e
                dve.wait_ge(o_ready, i + 1)
                src = ps[h0:h0 + HD, 6 + i % 2, :]
                if b < NB:
                    dst = qz[h0:h0 + HD, 4 * a:4 * a + 4, b * WIN:(b + 1) * WIN]
                    dve.tensor_copy(dst, src.rearrange("p (j q) -> p j q", j=4)).then_inc(o_copied, 1)
                else:
                    dst = qz[h0:h0 + HD, 4 * a:4 * a + 4, SEQ:T].rearrange("p j (r t) -> p j r t", r=DEC_B)
                    dve.tensor_copy(dst, src[:, 0:32 * DEC_B].rearrange("p (r j t) -> p j r t", r=DEC_B, j=4))\
                       .then_inc(o_copied, 1)

            dve.wait_ge(hnorm, 2 + KD)
            for a in range(2):
                src = qz[:, 4 * a:4 * a + 4, SEQ:T].rearrange("p j (r t) -> p r j t", r=DEC_B)
                dst = convin[:, 256 * a:256 * a + 256].rearrange("p (r j t) -> p r j t", r=DEC_B, j=4)
                dve.tensor_copy(dst, src).then_inc(qs_ready, 1)
            dve.wait_ge(att_in, 16 * N_ATT_IN)

            before_exp(0)
            for i in range(NSTEP):
                if i + 1 < NSTEP:
                    before_exp(i + 1)
                after_exp(i)
                if i >= 1:
                    take_out(i - 1)
            take_out(NSTEP - 1)
            for k in range(KD):
                dve.wait_ge(z_hi, KD + k + 1)
                dve.tensor_tensor(nlo[:, k, :], qz[:, k, :], nhi[:, k, :].bitcast(F32), ALU.subtract).then_inc(z_lo, 1)
            with dve.Fori(0, KD // 2) as i:
                residual(N_O + i, i, KD * P, bias_col=C_BO)
            recips(3)
            norm(4, C_FN + 1)
            ffn(1, N_F1)
            for m in range(len(ends)):
                if m % 2 == 1:
                    dve.wait_ge(tr_ready, NSET + m + 1)
                    view, dst = end_out(m)
                    dve.tensor_copy(dst, view).then_inc(tr_dve, 1)

        @block.gpsimd
        def _(pool):
            seq = Tally(pool, pool_seq)
            seq.mark(pool.memset(ident[:, :], 0.0))
            seq.settle()
            pool.affine_select(out=ident[:, :], in_=ident[:, :], compare_op=ALU.not_equal, fill=1.0, base=0,
                               pattern=[[-1, P]], channel_multiplier=1).then_inc(const_ready, 1)
            pool.wait_ge(tr_act, n_set_act)
            pool.wait_ge(tr_dve, n_set_dve)

            def sum_squares(v):
                for c in range(3):
                    seq.mark(pool.memset(t2[:, chunk(c)], 0.0))
                seq.settle()
                if v == 0:
                    for k in range(KD):
                        for c in range(3):
                            add(v, k, c)
                else:
                    with pool.Fori(0, KD) as k:
                        for c in range(3):
                            add(v, k, c)

            def add(v, k, c):
                pool.wait_ge(sq_done, 24 * v + 3 * k + c + 1)
                if v > 0 or k > 0:
                    pool.wait_ge(sq_added, 24 * v + 3 * k + c - 2)
                pool.tensor_tensor(t2[:, chunk(c)], t2[:, chunk(c)], t1[:, chunk(c)], ALU.add).then_inc(sq_added, 1)

            sum_squares(0)

            def history(hist, src, convs, stashes):
                _, gs = sp_view(convin, hist)
                wait(pool, conv_done, convs)
                wait(pool, stash_done, stashes)
                pool.tensor_copy(gs[:, :, 0:hist], src.rearrange("p o (b w) -> p (o b) w", b=DEC_B))\
                    .then_inc(hist_ready, 1)

            def new_state(hist, dst_p, dst_s, b, n):
                gp, gs = sp_view(convin, hist)
                pool.wait_ge(bank_free[b], n + 1)
                pool.tensor_copy(dst_p, gp[:, SEQ:SEQ + hist].rearrange("p (o w) -> p o w", o=1))
                pool.tensor_copy(dst_s.rearrange("p o (b w) -> p (o b) w", b=DEC_B), gs[:, :, DEC_T:])\
                    .then_inc(stash_done, 1)

            def lru_block(c):
                for s in range(2):
                    kt = 2 * c + s
                    history(3, pcol[:, ds(kt, 1), C_SCONV:C_SCONV + 24], 2 * kt, kt)
                    pool.wait_ge(hist_ready, kt + 1)
                    new_state(3, lstash[:, ds(kt, 1), 32:35], lstash[:, ds(kt, 1), 0:24], 3 * s + 2, 4 * c)
                for m in range(2):
                    kt = 2 * c + m
                    pool.wait_ge(scan_done, kt + 1)
                    pool.tensor_copy(lstash[:, ds(kt, 1), 35:36], y[:, SEQ - 1:SEQ].rearrange("p (o t) -> p o t", o=1))
                    pool.tensor_copy(lstash[:, ds(kt, 1), 24:32].rearrange("p o b -> p (o b)"),
                                     requests(y[:, SEQ:T])[:, :, DEC_T - 1]).then_inc(hlast_done, 1)

            lru_block(0)
            with pool.Fori(1, LRU_BLOCKS) as c:
                lru_block(c)
            def ffn(layer):
                base = layer * FT
                with pool.Fori(0, FT) as f:
                    g = base + f
                    history(2, fcol[:, ds(f, 1), 20 * layer + F_S:20 * layer + F_S + 16], 2 * (KD + g), KD + g)
                    _, gs = sp_view(convin, 2)
                    gp, _ = sp_view(convin, 2)
                    pool.wait_ge(conv_done, 2 * (KD + g) + 2)
                    pool.tensor_copy(fstash[:, ds(f, 1), 0:2], gp[:, SEQ:SEQ + 2].rearrange("p (o w) -> p o w", o=1))
                    pool.tensor_copy(fstash[:, ds(f, 1), 2:18].rearrange("p o (b w) -> p (o b) w", b=DEC_B),
                                     gs[:, :, DEC_T:]).then_inc(stash_done, 1)

            pool.wait_ge(z_ready, KD)
            sum_squares(1)
            ffn(0)
            sum_squares(2)
            pool.dma_start(strip_in_sb[0:BUCKETS, FV:FV + HEADS], A["rel_bias"]).then_inc(strip_in, 16)
            pool.dma_start(strip_in_sb[:, 0:FV], A["onehot"]).then_inc(strip_in, 16)
            for i in range(NSTEP):
                a, e, b = steps[i]
                m = 4 if b < NB else 2
                inv = stat[:, 6, 4 * (i % NPB):4 * (i % NPB) + m].rearrange("p (j o) -> p j o", o=1)
                if b < NB:
                    w = pb[i % NPB][:, :, (0 if b > 0 else WIN):]
                else:
                    w = pb[i % NPB][:, :, :].rearrange("p a b -> p (a b)")[:, 0:2 * LS].rearrange("p (h s) -> p h s", h=2)
                pool.wait_ge(inv_ready, i + 1)
                pool.tensor_tensor(w, w, inv.broadcast_to([P, m, w.shape[2]]), ALU.mult).then_inc(p_ready, 1)
            pool.wait_ge(z_hi, KD + 1)
            pool.wait_ge(o_copied, NSTEP)
            sum_squares(3)
            pool.memset(convin[:, 0:FFN_W - 1], 0.0)
            pool.wait_ge(fst_cp, STATE0[1])
            ffn(1)


def onehot_strip():
    dist = (2 * WIN - 1) - np.arange(FV)
    exact = BUCKETS // 2
    d = np.maximum(dist, 0)
    df = np.maximum(d, 1).astype(np.float32)
    large = exact + (np.log(df / exact) / np.float32(np.log(WIN / exact)) * (BUCKETS - exact)).astype(np.int32)
    bucket = np.where(d < exact, d, np.minimum(large, BUCKETS - 1))
    valid = (dist >= 0) & (dist < WIN)
    rows = np.zeros((BUCKETS + 1, FV), np.float32)
    rows[bucket[valid], np.arange(FV)[valid]] = 1.0
    rows[BUCKETS, ~valid] = NEG
    return rows


_OUTS = [("y_prompt", (1, SEQ, D)), ("y_sample", (DEC_B, DEC_T, D)), ("lru_h_p", (1, 1, D)),
         ("lru_conv_p", (1, 1, CONV_W - 1, D)), ("ffn_conv_p", (2, 1, FFN_W - 1, D_FF)),
         ("k_win_p", (1, WIN, KV_HEADS, HD)), ("v_win_p", (1, WIN, KV_HEADS, HD)), ("lru_h_s", (1, DEC_B, D)),
         ("lru_conv_s", (1, DEC_B, CONV_W - 1, D)), ("ffn_conv_s", (2, DEC_B, FFN_W - 1, D_FF)),
         ("k_win_s", (DEC_B, WIN, KV_HEADS, HD)), ("v_win_s", (DEC_B, WIN, KV_HEADS, HD))]


def kernel(**inputs):
    import numpy as _np
    import concourse.bacc as _bacc
    from concourse import mybir as _mybir
    from concourse.bass_utils import run_bass_kernel_spmd as _run

    nc = _bacc.Bacc("TRN2", target_bir_lowering=False, num_devices=1)
    arrays, A = {}, {}
    for name, a in [*inputs.items(), ("onehot", onehot_strip())]:
        a = _np.ascontiguousarray(a)
        arrays[f"in_{name}"] = a
        A[name] = nc.dram_tensor(f"in_{name}", a.shape, _mybir.dt.from_np(a.dtype), kind="ExternalInput").ap()
    for name, shape in _OUTS:
        A[name] = nc.dram_tensor(f"out_{name}", shape, _mybir.dt.float32, kind="ExternalOutput").ap()
    build(nc, A)
    r = _run(nc, [arrays], core_ids=[0])
    return tuple(r.results[0][f"out_{name}"] for name, _ in _OUTS)
```

```python
from contextlib import ExitStack

import numpy as np

import concourse.bass as bass
from concourse import mybir

P = 128
F32 = mybir.dt.float32
F32R = mybir.dt.float32r
ACT = mybir.ActivationFunctionType
ALU = mybir.AluOpType
AX_X = mybir.AxisListType.X
ds = bass.ds

D = 1024
SEQ = 1024
DEC_B = 8
DEC_T = 8
NS = DEC_B * DEC_T
T = SEQ + NS
KD = D // P
LRU_BLOCKS = 4
CONV_W = 4
D_FF = 3 * D
FT = D_FF // P
FFN_W = 3
HEADS = 16
KV_HEADS = 4
HD = 64
WIN = 128
NB = SEQ // WIN
LS = WIN + DEC_T
BUCKETS = 32
EPS = 1e-6
NEG = -1e30
C_GATE = 8.0
SCALE = HD ** -0.5
CHUNKS = [(0, 384), (384, 384), (768, 320)]
FB = 6
NFB = FT // FB
FV = 384

N_A = 0
N_OUT = N_A + 4 * LRU_BLOCKS
N_F0 = N_OUT + KD // 2
N_KV = N_F0 + NFB * (FB + KD // 2)
N_Q = N_KV + 2
N_O = N_Q + KD // 2
N_F1 = N_O + KD // 2
N_END = N_F1 + NFB * (FB + KD // 2)

(C_ANORM, C_CONVW, C_CONVB, C_RB, C_IB, C_LAM, C_KVN, C_BN, C_FN, C_BO, C_BQ, C_BKV, C_SCONV, C_SH) = \
    (0, 1, 5, 6, 7, 8, 9, 10, 11, 13, 14, 15, 16, 40)
NPROW = 48
N_PRM, N_FRM = 18, 10
NPB = 3
N_ATT_IN = 36
LROW = 36
NFROW = 40
F_W, F_B, F_S = 0, 3, 4


class Tally:

    def __init__(self, eng, sem):
        self.eng, self.sem, self.at = eng, sem, 0

    def mark(self, ins):
        ins.then_inc(self.sem, 1)
        self.at = self.at + 1

    def settle(self):
        self.eng.wait_ge(self.sem, self.at)


def wait(eng, sem, value):
    if not isinstance(value, int) or value > 0:
        eng.wait_ge(sem, value)


def build(nc, A):
    with ExitStack() as ctx:
        def sem(name):
            return ctx.enter_context(nc.semaphore(name))

        base = (nc.sbuf_base + 63) // 64 * 64
        top = [base]

        def at(name, shape, dt, offset):
            return nc.alloc_sbuf_tensor_at(name, shape, dt, offset=offset)

        def take(name, shape, dt):
            offset = top[0]
            top[0] += (int(np.prod(shape[1:])) * 4 + 31) // 32 * 32
            return at(name, shape, dt, offset)

        x = take("x", [P, KD, T], F32)
        reg_n = top[0]
        nhi = take("nhi", [P, KD, T], F32R)
        nlo = take("nlo", [P, KD, T], F32R)
        reg_h = top[0]
        hhi = take("hhi", [P, FB, T], F32R)
        hlo = take("hlo", [P, FB, T], F32R)
        raw = [take(f"raw{s}", [P, KD * P], F32) for s in range(2)]
        whi = [take(f"whi{s}", [P, KD * P], F32R) for s in range(2)]
        wlo = [take(f"wlo{s}", [P, KD * P], F32R) for s in range(2)]
        convin = take("convin", [P, 1120], F32)
        y = take("y", [P, T], F32)
        rstd = take("rstd", [P, T], F32)
        t1 = take("t1", [P, T], F32)
        t2 = take("t2", [P, T], F32)
        pcol = take("pcol", [P, KD, NPROW + 4], F32)
        lstash = pcol[:, :, C_SCONV:C_SCONV + LROW]
        fcol = take("fcol", [P, FT, NFROW], F32)
        fstash = take("fstash", [P, FT, 2 + 2 * DEC_B], F32)
        ident = take("ident", [P, P], F32)
        ones = take("ones", [P, P], F32)
        blockones = take("blockones", [P, P], F32)
        epst = take("epst", [P, 1], F32)
        qkn = take("qkn", [P, 2], F32)
        sp = take("sp", [P, 2, KD], F32)
        spt = take("spt", [P, 4, KD], F32)
        h0a = take("h0a", [P, DEC_B], F32)
        sinkb = take("sinkb", [P, HEADS], F32)
        sinks_s = take("sinks_s", [P, KV_HEADS], F32)
        stat = take("stat", [P, 8, 4 * NPB], F32)
        assert top[0] <= nc.sbuf_usable_end, top[0]

        z = at("z", [P, KD, T], F32, reg_h)
        xchi = at("xchi", [P, 2, T], F32R, reg_h + KD * T * 4)
        xclo = at("xclo", [P, 2, T], F32R, reg_h + (KD + 2) * T * 4)
        xrows = at("xrows", [P, 9, D], F32, reg_h)
        prow = xrows[NS:NS + NPROW, 8, :]
        frow = at("frow", [NFROW, D_FF], F32, reg_h + 9 * D * 4)
        qz = at("qz", [P, KD, T], F32, reg_h)
        kf = at("kf", [P, 2, T], F32, reg_h + KD * T * 4)
        vt = at("vt", [P, NB, 256], F32, reg_h + (KD + 2) * T * 4)
        tlast = at("tlast", [P, 2, T], F32, reg_n + (2 * KD - 2) * T * 4)
        top[0] = reg_n
        bias = take("bias", [P, HEADS, 2 * WIN], F32)
        sbias = take("sbias", [P, KV_HEADS, LS], F32)
        ck = take("ck", [P, DEC_B, 256], F32)
        kct = take("kct", [P, 2, DEC_B * WIN], F32)
        cv = take("cv", [P, DEC_B, 256], F32)
        vnew = take("vnew", [DEC_T, DEC_B, 256], F32)
        pb = [take("pb0", [P, 4, 2 * WIN], F32), take("pb1", [P, 4, 2 * WIN], F32),
              y[:, 0:8 * WIN].rearrange("p (j s) -> p j s", j=4)]
        pt = take("pt", [P, 2, 512], F32)
        kvrow = take("kvrow", [P, 2, 256], F32)
        assert top[0] <= reg_h
        yrows = at("yrows", [P, 9, D], F32, reg_n)
        fout = at("fout", [18, D_FF], F32, reg_h)
        lout = at("lout", [LROW, D], F32, reg_h + D_FF * 4)

        ps = ctx.enter_context(nc.psum_tensor("ps", [P, 8, 512], F32))

        raw_ready = [sem(f"raw_ready{s}") for s in range(2)]
        hi_ready = [sem(f"hi_ready{s}") for s in range(2)]
        lo_ready = [sem(f"lo_ready{s}") for s in range(2)]
        bank_ready = [sem(f"bank_ready{b}") for b in range(6)]
        bank_free = [sem(f"bank_free{b}") for b in range(6)]
        rows_in = [sem(f"rows_in{i}") for i in range(3)]
        const_ready = sem("const_ready")
        prm_in = sem("prm_in")
        frm_in = sem("frm_in")
        sq_dve = sem("sq_dve")
        tr_ready = sem("tr_ready")
        tr_act = sem("tr_act")
        tr_dve = sem("tr_dve")
        dve_seq = sem("dve_seq")
        pool_seq = sem("pool_seq")
        sq_done = sem("sq_done")
        sq_added = sem("sq_added")
        stat_ready = sem("stat_ready")
        stat_sqrt = sem("stat_sqrt")
        xn_mult = sem("xn_mult")
        xn_hi = sem("xn_hi")
        xn_lo = sem("xn_lo")
        sp_exp = sem("sp_exp")
        sp_ready = sem("sp_ready")
        hist_ready = sem("hist_ready")
        conv_done = sem("conv_done")
        stash_done = sem("stash_done")
        gelu_done = sem("gelu_done")
        hhi_done = sem("hhi_done")
        hlo_done = sem("hlo_done")
        xc_hi = sem("xc_hi")
        xc_lo = sem("xc_lo")
        tanh_done = sem("tanh_done")
        a_ready = sem("a_ready")
        one_a2 = sem("one_a2")
        root_ready = sem("root_ready")
        scan_done = sem("scan_done")
        hlast_done = sem("hlast_done")
        z_ready = sem("z_ready")
        z_hi = sem("z_hi")
        z_lo = sem("z_lo")
        fst_tr = sem("fst_tr")
        fst_cp = sem("fst_cp")
        states_out = sem("states_out")
        win_out = sem("win_out")
        y_out = sem("y_out")
        strip_in = sem("strip_in")
        strip_one = sem("strip_one")
        strip_mm = sem("strip_mm")
        strip_cp = sem("strip_cp")
        strip_out = sem("strip_out")
        att_in = sem("att_in")
        vnew_in = sem("vnew_in")
        hsq = sem("hsq")
        hmean = sem("hmean")
        hroot = sem("hroot")
        hnorm = sem("hnorm")
        prep_tr = sem("prep_tr")
        prep_cp = sem("prep_cp")
        qs_ready = sem("qs_ready")
        sc_ready = sem("sc_ready")
        sc_read = sem("sc_read")
        max_ready = sem("max_ready")
        exp_done = sem("exp_done")
        inv_ready = sem("inv_ready")
        p_ready = sem("p_ready")
        pt_ready = sem("pt_ready")
        pt_copied = sem("pt_copied")
        o_ready = sem("o_ready")
        o_copied = sem("o_copied")
        qkv_ev = sem("qkv_ev")

        strip_dram = nc.dram_tensor("strip", [HEADS * P * FV], F32, kind="Internal").ap()
        strip_in_sb = at("strip_in_sb", [BUCKETS + 1, FV + HEADS], F32, reg_h + (KD + 2) * T * 4)
        strip_sb2 = at("strip_sb2", [HEADS, FV], F32, reg_h + (KD + 2) * T * 4 + 4 * (FV + HEADS))

        def chunk(c):
            return ds(CHUNKS[c][0], CHUNKS[c][1])

        def bank(b, c):
            return ps[:, b, 0:CHUNKS[c][1]]

        def sp_view(buf, hist):
            w = SEQ + hist
            return buf[:, 0:w], buf[:, w:w + DEC_B * (DEC_T + hist)].rearrange("p (b t) -> p b t", b=DEC_B)

        def gate_tiles(c, m):
            if m == 0:
                return t1[:, :], t2[:, :]
            if isinstance(c, int) and c == LRU_BLOCKS - 1:
                return tlast[:, 0, :], tlast[:, 1, :]
            return tuple(z[:, ds(2 * c + 2 + i, 1), :].rearrange("p o t -> p (o t)") for i in range(2))

        def requests(ap):
            return ap.rearrange("p (b t) -> p b t", b=DEC_B)

        def w_cols(w, col):
            return w.rearrange("(k p) n -> p k n", p=P)[:, :, ds(col, P)]

        setup = [("x", tt, half) for tt in range(3) for half in range(2)]
        setup += [("p", half) for half in range(2)]
        setup += [("x", tt, half) for tt in range(3, 9) for half in range(2)]
        setup += [("f", half) for half in range(2)]
        SET_BANK = [0, 1, 2, 3, 4, 5] + [0, 1] + [2, 3, 4, 5, 0, 1] + [2, 1, 4, 5, 2, 1] + [4, 5]
        SET_END = [8, 14, 22]
        NSET = len(setup)

        def sq_base(v):
            return 0 if v == 0 else 24 * v - 12

        def job_out(job, bank_no):
            if job[0] == "p":
                h = job[1]
                return (ps[:, bank_no, 0:4 * NPROW].rearrange("p (k c) -> p k c", k=4), pcol[:, 4 * h:4 * h + 4, 0:NPROW])
            if job[0] == "f":
                h = job[1]
                return (ps[:, bank_no, 0:12 * NFROW].rearrange("p (k c) -> p k c", k=12),
                        fcol[:, 12 * h:12 * h + 12, :])
            _, tt, h = job
            w = P if tt < 8 else NS
            return (ps[:, bank_no, 0:4 * w].rearrange("p (k c) -> p k c", k=4),
                    x[:, 4 * h:4 * h + 4, tt * P:tt * P + w])

        ends = [(tt, half) for tt in range(9) for half in range(2)]
        TR_DVE_END, TR_ACT_END = [], []
        n_set_act, n_set_dve = (NSET + 1) // 2, NSET // 2
        for g in range(3):
            m = 6 * (g + 1)
            TR_ACT_END.append(n_set_act + (m + 1) // 2)
            TR_DVE_END.append(n_set_dve + m // 2)

        def end_out(m):
            tt, h = ends[m]
            w = P if tt < 8 else NS
            return ps[0:w, m % 8, :], yrows[0:w, tt, 512 * h:512 * h + 512]

        steps = [(a, e, b) for a in range(2) for e in range(2) for b in range(NB + 1)]
        NSTEP = len(steps)

        STATE0 = [0, 8, 14]

        def state_jobs(layer):
            jobs = []
            if layer == 0:
                for m in range(2):
                    b = 6 + len(jobs) % 2
                    outs = [(ps[0:LROW, b, i * P:(i + 1) * P], lstash[:, 4 * m + i, :]) for i in range(4)]
                    jobs.append((outs, ps[0:LROW, b, :], lout[:, m * 512:(m + 1) * 512]))
            for m in range(FT // 4):
                b = 6 + len(jobs) % 2
                outs = [(ps[0:18, b, i * P:(i + 1) * P], fstash[:, 4 * m + i, :]) for i in range(4)]
                jobs.append((outs, ps[0:18, b, :], fout[:, m * 512:(m + 1) * 512]))
            return jobs

        PREP_CK0 = 6

        def prep_jobs():
            jobs = []
            for m in range(4):
                outs = []
                for q in range(4):
                    blk, a = 2 * m + q // 2, q % 2
                    src = (t1, t2)[a]
                    outs.append((ps[:, m, q * P:(q + 1) * P], src[:, blk * P:(blk + 1) * P]))
                jobs.append((outs, ps[:, m, :].rearrange("p (b c) -> p b c", b=2), vt[:, 2 * m:2 * m + 2, :]))
            outs = [(ps[:, 4, a * P:(a + 1) * P], kf[:, a, SEQ - WIN:SEQ]) for a in range(2)]
            jobs.append((outs, ps[:, 4, 0:256], kvrow[:, 0, :]))
            outs = [(ps[0:NS, 5, a * P:(a + 1) * P], kf[:, a, SEQ:T]) for a in range(2)]
            outs += [(ps[0:NS, 5, 256 + a * P:256 + (a + 1) * P], (t1, t2)[a][:, SEQ:T]) for a in range(2)]
            jobs.append((outs, ps[0:NS, 5, :].rearrange("p (b c) -> p b c", b=2), None))
            for m in range(4):
                outs = []
                for q in range(4):
                    r, a = 4 * (m % 2) + q, m // 2
                    outs.append((ps[:, (6 + m) % 8, q * P:(q + 1) * P], ck[:, r, a * P:(a + 1) * P]))
                jobs.append((outs, ps[:, (6 + m) % 8, :], kct[:, m // 2, 512 * (m % 2):512 * (m % 2) + 512]))
            return jobs

        block = ctx.enter_context(nc.Block())

        @block.sync
        def _(eng):
            def token_rows(g):
                if g < 2:
                    src = A["x_prompt"][0, 384 * g:384 * g + 384, :].rearrange("(i p) d -> p i d", p=P)
                    eng.dma_start(xrows[:, 3 * g:3 * g + 3, :], src).then_inc(rows_in[g], 16)
                else:
                    src = A["x_prompt"][0, 768:1024, :].rearrange("(i p) d -> p i d", p=P)
                    eng.dma_start(xrows[:, 6:8, :], src).then_inc(rows_in[g], 16)
                    eng.dma_start(xrows[0:NS, 8, :], A["x_sample"].rearrange("b t d -> (b t) d"))\
                       .then_inc(rows_in[g], 16)

            def load(n, s, src, cols):
                if not isinstance(n, int):
                    n = eng.snap(eng.to_reg(n))
                    eng.wait_ge(rows_in[0], 16)
                wait(eng, lo_ready[s], n)
                eng.dma_start(raw[s][:, 0:cols].rearrange("p (k n) -> p k n", n=P), src).then_inc(raw_ready[s], 16)

            w_in, w_out = A["a_w_in"][0], A["a_w_out"][0]

            def gate_w(w, c, m):
                return w[0][ds(c, 1), :, m * P:(m + 1) * P].rearrange("a (k p) n -> p (a k) n", p=P)

            def conv_loads(c):
                for s in range(2):
                    load(4 * c, s, w_cols(w_in, D + c * 256 + s * P), KD * P)

            def lru_loads(c):
                if not isinstance(c, int):
                    conv_loads(c)
                for s in range(2):
                    load(4 * c + 1, s, w_cols(w_in, c * 256 + s * P), KD * P)
                for m in range(2):
                    load(4 * c + 2 + m, 0, gate_w(A["a_gate_r_w"], c, m), 2 * P)
                    load(4 * c + 2 + m, 1, gate_w(A["a_gate_i_w"], c, m), 2 * P)

            token_rows(0)
            token_rows(1)
            conv_loads(0)
            token_rows(2)
            count = 0
            for layer in range(2):
                o = 20 * layer
                for r, src in ((0, A["f_conv_w"][layer]), (3, A["f_conv_b"][layer:layer + 1, :]),
                               (4, A["state_ffn_conv"][layer].rearrange("b w d -> (b w) d"))):
                    eng.dma_start(frow[o + r:o + r + src.shape[0], :], src).then_inc(frm_in, 16)
                    count += 1
            with nc.allow_non_contiguous_dma(reason="64 single elements each"):
                for e in range(2):
                    for i, name in enumerate(("q_norm", "k_norm")):
                        src = A[name][0, :] if name == "q_norm" else A[name]
                        eng.dma_start(qkn[HD * e:HD * e + HD, i:i + 1], src.rearrange("(d o) -> d o", o=1))\
                           .then_inc(frm_in, 16)
                        count += 1
            assert count == N_FRM, count
            lru_loads(0)
            with eng.Fori(1, LRU_BLOCKS) as c:
                lru_loads(c)
            with eng.Fori(0, KD // 2) as i:
                for s in range(2):
                    load(N_OUT + i, s, w_cols(w_out, i * 256 + s * P), KD * P)

            def ffn(layer, n0):
                up, down = A["f_w_up"][layer], A["f_w_down"][layer]
                with eng.Fori(0, NFB) as b:
                    with eng.Fori(0, FB) as j:
                        for s in range(2):
                            load(n0 + b * (FB + KD // 2) + j, s, w_cols(up, s * D_FF + b * (FB * P) + j * P), KD * P)
                    with eng.Fori(0, KD // 2) as i:
                        for s in range(2):
                            src = down.rearrange("(k p) n -> p k n", p=P)[:, ds(b * FB, FB), ds(i * 256 + s * P, P)]
                            load(n0 + b * (FB + KD // 2) + FB + i, s, src, FB * P)

            ffn(0, N_F0)
            for m in range(2):
                for s in range(2):
                    load(N_KV + m, s, w_cols(A["w_kv"], (2 * m + s) * P), KD * P)
            wq = A["w_q"][0].rearrange("(k p) (a e j d) -> p k a e j d", p=P, a=2, e=2, j=4)
            for t in range(KD):
                a, j, n, s = t // 4, t % 4, N_Q + t // 2, t % 2
                eng.wait_ge(lo_ready[s], n)
                for e in range(2):
                    dst = raw[s][:, :].rearrange("p (k e d) -> p k e d", k=KD, e=2)[:, :, e, :]
                    eng.dma_start(dst, wq[:, :, a, e, j, :]).then_inc(raw_ready[s], 16)
            wo = A["w_o"][0].rearrange("(a e j d) n -> d a e j n", a=2, e=2, j=4)
            for t in range(KD):
                n, s = N_O + t // 2, t % 2
                eng.wait_ge(lo_ready[s], n)
                for e in range(2):
                    for a in range(2):
                        dst = raw[s][HD * e:HD * e + HD, a * 512:a * 512 + 512].rearrange("p (j n) -> p j n", j=4)
                        eng.dma_start(dst, wo[:, a, e, :, t * P:(t + 1) * P]).then_inc(raw_ready[s], 16)
            ffn(1, N_F1)

            for g in range(3):
                eng.wait_ge(tr_dve, TR_DVE_END[g])
                eng.wait_ge(tr_act, TR_ACT_END[g])
                if g < 2:
                    dst = A["y_prompt"][0, 384 * g:384 * g + 384, :].rearrange("(i p) d -> p i d", p=P)
                    eng.dma_start(dst, yrows[:, 3 * g:3 * g + 3, :]).then_inc(y_out, 16)
                else:
                    dst = A["y_prompt"][0, 768:1024, :].rearrange("(i p) d -> p i d", p=P)
                    eng.dma_start(dst, yrows[:, 6:8, :]).then_inc(y_out, 16)
                    eng.dma_start(A["y_sample"].rearrange("b t d -> (b t) d"), yrows[0:NS, 8, :])\
                       .then_inc(y_out, 16)
            eng.wait_ge(y_out, 16 * 4)

        def raw_count_at(n, phase):
            q, o = KD // 2, KD // 2
            if phase == "q":
                return 16 * (N_Q + 2 * (n - N_Q + 1))
            if phase == "o":
                return 16 * (N_Q + 2 * q + 4 * (n - N_O + 1))
            if phase == "f1":
                return 16 * (n + 1) + 16 * (q + 3 * o)
            return 16 * (n + 1)

        @block.tensor
        def _(pe):
            pe.wait_ge(const_ready, 4)

            def set_up(first, end):
                for m in range(first, end):
                    job, bk = setup[m], SET_BANK[m]
                    before_m = [i for i in range(m) if SET_BANK[i] == bk]
                    if before_m:
                        pe.wait_ge(tr_act if before_m[-1] % 2 == 0 else tr_dve, before_m[-1] // 2 + 1)
                    if job[0] == "p":
                        pe.wait_ge(prm_in, 16 * N_PRM)
                        for i in range(4):
                            k = 4 * job[1] + i
                            last = pe.transpose(ps[:, bk, i * NPROW:(i + 1) * NPROW], prow[:, k * P:(k + 1) * P],
                                                ident[NS:NS + NPROW, NS:NS + NPROW])
                    elif job[0] == "f":
                        pe.wait_ge(frm_in, 16 * N_FRM)
                        for i in range(12):
                            k = 12 * job[1] + i
                            last = pe.transpose(ps[:, bk, i * NFROW:(i + 1) * NFROW], frow[:, k * P:(k + 1) * P],
                                                ident[0:NFROW, 0:NFROW])
                    else:
                        _, tt, h = job
                        w = P if tt < 8 else NS
                        pe.wait_ge(rows_in[tt // 3], 32 if tt >= 6 else 16)
                        for i in range(4):
                            k = 4 * h + i
                            last = pe.transpose(ps[:, bk, i * w:(i + 1) * w], xrows[0:w, tt, k * P:(k + 1) * P],
                                                ident[0:w, 0:w])
                    last.then_inc(tr_ready, 1)

            def piece(n, s, c, nk, mhi, mlo, before=None):
                wait(pe, bank_free[3 * s + c], n)
                out = bank(3 * s + c, c)
                for k in range(nk):
                    if before:
                        before(c, k)
                    w = ds(k * P, P)
                    pe.matmul(out, whi[s][:, w], mhi[:, k, chunk(c)], start=(k == 0), stop=False)
                    pe.matmul(out, whi[s][:, w], mlo[:, k, chunk(c)], start=False, stop=False)
                    last = pe.matmul(out, wlo[s][:, w], mhi[:, k, chunk(c)], start=False, stop=(k == nk - 1))
                last.then_inc(bank_ready[3 * s + c], 1)

            def unit(n, s, nk, mhi, mlo, before=None, stats_of=None):
                pe.wait_ge(hi_ready[s], n + 1)
                pe.wait_ge(lo_ready[s], n + 1)
                for c in range(3):
                    if c == 2 and stats_of is not None:
                        stats(stats_of, 0)
                    piece(n, s, c, nk, mhi, mlo, before)

            def stats(v, c):
                if v == 0:
                    pe.wait_ge(sq_added, 4 * c + 4)
                    pe.wait_ge(sq_dve, c + 1)
                else:
                    pe.wait_ge(sq_added, sq_base(v) + 22 + c)
                if c == 2:
                    pe.wait_ge(stat_sqrt, 3 * v + 1)
                out = bank(6 + c % 2, c)
                last = pe.matmul(out, ones[:, :], t2[:, chunk(c)], start=True, stop=(v > 0))
                if v == 0:
                    last = pe.matmul(out, ones[:, :], convin[:, ds(384, CHUNKS[c][1])], start=False, stop=True)
                last.then_inc(stat_ready, 1)

            def first_pair(n, u, v):
                if v is not None:
                    stats(v, 1)
                for c in range(3):
                    for s in range(2):
                        if c == 0:
                            pe.wait_ge(hi_ready[s], n + 1)
                            pe.wait_ge(lo_ready[s], n + 1)
                        piece(n, s, c, KD, nhi, nlo, normed(u) if s == 0 else None)
                        if c == 0 and s == 0 and v:
                            stats(v, 2)
                    if c == 0 and v == 0:
                        set_up(SET_END[1], SET_END[2])
                        stats(0, 2)
                        pe.wait_ge(tr_act, n_set_act)
                        pe.wait_ge(tr_dve, n_set_dve)

            def normed(u):
                def before(c, k):
                    if k % 2 == 0:
                        pe.wait_ge(xn_lo, 24 * u + 8 * c + k + 2)
                return before

            set_up(0, SET_END[1])
            pe.wait_ge(tr_act, SET_END[1] // 2)
            pe.wait_ge(tr_dve, SET_END[1] // 2)
            stats(0, 0)

            def lru_block(c, first=False):
                if first:
                    first_pair(0, 0, 0)
                else:
                    for s in range(2):
                        unit(4 * c, s, KD, nhi, nlo)
                for s in range(2):
                    unit(4 * c + 1, s, KD, nhi, nlo)
                pe.wait_ge(xc_lo, 2 * c + 2)
                for m in range(2):
                    for s in range(2):
                        unit(4 * c + 2 + m, s, 2, xchi, xclo)

            lru_block(0, first=True)
            with pe.Fori(1, LRU_BLOCKS) as c:
                lru_block(c)

            def z_split(base_count):
                def before(c, k):
                    pe.wait_ge(z_lo, base_count + k + 1)
                return before

            for ks in (range(KD - 2), range(KD - 2, KD)):
                for s in range(2):
                    if ks[0] == 0:
                        pe.wait_ge(hi_ready[s], N_OUT + 1)
                        pe.wait_ge(lo_ready[s], N_OUT + 1)
                    for c in range(3):
                        if ks[0] == 0:
                            pe.wait_ge(bank_free[3 * s + c], N_OUT)
                        for k in ks:
                            pe.wait_ge(z_lo, k + 1)
                            w, out = ds(k * P, P), bank(3 * s + c, c)
                            pe.matmul(out, whi[s][:, w], nhi[:, k, chunk(c)], start=(k == 0), stop=False)
                            pe.matmul(out, whi[s][:, w], nlo[:, k, chunk(c)], start=False, stop=False)
                            last = pe.matmul(out, wlo[s][:, w], nhi[:, k, chunk(c)], start=False, stop=(k == KD - 1))
                        if ks[0] > 0:
                            last.then_inc(bank_ready[3 * s + c], 1)
            with pe.Fori(1, KD // 2 - 1) as i:
                for s in range(2):
                    unit(N_OUT + i, s, KD, nhi, nlo)
            for s in range(2):
                unit(N_F0 - 1, s, KD, nhi, nlo, stats_of=1 if s == 1 else None)

            def ffn(layer, n0, u, v):
                def block_(b, first, last):
                    nb = n0 + b * (FB + KD // 2)
                    f1 = layer * FT + b * FB + FB
                    if first:
                        first_pair(nb, u, v)
                    with pe.Fori(1 if first else 0, FB) as j:
                        unit(nb + j, 0, KD, nhi, nlo)
                        unit(nb + j, 1, KD, nhi, nlo)

                    def hidden(c, k):
                        if c == 0 and k == 0:
                            pe.wait_ge(hlo_done, 3 * f1 - 3)
                        if k == FB - 1:
                            pe.wait_ge(hlo_done, 3 * f1 - 2 + c)
                    with pe.Fori(0, KD // 2 - last) as i:
                        for s in range(2):
                            unit(nb + FB + i, s, FB, hhi, hlo, hidden if s == 0 else None)
                    if last:
                        for s in range(2):
                            unit(nb + FB + KD // 2 - 1, s, FB, hhi, hlo, stats_of=2 if layer == 0 and s == 1 else None)

                block_(0, True, False)
                with pe.Fori(1, NFB - 1) as b:
                    block_(b, False, False)
                block_(NFB - 1, False, True)

            def states(layer):
                pe.wait_ge(stash_done, KD + (layer + 1) * FT)
                if layer == 0:
                    pe.wait_ge(hlast_done, KD)
                for m, (outs, _, _) in enumerate(state_jobs(layer)):
                    if m >= 2:
                        pe.wait_ge(fst_cp, STATE0[layer] + m - 1)
                    for o, t in outs:
                        last = pe.transpose(o, t, ident[:, :])
                    last.then_inc(fst_tr, 1)
                pe.wait_ge(fst_cp, STATE0[layer + 1])

            ffn(0, N_F0, 1, 1)
            first_pair(N_KV, 2, 2)
            for s in range(2):
                unit(N_KV + 1, s, KD, nhi, nlo)
            states(0)
            def head_stats(i):
                for c in range(3):
                    pe.wait_ge(hsq, i + 1)
                    if 3 * i + c >= 2:
                        pe.wait_ge(hroot, 3 * i + c - 1)
                    pe.matmul(bank(6 + (3 * i + c) % 2, c), blockones[:, :], y[:, chunk(c)], start=True, stop=True)\
                      .then_inc(hmean, 1)

            pe.wait_ge(strip_in, 32)
            pe.wait_ge(strip_one, 1)
            head_stats(0)
            head_stats(1)
            pe.wait_ge(hroot, 6)
            pe.matmul(ps[0:HEADS, 6, 0:FV], strip_in_sb[:, FV:FV + HEADS], strip_in_sb[:, 0:FV], start=True,
                      stop=True).then_inc(strip_mm, 1)
            pe.wait_ge(strip_cp, 1)
            first_pair(N_Q, 3, None)
            head_stats(2)
            for t in range(2, KD):
                unit(N_Q + t // 2, t % 2, KD, nhi, nlo)
                head_stats(2 + t - 1)
            head_stats(2 + KD - 1)

            pe.wait_ge(hroot, 3 * (2 + KD))
            pe.wait_ge(hnorm, 2 + KD)
            for b in range(6):
                pe.wait_ge(bank_free[b], N_O)
            jobs = prep_jobs()
            for m, (outs, _, _) in enumerate(jobs):
                if m >= 8:
                    pe.wait_ge(prep_cp, m - 7)
                if m == PREP_CK0:
                    pe.wait_ge(att_in, 16 * N_ATT_IN)
                for o, i in outs:
                    last = pe.transpose(o, i, ident[0:i.shape[0], 0:i.shape[0]])
                last.then_inc(prep_tr, 1)
            pe.wait_ge(prep_cp, len(jobs))
            pe.wait_ge(att_in, 16 * N_ATT_IN)
            pe.wait_ge(vnew_in, 16 * DEC_B)
            pe.wait_ge(qs_ready, 2)

            def scores(i):
                a, e, b = steps[i]
                h0 = HD * e
                if i >= 2:
                    pe.wait_ge(sc_read, i - 1)
                if b < NB:
                    k0 = 0 if b > 0 else WIN
                    for j in range(4):
                        out = ps[:, 2 * (i % 2) + j // 2, (j % 2) * 256 + k0:(j % 2) * 256 + 256]
                        last = pe.matmul(out, qz[h0:h0 + HD, 4 * a + j, b * WIN:(b + 1) * WIN],
                                         kf[h0:h0 + HD, a, (b - 1) * WIN + k0:(b + 1) * WIN], start=True, stop=True)
                else:
                    for r in range(DEC_B):
                        new = ds(SEQ + r * DEC_T, DEC_T)
                        q = convin[h0:h0 + HD, ds(256 * a + 32 * r, 32)]
                        o0 = 32 * (r % 4)
                        c0 = LS * (r // 4)
                        pe.matmul(ps[o0:o0 + 32, 2 * (i % 2), c0:c0 + WIN], q, kct[h0:h0 + HD, a, r * WIN:(r + 1) * WIN],
                                  start=True, stop=True)
                        last = pe.matmul(ps[o0:o0 + 32, 2 * (i % 2), c0 + WIN:c0 + LS], q, kf[h0:h0 + HD, a, new],
                                         start=True, stop=True)
                last.then_inc(sc_ready, 1)

            def transposes(i):
                a, e, b = steps[i]
                pe.wait_ge(p_ready, i + 1)
                if i >= 1:
                    pe.wait_ge(pt_copied, i)
                if b < NB:
                    for h in range(0 if b > 0 else 1, 2):
                        for j in range(4):
                            last = pe.transpose(ps[:, 4 + h, j * P:(j + 1) * P], pb[i % NPB][:, j, h * P:(h + 1) * P],
                                                ident[:, :])
                else:
                    flat = pb[i % NPB][:, :, :].rearrange("p a b -> p (a b)")
                    for h in range(2):
                        pe.transpose(ps[:, 4, h * P:(h + 1) * P], flat[:, h * LS:h * LS + WIN], ident[:, :])
                        last = pe.transpose(ps[0:DEC_T, 5, h * P:(h + 1) * P], flat[:, h * LS + WIN:(h + 1) * LS],
                                            ident[:, :])
                last.then_inc(pt_ready, 1)

            def values(i):
                a, e, b = steps[i]
                h0, g = HD * e, 2 * a + e
                out = 6 + i % 2
                pe.wait_ge(pt_copied, i + 1)
                if i >= 2:
                    pe.wait_ge(o_copied, i - 1)
                col = ds(g * HD, HD)
                if b < NB:
                    for h in range(0 if b > 0 else 1, 2):
                        last = pe.matmul(ps[h0:h0 + HD, out, :], vt[:, b - 1 + h, col], pt[:, h, :],
                                         start=(h == 0 or b == 0), stop=(h == 1))
                else:
                    for r in range(DEC_B):
                        c0 = 32 * r
                        pe.matmul(ps[h0:h0 + HD, out, c0:c0 + 32], cv[:, r, col], pt[:, 0, c0:c0 + 32],
                                  start=True, stop=False)
                        last = pe.matmul(ps[h0:h0 + HD, out, c0:c0 + 32], vnew[:, r, col], pt[0:DEC_T, 1, c0:c0 + 32],
                                         start=False, stop=True)
                last.then_inc(o_ready, 1)

            scores(0)
            scores(1)
            for i in range(NSTEP):
                if i + 2 < NSTEP:
                    scores(i + 2)
                if i >= 1:
                    values(i - 1)
                transposes(i)
            values(NSTEP - 1)
            pe.wait_ge(sc_read, NSTEP)
            pe.wait_ge(pt_copied, NSTEP)
            pe.wait_ge(o_copied, NSTEP)

            unit(N_O, 0, KD, nhi, nlo, z_split(KD))
            unit(N_O, 1, KD, nhi, nlo)
            with pe.Fori(1, KD // 2 - 1) as i:
                for s in range(2):
                    unit(N_O + i, s, KD, nhi, nlo)
            for s in range(2):
                unit(N_F1 - 1, s, KD, nhi, nlo, stats_of=3 if s == 1 else None)
            ffn(1, N_F1, 4, 3)
            states(1)

            for b in range(6):
                pe.wait_ge(bank_free[b], N_END)
            for m, (tt, h) in enumerate(ends):
                if m >= 8:
                    pe.wait_ge(tr_act if m % 2 == 0 else tr_dve,
                               (n_set_act if m % 2 == 0 else n_set_dve) + (m - 8) // 2 + 1)
                w = P if tt < 8 else NS
                for i in range(4):
                    last = pe.transpose(ps[0:w, m % 8, i * P:(i + 1) * P], x[:, 4 * h + i, tt * P:tt * P + w],
                                        ident[:, :])
                last.then_inc(tr_ready, 1)

        @block.scalar
        def _(act):
            rows = [(0, A["a_norm"]), (1, A["a_conv_w"][0]), (5, A["a_conv_b"]), (6, A["a_gate_r_b"]),
                    (7, A["a_gate_i_b"]), (8, A["a_lambda"]), (9, A["kv_norm"].rearrange("(a d) -> a d", a=1)),
                    (10, A["b_norm"]), (11, A["f_norm"]), (13, A["b_o"]),
                    (16, A["state_lru_conv"][0].rearrange("b w d -> (b w) d")), (40, A["state_lru_h"][0])]
            count = 0
            for r, src in rows:
                act.dma_start(prow[r:r + src.shape[0], :], src).then_inc(prm_in, 16)
                count += 1
            bq = A["b_q"].rearrange("o (a e j d) -> o a e j d", a=2, e=2, j=4)
            for e in range(2):
                for a in range(2):
                    dst = prow[14:15, a * 512:a * 512 + 512].rearrange("o (j e d) -> o j e d", j=4, e=2)[:, :, e, :]
                    act.dma_start(dst, bq[:, a, e, :, :]).then_inc(prm_in, 16)
                    count += 1
            for h in range(2):
                act.dma_start(prow[15:16, 512 * h:512 * h + 512], A["b_kv"].rearrange("(a d) -> a d", a=1))\
                   .then_inc(prm_in, 16)
                count += 1
            assert count == N_PRM, count

            def set_up(first, end):
                for m in range(first, end, 2):
                    act.wait_ge(tr_ready, m + 1)
                    view, dst = job_out(setup[m], SET_BANK[m])
                    act.activation(dst, view, ACT.Copy).then_inc(tr_act, 1)

            def prep(n, s, cols, phase=""):
                act.wait_ge(raw_ready[s], raw_count_at(n, phase))
                wait(act, bank_ready[3 * s + 2], n)
                act.activation(whi[s][:, 0:cols], raw[s][:, 0:cols], ACT.Copy).then_inc(hi_ready[s], 1)

            act.wait_ge(const_ready, 4)

            def apart():
                act.wait_ge(const_ready, 4)

            def square(v, k, c):
                act.wait_ge(sq_added, sq_base(v) + 3 * k + c - 2)
                act.activation(t1[:, chunk(c)], x[:, k, chunk(c)], ACT.Square).then_inc(sq_done, 1)

            def root(v, c):
                act.wait_ge(stat_ready, 3 * v + c + 1)
                act.activation(rstd[:, chunk(c)], bank(6 + c % 2, c), ACT.Sqrt, bias=epst[:, 0:1])\
                   .then_inc(stat_sqrt, 1)

            def norm_hi(u, v, chunks=range(3)):
                for c in chunks:
                    w = CHUNKS[c][1]
                    for k in range(KD):
                        act.wait_ge(xn_mult, 24 * u + 8 * c + k + 1)
                        act.activation(nhi[:, k, chunk(c)], y[:, ds((k % 2) * 384, w)], ACT.Copy).then_inc(xn_hi, 1)
                        if k == 3 and c < 2 and v is not None and (v, c) != (0, 0):
                            root(v, c + 1)

            def squares_in(c):
                act.wait_ge(tr_act, SET_END[c] // 2)
                act.wait_ge(tr_dve, SET_END[c] // 2)
                for k in range(4):
                    i = 4 * c + k
                    wait(act, sq_added, i - 1 if i >= 2 else 0)
                    act.activation(t1[:, ds((i % 2) * 384, CHUNKS[c][1])], x[:, k, chunk(c)], ACT.Square)\
                       .then_inc(sq_done, 1)

            set_up(0, SET_END[0])
            squares_in(0)
            set_up(SET_END[0], SET_END[1])
            root(0, 0)
            squares_in(1)
            prep(0, 0, KD * P)
            prep(0, 1, KD * P)
            norm_hi(0, 0, [0])
            root(0, 1)
            set_up(SET_END[1], SET_END[2])
            squares_in(2)
            norm_hi(0, 0, [1, 2])
            act.wait_ge(sp_ready, 1)
            act.activation(spt[:, 1, :], spt[:, 0, :], ACT.Exp, scale=-1.0).then_inc(sp_exp, 1)

            def evac_conv(s, n, hist, convs, stashes):
                gp, gs = sp_view(convin, hist)
                wait(act, conv_done, convs)
                wait(act, stash_done, stashes)
                for c in range(3):
                    act.wait_ge(bank_ready[3 * s + c], n + 1)
                    lo, w = CHUNKS[c]
                    b = 3 * s + c
                    if c == 2:
                        act.activation(gs[:, :, hist:], requests(ps[:, b, SEQ - lo:w]), ACT.Copy)
                        w = SEQ - lo
                    act.activation(gp[:, hist + lo:hist + lo + w], ps[:, b, 0:w], ACT.Copy).then_inc(bank_free[b], 1)

            def lru_block(c, last):
                for s in range(2):
                    n, kt = 4 * c, 2 * c + s
                    evac_conv(s, n, 3, 2 * kt, kt)
                    prep(n + 1, s, KD * P)
                    act.wait_ge(conv_done, 2 * kt + 2)
                    act.activation(xchi[:, s, :], y[:, :], ACT.Copy).then_inc(xc_hi, 1)
                wait(act, scan_done, 2 * c)
                for s in range(2):
                    n = 4 * c + 1
                    for ch in range(3):
                        b = 3 * s + ch
                        act.wait_ge(bank_ready[b], n + 1)
                        apart()
                        act.activation(z[:, ds(2 * c + s, 1), chunk(ch)], bank(b, ch).rearrange("p (o t) -> p o t", o=1),
                                       ACT.Gelu_apprx_tanh).then_inc(bank_free[b], 1)
                        if ch == 1:
                            prep(n + 1, s, 2 * P)
                if last:
                    act.wait_ge(bank_ready[5], 4 * c + 2)
                    for k in range(KD - 2):
                        act.wait_ge(z_ready, k + 1)
                        act.activation(nhi[:, k, :], z[:, k, :], ACT.Copy).then_inc(z_hi, 1)
                wait(act, scan_done, 2 * c)
                for m in range(2):
                    n, kt = 4 * c + 2 + m, 2 * c + m
                    for s, t, col in zip(range(2), gate_tiles(c, m), (C_RB, C_IB)):
                        for ch in range(3):
                            b = 3 * s + ch
                            apart()
                            act.wait_ge(bank_ready[b], n + 1)
                            act.activation(t[:, chunk(ch)], bank(b, ch), ACT.Sigmoid,
                                           bias=pcol[:, ds(kt, 1), col]).then_inc(bank_free[b], 1)
                            if ch == 1:
                                prep(n + 1, s, 2 * P if m == 0 else KD * P)
                for m in range(2):
                    n, kt = 4 * c + 2 + m, 2 * c + m
                    t = gate_tiles(c, m)[0]
                    act.wait_ge(bank_free[2], n + 1)
                    apart()
                    act.activation(rstd[:, :], t, ACT.Tanh, scale=sp[:, 0, ds(kt, 1)]).then_inc(tanh_done, 1)
                    apart()
                    act.wait_ge(tanh_done, kt + 1)
                    act.activation(t, t, ACT.Exp, scale=sp[:, 1, ds(kt, 1)]).then_inc(a_ready, 1)
                    act.wait_ge(one_a2, kt + 1)
                    act.activation(y[:, :], y[:, :], ACT.Sqrt).then_inc(root_ready, 1)

            lru_block(0, False)
            with act.Fori(1, LRU_BLOCKS - 1) as c:
                lru_block(c, False)
            lru_block(LRU_BLOCKS - 1, True)
            for k in range(KD - 2, KD):
                act.wait_ge(z_ready, k + 1)
                act.activation(nhi[:, k, :], z[:, k, :], ACT.Copy).then_inc(z_hi, 1)

            def residual(n, i, v, last_cols, phase, last=False):
                for s in range(2):
                    for c in range(3):
                        if last and s == 1 and c == 2:
                            root(v, 0)
                        act.wait_ge(bank_free[3 * s + c], n + 1)
                        act.wait_ge(sq_added, sq_base(v) + 6 * i + 3 * s + c - 2)
                        apart()
                        act.activation(t1[:, chunk(c)].rearrange("p (o t) -> p o t", o=1),
                                       x[:, ds(2 * i + s, 1), chunk(c)], ACT.Square).then_inc(sq_done, 1)
                    prep(n + 1, s, last_cols, phase)

            with act.Fori(0, KD // 2 - 1) as i:
                residual(N_OUT + i, i, 1, KD * P, "")
            residual(N_F0 - 1, KD // 2 - 1, 1, KD * P, "", last=True)
            norm_hi(1, 1)

            def ffn(layer, n0, v, phase):
                def block_(b, last):
                    nb = n0 + b * (FB + KD // 2)

                    def tile(j, next_cols):
                        n = nb + j
                        f = layer * FT + b * FB + j
                        evac_conv(0, n, 2, 2 * (KD + f), KD + f)
                        prep(n + 1, 0, next_cols, phase)
                        act.wait_ge(conv_done, 2 * (KD + f) + 2)
                        act.activation(y[:, :], y[:, :], ACT.Gelu_apprx_tanh).then_inc(gelu_done, 1)
                        for c in range(3):
                            act.wait_ge(bank_free[3 + c], n + 1)
                            apart()
                            act.activation(hhi[:, ds(j, 1), chunk(c)], y[:, chunk(c)].rearrange("p (o t) -> p o t", o=1),
                                           ACT.Copy).then_inc(hhi_done, 1)
                        prep(n + 1, 1, next_cols, phase)

                    with act.Fori(0, FB - 1) as j:
                        tile(j, KD * P)
                    tile(FB - 1, FB * P)
                    nd = nb + FB
                    if last and layer == 0:
                        with act.Fori(0, KD // 2 - 1) as i:
                            residual(nd + i, i, v, FB * P, phase)
                        residual(nd + KD // 2 - 1, KD // 2 - 1, v, KD * P, "", last=True)
                    else:
                        with act.Fori(0, KD // 2 - 1) as i:
                            for s in range(2):
                                prep(nd + i + 1, s, FB * P, phase)
                        if not last:
                            for s in range(2):
                                prep(nd + KD // 2, s, KD * P, phase)

                with act.Fori(0, NFB - 1) as b:
                    block_(b, False)
                block_(NFB - 1, True)

            def states(layer):
                for m, (_, view, dst) in enumerate(state_jobs(layer)):
                    act.wait_ge(fst_tr, STATE0[layer] + m + 1)
                    act.activation(dst, view, ACT.Copy).then_inc(fst_cp, 1)
                act.wait_ge(fst_cp, STATE0[layer + 1])
                act.dma_start(A["ffn_conv_p"][layer, 0], fout[0:2, :]).then_inc(states_out, 16)
                act.dma_start(A["ffn_conv_s"][layer].rearrange("b w d -> (b w) d"), fout[2:18, :])\
                   .then_inc(states_out, 16)
                if layer == 0:
                    for dst, lo, hi in ((A["lru_conv_p"][0, 0], 32, 35),
                                        (A["lru_conv_s"][0].rearrange("b w d -> (b w) d"), 0, 24),
                                        (A["lru_h_p"][0], 35, 36), (A["lru_h_s"][0], 24, 32)):
                        act.dma_start(dst, lout[lo:hi, :]).then_inc(states_out, 16)

            ffn(0, N_F0, 2, "")

            norm_hi(2, 2)

            def head_roots(i):
                for c in range(3):
                    act.wait_ge(hmean, 3 * i + c + 1)
                    if c == 0:
                        act.wait_ge(hnorm, i)
                    act.activation(convin[:, chunk(c)], bank(6 + (3 * i + c) % 2, c), ACT.Sqrt, bias=epst[:, 0:1])\
                       .then_inc(hroot, 1)

            for m in range(2):
                for s in range(2):
                    n = N_KV + m
                    for c in range(3):
                        b = 3 * s + c
                        dst = kf[:, s, chunk(c)] if m == 0 else (t1, t2)[s][:, chunk(c)]
                        act.wait_ge(bank_ready[b], n + 1)
                        act.activation(dst, bank(b, c), ACT.Identity, bias=pcol[:, 2 * m + s, C_BKV:C_BKV + 1])\
                           .then_inc(bank_free[b], 1)
                    prep(n + 1, s, KD * P, "q" if m == 1 else "")
            states(0)
            for s in range(2):
                act.wait_ge(bank_free[3 * s + 2], N_KV + 1)
                if s == 1:
                    act.wait_ge(hmean, 3)
                act.activation(y[:, :], kf[:, s, :], ACT.Square).then_inc(hsq, 1)
                head_roots(s)
            act.wait_ge(strip_mm, 1)
            act.activation(strip_sb2[:, :], ps[0:HEADS, 6, 0:FV], ACT.Copy).then_inc(strip_cp, 1)
            act.wait_ge(strip_cp, 1)
            src = strip_sb2[:, :].rearrange("h (o v) -> h o v", o=1).broadcast_to([HEADS, P, FV])
            act.dma_start(strip_dram.rearrange("(h r v) -> h r v", h=HEADS, r=P), src).then_inc(strip_out, 16)
            norm_hi(3, None)
            act.wait_ge(states_out, 16 * 6)
            for t in range(KD):
                n, s = N_Q + t // 2, t % 2
                for c in range(3):
                    b = 3 * s + c
                    act.wait_ge(bank_ready[b], n + 1)
                    act.activation(qz[:, t, chunk(c)], bank(b, c), ACT.Identity, bias=pcol[:, t, C_BQ:C_BQ + 1])\
                       .then_inc(bank_free[b], 1)
                prep(n + 1, s, KD * P, "q" if t < KD - 2 else "o")
                act.wait_ge(bank_free[3 * s + 2], n + 1)
                act.wait_ge(hmean, 3 * (2 + t))
                act.activation(y[:, :], qz[:, t, :], ACT.Square).then_inc(hsq, 1)
                head_roots(2 + t)

            act.wait_ge(bank_ready[5], N_O)
            act.wait_ge(strip_out, 16)
            act.dma_start(ck[:, :, :], A["cache_k_win"].rearrange("r w h d -> w r (h d)")).then_inc(att_in, 16)
            act.dma_start(cv[:, :, :], A["cache_v_win"].rearrange("r w h d -> w r (h d)")).then_inc(att_in, 16)
            src = bass.AP(strip_dram.tensor, WIN - 1, [[FV - 1, P], [P * FV, HEADS], [1, 2 * WIN]])
            act.dma_start(bias[:, :, :], src).then_inc(att_in, 16)
            for r in range(4):
                for j in range(4):
                    src = bass.AP(strip_dram.tensor, WIN - 1 + j * P * FV,
                                  [[FV - 1, DEC_T], [4 * P * FV, KV_HEADS], [1, LS]])
                    p0 = 32 * r + DEC_T * j
                    act.dma_start(sbias[p0:p0 + DEC_T, :, :], src).then_inc(att_in, 16)
            with nc.allow_non_contiguous_dma(reason="a few single elements"):
                act.dma_start(sinkb[:, :], bass.AP(A["sinks"].tensor, 0, [[0, P], [1, HEADS]])).then_inc(att_in, 16)
                for r in range(4):
                    for j in range(4):
                        p0 = 32 * r + DEC_T * j
                        src = bass.AP(A["sinks"].tensor, j, [[0, DEC_T], [4, KV_HEADS], [1, 1]])
                        act.dma_start(sinks_s[p0:p0 + DEC_T, :].rearrange("p (g o) -> p g o", o=1), src).then_inc(att_in, 16)

            jobs = prep_jobs()
            for m, (_, view, dst) in enumerate(jobs):
                act.wait_ge(prep_tr, m + 1)
                if dst is None:
                    act.activation(kvrow[0:NS, 1, :], ps[0:NS, 5, 0:256], ACT.Copy)
                    act.activation(pt[0:NS, 0, 0:256], ps[0:NS, 5, 256:512], ACT.Copy).then_inc(prep_cp, 1)
                else:
                    act.activation(dst, view, ACT.Copy).then_inc(prep_cp, 1)
                if m == 5:
                    act.wait_ge(prep_cp, 6)
                    for r in range(DEC_B):
                        act.dma_start(vnew[:, r, :], pt[r * DEC_T:(r + 1) * DEC_T, 0, 0:256]).then_inc(vnew_in, 16)
                    for name, cache, rows in (("k", A["cache_k_win"], kvrow[0:NS, 1, :]),
                                              ("v", A["cache_v_win"], pt[0:NS, 0, 0:256])):
                        out = A[f"{name}_win_s"].rearrange("r w h d -> r w (h d)")
                        act.dma_start(out[:, 0:WIN - DEC_T, :], cache.rearrange("r w h d -> r w (h d)")[:, DEC_T:, :])\
                           .then_inc(win_out, 16)
                        for r in range(DEC_B):
                            act.dma_start(out[r, WIN - DEC_T:, :], rows[r * DEC_T:(r + 1) * DEC_T, :])\
                               .then_inc(win_out, 16)
                    act.dma_start(A["k_win_p"][0].rearrange("w h d -> w (h d)"), kvrow[:, 0, :]).then_inc(win_out, 16)
                    act.dma_start(A["v_win_p"][0].rearrange("w h d -> w (h d)"), vt[:, NB - 1, :])\
                       .then_inc(win_out, 16)

            def exps(i):
                a, e, b = steps[i]
                st = stat[:, :, 4 * (i % NPB):4 * (i % NPB) + 4]
                act.wait_ge(max_ready, i + 1)
                if b < NB:
                    k0 = 0 if b > 0 else WIN
                    for j in range(4):
                        w = pb[i % NPB][:, j, k0:]
                        act.activation(w, w, ACT.Exp, bias=st[:, 1, j:j + 1], accum_out=st[:, 2, j:j + 1])
                else:
                    flat = pb[i % NPB][:, :, :].rearrange("p a b -> p (a b)")
                    for h in range(2):
                        w = flat[:, h * LS:(h + 1) * LS]
                        act.activation(w, w, ACT.Exp, bias=st[:, 1, h:h + 1], accum_out=st[:, 2, h:h + 1])
                m = 4 if b < NB else 2
                act.activation(st[:, 3, 0:m], st[:, 4, 0:m], ACT.Exp).then_inc(exp_done, 1)

            act.wait_ge(vnew_in, 16 * DEC_B)
            act.wait_ge(win_out, 16 * (4 + 2 * DEC_B))
            exps(0)
            for i in range(NSTEP):
                a, e, b = steps[i]
                if i + 1 < NSTEP:
                    exps(i + 1)
                act.wait_ge(pt_ready, i + 1)
                if i >= 1:
                    act.wait_ge(o_ready, i)
                if b < NB:
                    if b > 0:
                        act.activation(pt[:, 0, :], ps[:, 4, :], ACT.Copy)
                    act.activation(pt[:, 1, :], ps[:, 5, :], ACT.Copy).then_inc(pt_copied, 1)
                else:
                    act.activation(pt[:, 0, 0:256], ps[:, 4, 0:256], ACT.Copy)
                    act.activation(pt[0:DEC_T, 1, 0:256], ps[0:DEC_T, 5, 0:256], ACT.Copy).then_inc(pt_copied, 1)
            for k in range(KD):
                act.wait_ge(o_copied, NSTEP)
                act.activation(nhi[:, k, :], qz[:, k, :], ACT.Copy).then_inc(z_hi, 1)
            with act.Fori(0, KD // 2 - 1) as i:
                residual(N_O + i, i, 3, KD * P, "o")
            residual(N_O + KD // 2 - 1, KD // 2 - 1, 3, KD * P, "f1", last=True)
            norm_hi(4, 3)
            ffn(1, N_F1, 4, "f1")
            states(1)

            for m in range(len(ends)):
                if m % 2 == 0:
                    act.wait_ge(tr_ready, NSET + m + 1)
                    view, dst = end_out(m)
                    act.activation(dst, view, ACT.Copy).then_inc(tr_act, 1)
            act.wait_ge(states_out, 16 * 8)

        @block.vector
        def _(dve):
            seq = Tally(dve, dve_seq)

            dve.memset(ones[:, :], 1.0 / D).then_inc(const_ready, 1)
            dve.memset(epst[:, :], EPS).then_inc(const_ready, 1)
            seq.mark(dve.memset(blockones[:, :], 0.0))
            seq.settle()
            dve.memset(blockones[0:HD, 0:HD], 1.0 / HD)
            dve.memset(blockones[HD:P, HD:P], 1.0 / HD).then_inc(const_ready, 1)
            def set_up(first, end):
                for m in range(first + 1, end, 2):
                    dve.wait_ge(tr_ready, m + 1)
                    view, dst = job_out(setup[m], SET_BANK[m])
                    dve.tensor_copy(dst, view).then_inc(tr_dve, 1)

            def prep(n, s, cols):
                dve.wait_ge(hi_ready[s], n + 1)
                dve.tensor_tensor(wlo[s][:, 0:cols], raw[s][:, 0:cols], whi[s][:, 0:cols].bitcast(F32), ALU.subtract)\
                   .then_inc(lo_ready[s], 1)

            def recip(v, c):
                dve.wait_ge(stat_sqrt, 3 * v + c + 1)
                seq.mark(dve.reciprocal(rstd[:, chunk(c)], rstd[:, chunk(c)]))

            def norm(u, gain, v, chunks=range(3)):
                order = [(c, k) for c in chunks for k in range(KD)]
                for j in range(len(order) + 1):
                    i = 8 * order[0][0] + j
                    if j < len(order):
                        c, k = order[j]
                        if k == 0 and v is not None:
                            seq.settle()
                        if i >= 2:
                            dve.wait_ge(xn_lo, 24 * u + i - 1)
                        dve.scalar_tensor_tensor(y[:, ds((k % 2) * 384, CHUNKS[c][1])], x[:, k, chunk(c)],
                                                 pcol[:, k, gain:gain + 1], rstd[:, chunk(c)], ALU.mult, ALU.mult)\
                           .then_inc(xn_mult, 1)
                    if j >= 1:
                        c, k = order[j - 1]
                        dve.wait_ge(xn_mult, 24 * u + i)
                        dve.wait_ge(xn_hi, 24 * u + i)
                        dve.tensor_tensor(nlo[:, k, chunk(c)], y[:, ds((k % 2) * 384, CHUNKS[c][1])],
                                          nhi[:, k, chunk(c)].bitcast(F32), ALU.subtract).then_inc(xn_lo, 1)
                        if k == 5 and c < 2 and v is not None and (v, c) != (0, 0):
                            recip(v, c + 1)

            def squares_in(c):
                dve.wait_ge(tr_act, SET_END[c] // 2)
                dve.wait_ge(tr_dve, SET_END[c] // 2)
                wait(dve, stat_ready, c)
                w = CHUNKS[c][1]
                part, total = convin[:, 0:w], convin[:, 384:384 + w]
                for k in range(4, KD):
                    seq.mark(dve.tensor_tensor(part if k > 4 else total, x[:, k, chunk(c)], x[:, k, chunk(c)], ALU.mult))
                    seq.settle()
                    if k > 4:
                        ins = dve.tensor_tensor(total, total, part, ALU.add)
                        if k < KD - 1:
                            seq.mark(ins)
                            seq.settle()
                        else:
                            ins.then_inc(sq_dve, 1)

            set_up(0, SET_END[0])
            squares_in(0)
            set_up(SET_END[0], SET_END[1])
            recip(0, 0)
            squares_in(1)
            prep(0, 0, KD * P)
            prep(0, 1, KD * P)
            norm(0, C_ANORM, 0, [0])
            recip(0, 1)
            set_up(SET_END[1], SET_END[2])
            squares_in(2)
            norm(0, C_ANORM, 0, [1, 2])
            dve.wait_ge(sq_dve, 3)
            seq.mark(dve.memset(convin[:, 0:CONV_W - 1], 0.0))

            lam = pcol[:, :, C_LAM]
            seq.mark(dve.tensor_scalar(spt[:, 2, :], lam, -1.0, 0.0, ALU.mult, ALU.max))
            seq.mark(dve.tensor_scalar(spt[:, 3, :], lam, 0.0, None, ALU.max))
            seq.settle()
            dve.tensor_tensor(spt[:, 0, :], spt[:, 2, :], spt[:, 3, :], ALU.add).then_inc(sp_ready, 1)
            dve.wait_ge(sp_exp, 1)
            seq.mark(dve.tensor_scalar(spt[:, 0, :], spt[:, 1, :], 2.0, None, ALU.add))
            seq.settle()
            seq.mark(dve.reciprocal(spt[:, 0, :], spt[:, 0, :]))
            seq.settle()
            seq.mark(dve.tensor_tensor(spt[:, 0, :], spt[:, 0, :], spt[:, 1, :], ALU.mult))
            seq.settle()
            seq.mark(dve.tensor_tensor(spt[:, 1, :], spt[:, 0, :], spt[:, 0, :], ALU.mult))
            seq.settle()
            terms = 9
            seq.mark(dve.tensor_scalar(spt[:, 3, :], spt[:, 1, :], 1.0 / (2 * terms + 1), 1.0 / (2 * terms - 1),
                                       ALU.mult, ALU.add))
            seq.settle()
            for i in range(terms - 2, -1, -1):
                seq.mark(dve.tensor_tensor(spt[:, 3, :], spt[:, 3, :], spt[:, 1, :], ALU.mult))
                seq.settle()
                seq.mark(dve.tensor_scalar(spt[:, 3, :], spt[:, 3, :], 1.0 / (2 * i + 1), None, ALU.add))
                seq.settle()
            seq.mark(dve.tensor_tensor(spt[:, 3, :], spt[:, 3, :], spt[:, 0, :], ALU.mult))
            seq.settle()
            seq.mark(dve.scalar_tensor_tensor(spt[:, 3, :], spt[:, 3, :], 2.0, spt[:, 2, :], ALU.mult, ALU.add))
            seq.settle()
            seq.mark(dve.tensor_scalar(sp[:, 0, :], spt[:, 3, :], C_GATE, None, ALU.mult))
            seq.mark(dve.tensor_scalar(sp[:, 1, :], spt[:, 3, :], -C_GATE, None, ALU.mult))
            seq.settle()


            def conv(taps, hist, w, b, hists, free_banks, n, before):
                gp, gs = sp_view(convin, hist)
                before()
                for bk in free_banks:
                    dve.wait_ge(bank_free[bk], n + 1)
                dve.wait_ge(hist_ready, hists)
                yp, ys = y[:, 0:SEQ], requests(y[:, SEQ:T])
                for i in range(taps):
                    t = taps - 1 - i
                    for o, g, m in ((yp, gp[:, t:t + SEQ], "p"), (ys, gs[:, :, t:t + DEC_T], "s")):
                        if i == 0:
                            ins = dve.tensor_scalar(o, g, w(t), b, ALU.mult, ALU.add)
                        else:
                            ins = dve.scalar_tensor_tensor(o, g, w(t), o, ALU.mult, ALU.add)
                        if i < taps - 1:
                            seq.mark(ins)
                        else:
                            ins.then_inc(conv_done, 1)
                    if i < taps - 1:
                        seq.settle()

            def lru_block(c, last, start):
                seq.at = start
                for s in range(2):
                    n, kt = 4 * c, 2 * c + s
                    wait(dve, hlast_done, 2 * c)
                    wait(dve, xc_lo, kt)
                    wait(dve, z_ready, 2 * c)
                    conv(CONV_W, 3, lambda t: pcol[:, ds(kt, 1), C_CONVW + t], pcol[:, ds(kt, 1), C_CONVB], kt + 1,
                         (3 * s, 3 * s + 1, 3 * s + 2), n, lambda: prep(n + 1, s, KD * P))
                    dve.wait_ge(xc_hi, kt + 1)
                    dve.tensor_tensor(xclo[:, s, :], y[:, :], xchi[:, s, :].bitcast(F32), ALU.subtract)\
                       .then_inc(xc_lo, 1)
                for s in range(2):
                    prep(4 * c + 2, s, 2 * P)
                if last:
                    for k in range(KD - 2):
                        dve.wait_ge(z_hi, k + 1)
                        dve.tensor_tensor(nlo[:, k, :], z[:, k, :], nhi[:, k, :].bitcast(F32), ALU.subtract)\
                           .then_inc(z_lo, 1)
                for m in range(2):
                    for s in range(2):
                        prep(4 * c + 3 + m, s, 2 * P if m == 0 else KD * P)
                for m in range(2):
                    n, kt = 4 * c + 2 + m, 2 * c + m
                    ta, tb = gate_tiles(c, m)
                    dve.wait_ge(xc_lo, 2 * c + 2)
                    wait(dve, hlast_done, kt)
                    wait(dve, z_ready, kt)
                    seq.mark(dve.tensor_tensor(y[:, :], xchi[:, m, :].bitcast(F32), xclo[:, m, :].bitcast(F32), ALU.add))
                    seq.settle()
                    dve.wait_ge(bank_free[5], n + 1)
                    seq.mark(dve.tensor_tensor(tb, tb, y[:, :], ALU.mult))
                    seq.settle()
                    dve.wait_ge(a_ready, kt + 1)
                    seq.mark(dve.tensor_tensor(y[:, :], ta, ta, ALU.mult))
                    seq.settle()
                    dve.scalar_tensor_tensor(y[:, :], y[:, :], 1.0, rstd[:, :], ALU.add, ALU.mult).then_inc(one_a2, 1)
                    first1, first2 = (requests(t[:, SEQ:T])[:, :, 0] for t in (ta, tb))
                    h0 = pcol[:, ds(kt, 1), C_SH:C_SH + DEC_B].rearrange("p o b -> p (o b)")
                    seq.mark(dve.tensor_tensor(h0a[:, :], first1, h0, ALU.mult))
                    seq.settle()
                    seq.mark(dve.tensor_scalar(first1, first1, 0.0, None, ALU.mult))
                    dve.wait_ge(root_ready, kt + 1)
                    seq.mark(dve.tensor_tensor(tb, tb, y[:, :], ALU.mult))
                    seq.settle()
                    seq.mark(dve.tensor_tensor(first2, first2, h0a[:, :], ALU.add))
                    seq.settle()
                    dve.tensor_tensor_scan(y[:, :], ta, tb, 0.0, ALU.mult, ALU.add).then_inc(scan_done, 1)
                    dve.wait_ge(scan_done, kt + 1)
                    zt = z[:, ds(kt, 1), :].rearrange("p o t -> p (o t)")
                    dve.tensor_tensor(zt, zt, y[:, :], ALU.mult).then_inc(z_ready, 1)

            start = seq.at
            per = 2 * 2 * (CONV_W - 1) + 2 * 7
            lru_block(0, False, start)
            with dve.Fori(1, LRU_BLOCKS - 1) as c:
                lru_block(c, False, start + c * per)
            lru_block(LRU_BLOCKS - 1, True, start + (LRU_BLOCKS - 1) * per)
            assert seq.at == start + LRU_BLOCKS * per, (seq.at, start, per)
            for k in range(KD - 2, KD):
                dve.wait_ge(z_ready, k + 1)
                dve.wait_ge(z_hi, k + 1)
                dve.tensor_tensor(nlo[:, k, :], z[:, k, :], nhi[:, k, :].bitcast(F32), ALU.subtract).then_inc(z_lo, 1)

            def residual(n, i, next_cols, bias_col=None, last=False, v=None):
                for s in range(2):
                    for c in range(3):
                        if v is not None and s == 1 and c == 2:
                            recip(v, 0)
                        b = 3 * s + c
                        dve.wait_ge(bank_ready[b], n + 1)
                        xt = x[:, ds(2 * i + s, 1), chunk(c)].rearrange("p o t -> p (o t)")
                        if bias_col is None:
                            ins = dve.tensor_tensor(xt, bank(b, c), xt, ALU.add)
                        else:
                            ins = dve.scalar_tensor_tensor(xt, bank(b, c), pcol[:, ds(2 * i + s, 1), bias_col], xt,
                                                           ALU.add, ALU.add)
                        ins.then_inc(bank_free[b], 1)
                    if not last:
                        prep(n + 1, s, next_cols)

            with dve.Fori(0, KD // 2 - 1) as i:
                residual(N_OUT + i, i, KD * P)
            residual(N_F0 - 1, KD // 2 - 1, KD * P, v=1)
            norm(1, C_FN, 1)

            FT_MARKS = 2 * (FFN_W - 1)

            def ffn(layer, n0):
                start = seq.at

                def block_(b):
                    nb = n0 + b * (FB + KD // 2)

                    def tile(j, next_cols):
                        n = nb + j
                        f = b * FB + j
                        g = layer * FT + f
                        seq.at = start + f * FT_MARKS
                        col = 20 * layer
                        conv(FFN_W, 2, lambda t: fcol[:, ds(f, 1), col + F_W + t], fcol[:, ds(f, 1), col + F_B],
                             KD + g + 1, (0, 1, 2), n, lambda: prep(n + 1, 0, next_cols))
                        dve.wait_ge(gelu_done, g + 1)
                        for c in range(3):
                            dve.wait_ge(bank_ready[3 + c], n + 1)
                            dve.tensor_tensor(y[:, chunk(c)], bank(3 + c, c), y[:, chunk(c)], ALU.mult)\
                               .then_inc(bank_free[3 + c], 1)
                        for c in range(3):
                            dve.wait_ge(bank_free[3 + c], n + 1)
                            dve.wait_ge(hhi_done, 3 * g + c + 1)
                            ht = hhi[:, ds(j, 1), chunk(c)].rearrange("p o t -> p (o t)").bitcast(F32)
                            lt = hlo[:, ds(j, 1), chunk(c)].rearrange("p o t -> p (o t)")
                            dve.tensor_tensor(lt, y[:, chunk(c)], ht, ALU.subtract).then_inc(hlo_done, 1)
                        prep(n + 1, 1, next_cols)
                        dve.wait_ge(const_ready, 4)
                        dve.wait_ge(hlo_done, 3 * g + 3)

                    with dve.Fori(0, FB - 1) as j:
                        tile(j, KD * P)
                    tile(FB - 1, FB * P)
                    nd = nb + FB
                    with dve.Fori(0, KD // 2 - 1) as i:
                        residual(nd + i, i, FB * P)
                    return nd + KD // 2 - 1

                with dve.Fori(0, NFB - 1) as b:
                    residual(block_(b), KD // 2 - 1, KD * P)
                nd = block_(NFB - 1)
                seq.at = start + FT * FT_MARKS
                residual(nd, KD // 2 - 1, KD * P, last=(layer == 1), v=2 if layer == 0 else None)

            ffn(0, N_F0)
            dve.memset(strip_in_sb[BUCKETS:BUCKETS + 1, FV:FV + HEADS], 1.0).then_inc(strip_one, 1)
            norm(2, C_KVN, 2)

            def head_norm(i, tile_, gain):
                for c in range(3):
                    dve.wait_ge(hroot, 3 * i + c + 1)
                    seq.mark(dve.reciprocal(convin[:, chunk(c)], convin[:, chunk(c)]))
                seq.settle()
                dve.scalar_tensor_tensor(tile_, tile_, qkn[:, gain:gain + 1], convin[:, 0:T], ALU.mult, ALU.mult)\
                   .then_inc(hnorm, 1)

            for m in range(2):
                for s in range(2):
                    prep(N_KV + m + 1, s, KD * P)
            for s in range(2):
                head_norm(s, kf[:, s, :], 1)
            dve.wait_ge(bank_ready[5], N_Q)
            dve.wait_ge(hmean, 6)
            norm(3, C_BN, None)
            for t in range(KD):
                prep(N_Q + t // 2 + 1, t % 2, KD * P)
                head_norm(2 + t, qz[:, t, :], 0)

            def before_exp(i):
                a, e, b = steps[i]
                g = 2 * a + e
                st = stat[:, :, 4 * (i % NPB):4 * (i % NPB) + 4]
                dve.wait_ge(sc_ready, i + 1)
                if i >= NPB:
                    dve.wait_ge(pt_ready, i - NPB + 1)
                if b < NB:
                    m, k0 = 4, (0 if b > 0 else WIN)
                    sc = ps[:, 2 * (i % 2):2 * (i % 2) + 2, :].rearrange("p a (j s) -> p (a j) s", j=2)[:, :, k0:]
                    w = pb[i % NPB][:, :, k0:]
                    bs = bias[:, 4 * g:4 * g + 4, k0:]
                    sk = sinkb[:, 4 * g:4 * g + 4]
                    dve.scalar_tensor_tensor(w, sc, SCALE, bs, ALU.mult, ALU.add).then_inc(sc_read, 1)
                else:
                    m = 2
                    w = pb[i % NPB][:, :, :].rearrange("p a b -> p (a b)")[:, 0:2 * LS].rearrange("p (h s) -> p h s", h=2)
                    for h in range(2):
                        ins = dve.scalar_tensor_tensor(w[:, h, :], ps[:, 2 * (i % 2), h * LS:(h + 1) * LS], SCALE,
                                                       sbias[:, g, :], ALU.mult, ALU.add)
                    ins.then_inc(sc_read, 1)
                dve.wait_ge(sc_read, i + 1)
                seq.mark(dve.tensor_reduce(st[:, 0, 0:m], w, AX_X, ALU.max))
                seq.settle()
                if b < NB:
                    seq.mark(dve.tensor_tensor(st[:, 0, 0:m], st[:, 0, 0:m], sk, ALU.max))
                    seq.settle()
                    seq.mark(dve.tensor_tensor(st[:, 4, 0:m], sk, st[:, 0, 0:m], ALU.subtract))
                else:
                    seq.mark(dve.tensor_scalar(st[:, 0, 0:m], st[:, 0, 0:m], sinks_s[:, g:g + 1], None, ALU.max))
                    seq.settle()
                    seq.mark(dve.tensor_scalar(st[:, 4, 0:m], st[:, 0, 0:m], -1.0, sinks_s[:, g:g + 1], ALU.mult,
                                               ALU.add))
                dve.tensor_scalar(st[:, 1, 0:m], st[:, 0, 0:m], -1.0, None, ALU.mult).then_inc(max_ready, 1)

            def after_exp(i):
                a, e, b = steps[i]
                st = stat[:, :, 4 * (i % NPB):4 * (i % NPB) + 4]
                m = 4 if b < NB else 2
                dve.wait_ge(exp_done, i + 1)
                seq.mark(dve.tensor_tensor(st[:, 5, 0:m], st[:, 2, 0:m], st[:, 3, 0:m], ALU.add))
                seq.settle()
                dve.reciprocal(st[:, 6, 0:m], st[:, 5, 0:m]).then_inc(inv_ready, 1)

            def take_out(i):
                a, e, b = steps[i]
                h0 = HD * e
                dve.wait_ge(o_ready, i + 1)
                src = ps[h0:h0 + HD, 6 + i % 2, :]
                if b < NB:
                    dst = qz[h0:h0 + HD, 4 * a:4 * a + 4, b * WIN:(b + 1) * WIN]
                    dve.tensor_copy(dst, src.rearrange("p (j q) -> p j q", j=4)).then_inc(o_copied, 1)
                else:
                    dst = qz[h0:h0 + HD, 4 * a:4 * a + 4, SEQ:T].rearrange("p j (r t) -> p j r t", r=DEC_B)
                    dve.tensor_copy(dst, src[:, 0:32 * DEC_B].rearrange("p (r j t) -> p j r t", r=DEC_B, j=4))\
                       .then_inc(o_copied, 1)

            dve.wait_ge(hnorm, 2 + KD)
            for a in range(2):
                src = qz[:, 4 * a:4 * a + 4, SEQ:T].rearrange("p j (r t) -> p r j t", r=DEC_B)
                dst = convin[:, 256 * a:256 * a + 256].rearrange("p (r j t) -> p r j t", r=DEC_B, j=4)
                dve.tensor_copy(dst, src).then_inc(qs_ready, 1)
            dve.wait_ge(att_in, 16 * N_ATT_IN)

            before_exp(0)
            for i in range(NSTEP):
                if i + 1 < NSTEP:
                    before_exp(i + 1)
                after_exp(i)
                if i >= 1:
                    take_out(i - 1)
            take_out(NSTEP - 1)
            for k in range(KD):
                dve.wait_ge(z_hi, KD + k + 1)
                dve.tensor_tensor(nlo[:, k, :], qz[:, k, :], nhi[:, k, :].bitcast(F32), ALU.subtract).then_inc(z_lo, 1)
            with dve.Fori(0, KD // 2 - 1) as i:
                residual(N_O + i, i, KD * P, bias_col=C_BO)
            residual(N_F1 - 1, KD // 2 - 1, KD * P, bias_col=C_BO, v=3)
            norm(4, C_FN + 1, 3)
            ffn(1, N_F1)
            for m in range(len(ends)):
                if m % 2 == 1:
                    dve.wait_ge(tr_ready, NSET + m + 1)
                    view, dst = end_out(m)
                    dve.tensor_copy(dst, view).then_inc(tr_dve, 1)

        @block.gpsimd
        def _(pool):
            seq = Tally(pool, pool_seq)
            seq.mark(pool.memset(ident[:, :], 0.0))
            seq.settle()
            pool.affine_select(out=ident[:, :], in_=ident[:, :], compare_op=ALU.not_equal, fill=1.0, base=0,
                               pattern=[[-1, P]], channel_multiplier=1).then_inc(const_ready, 1)

            def sum_squares(v):
                for c in range(3):
                    seq.mark(pool.memset(t2[:, chunk(c)], 0.0))
                seq.settle()
                with pool.Fori(0, KD) as k:
                    for c in range(3):
                        pool.wait_ge(sq_done, sq_base(v) + 3 * k + c + 1)
                        pool.wait_ge(sq_added, sq_base(v) + 3 * k + c - 2)
                        pool.tensor_tensor(t2[:, chunk(c)], t2[:, chunk(c)], t1[:, chunk(c)], ALU.add)\
                            .then_inc(sq_added, 1)

            for i in range(12):
                c, k = i // 4, i % 4
                t = t1[:, ds((i % 2) * 384, CHUNKS[c][1])]
                pool.wait_ge(sq_done, i + 1)
                if k == 0:
                    pool.tensor_copy(t2[:, chunk(c)], t).then_inc(sq_added, 1)
                else:
                    pool.wait_ge(sq_added, i)
                    pool.tensor_tensor(t2[:, chunk(c)], t2[:, chunk(c)], t, ALU.add).then_inc(sq_added, 1)
            pool.wait_ge(tr_act, n_set_act)
            pool.wait_ge(tr_dve, n_set_dve)

            def history(hist, src, convs, stashes):
                _, gs = sp_view(convin, hist)
                wait(pool, conv_done, convs)
                wait(pool, stash_done, stashes)
                pool.tensor_copy(gs[:, :, 0:hist], src.rearrange("p o (b w) -> p (o b) w", b=DEC_B))\
                    .then_inc(hist_ready, 1)

            def new_state(hist, dst_p, dst_s, b, n):
                gp, gs = sp_view(convin, hist)
                pool.wait_ge(bank_free[b], n + 1)
                pool.tensor_copy(dst_p, gp[:, SEQ:SEQ + hist].rearrange("p (o w) -> p o w", o=1))
                pool.tensor_copy(dst_s.rearrange("p o (b w) -> p (o b) w", b=DEC_B), gs[:, :, DEC_T:])\
                    .then_inc(stash_done, 1)

            def lru_block(c):
                for s in range(2):
                    kt = 2 * c + s
                    history(3, pcol[:, ds(kt, 1), C_SCONV:C_SCONV + 24], 2 * kt, kt)
                    pool.wait_ge(hist_ready, kt + 1)
                    new_state(3, lstash[:, ds(kt, 1), 32:35], lstash[:, ds(kt, 1), 0:24], 3 * s + 2, 4 * c)
                for m in range(2):
                    kt = 2 * c + m
                    pool.wait_ge(scan_done, kt + 1)
                    pool.tensor_copy(lstash[:, ds(kt, 1), 35:36], y[:, SEQ - 1:SEQ].rearrange("p (o t) -> p o t", o=1))
                    pool.tensor_copy(lstash[:, ds(kt, 1), 24:32].rearrange("p o b -> p (o b)"),
                                     requests(y[:, SEQ:T])[:, :, DEC_T - 1]).then_inc(hlast_done, 1)

            lru_block(0)
            with pool.Fori(1, LRU_BLOCKS) as c:
                lru_block(c)
            def ffn(layer):
                base = layer * FT
                with pool.Fori(0, FT) as f:
                    g = base + f
                    history(2, fcol[:, ds(f, 1), 20 * layer + F_S:20 * layer + F_S + 16], 2 * (KD + g), KD + g)
                    _, gs = sp_view(convin, 2)
                    gp, _ = sp_view(convin, 2)
                    pool.wait_ge(conv_done, 2 * (KD + g) + 2)
                    pool.tensor_copy(fstash[:, ds(f, 1), 0:2], gp[:, SEQ:SEQ + 2].rearrange("p (o w) -> p o w", o=1))
                    pool.tensor_copy(fstash[:, ds(f, 1), 2:18].rearrange("p o (b w) -> p (o b) w", b=DEC_B),
                                     gs[:, :, DEC_T:]).then_inc(stash_done, 1)

            pool.wait_ge(z_ready, KD)
            sum_squares(1)
            ffn(0)
            sum_squares(2)
            pool.dma_start(strip_in_sb[0:BUCKETS, FV:FV + HEADS], A["rel_bias"]).then_inc(strip_in, 16)
            pool.dma_start(strip_in_sb[:, 0:FV], A["onehot"]).then_inc(strip_in, 16)
            for i in range(NSTEP):
                a, e, b = steps[i]
                m = 4 if b < NB else 2
                inv = stat[:, 6, 4 * (i % NPB):4 * (i % NPB) + m].rearrange("p (j o) -> p j o", o=1)
                if b < NB:
                    w = pb[i % NPB][:, :, (0 if b > 0 else WIN):]
                else:
                    w = pb[i % NPB][:, :, :].rearrange("p a b -> p (a b)")[:, 0:2 * LS].rearrange("p (h s) -> p h s", h=2)
                pool.wait_ge(inv_ready, i + 1)
                pool.tensor_tensor(w, w, inv.broadcast_to([P, m, w.shape[2]]), ALU.mult).then_inc(p_ready, 1)
            pool.wait_ge(z_hi, KD + 1)
            pool.wait_ge(o_copied, NSTEP)
            sum_squares(3)
            pool.memset(convin[:, 0:FFN_W - 1], 0.0)
            pool.wait_ge(fst_cp, STATE0[1])
            ffn(1)


def onehot_strip():
    dist = (2 * WIN - 1) - np.arange(FV)
    exact = BUCKETS // 2
    d = np.maximum(dist, 0)
    df = np.maximum(d, 1).astype(np.float32)
    large = exact + (np.log(df / exact) / np.float32(np.log(WIN / exact)) * (BUCKETS - exact)).astype(np.int32)
    bucket = np.where(d < exact, d, np.minimum(large, BUCKETS - 1))
    valid = (dist >= 0) & (dist < WIN)
    rows = np.zeros((BUCKETS + 1, FV), np.float32)
    rows[bucket[valid], np.arange(FV)[valid]] = 1.0
    rows[BUCKETS, ~valid] = NEG
    return rows


_OUTS = [("y_prompt", (1, SEQ, D)), ("y_sample", (DEC_B, DEC_T, D)), ("lru_h_p", (1, 1, D)),
         ("lru_conv_p", (1, 1, CONV_W - 1, D)), ("ffn_conv_p", (2, 1, FFN_W - 1, D_FF)),
         ("k_win_p", (1, WIN, KV_HEADS, HD)), ("v_win_p", (1, WIN, KV_HEADS, HD)), ("lru_h_s", (1, DEC_B, D)),
         ("lru_conv_s", (1, DEC_B, CONV_W - 1, D)), ("ffn_conv_s", (2, DEC_B, FFN_W - 1, D_FF)),
         ("k_win_s", (DEC_B, WIN, KV_HEADS, HD)), ("v_win_s", (DEC_B, WIN, KV_HEADS, HD))]


def kernel(**inputs):
    import numpy as _np
    import concourse.bacc as _bacc
    from concourse import mybir as _mybir
    from concourse.bass_utils import run_bass_kernel_spmd as _run

    nc = _bacc.Bacc("TRN2", target_bir_lowering=False, num_devices=1)
    arrays, A = {}, {}
    for name, a in [*inputs.items(), ("onehot", onehot_strip())]:
        a = _np.ascontiguousarray(a)
        arrays[f"in_{name}"] = a
        A[name] = nc.dram_tensor(f"in_{name}", a.shape, _mybir.dt.from_np(a.dtype), kind="ExternalInput").ap()
    for name, shape in _OUTS:
        A[name] = nc.dram_tensor(f"out_{name}", shape, _mybir.dt.float32, kind="ExternalOutput").ap()
    build(nc, A)
    r = _run(nc, [arrays], core_ids=[0])
    return tuple(r.results[0][f"out_{name}"] for name, _ in _OUTS)
```

```python
from contextlib import ExitStack

import numpy as np

import concourse.bass as bass
from concourse import mybir

P = 128
F32 = mybir.dt.float32
F32R = mybir.dt.float32r
ACT = mybir.ActivationFunctionType
ALU = mybir.AluOpType
AX_X = mybir.AxisListType.X
ds = bass.ds

D = 1024
SEQ = 1024
DEC_B = 8
DEC_T = 8
NS = DEC_B * DEC_T
T = SEQ + NS
KD = D // P
LRU_BLOCKS = 4
CONV_W = 4
D_FF = 3 * D
FT = D_FF // P
FFN_W = 3
HEADS = 16
KV_HEADS = 4
HD = 64
WIN = 128
NB = SEQ // WIN
LS = WIN + DEC_T
BUCKETS = 32
EPS = 1e-6
NEG = -1e30
C_GATE = 8.0
SCALE = HD ** -0.5
CHUNKS = [(0, 384), (384, 384), (768, 320)]
FB = 6
NFB = FT // FB
FV = 384

N_A = 0
N_OUT = N_A + 4 * LRU_BLOCKS
N_F0 = N_OUT + KD // 2
N_KV = N_F0 + NFB * (FB + KD // 2)
N_Q = N_KV + 2
N_O = N_Q + KD // 2
N_F1 = N_O + KD // 2
N_END = N_F1 + NFB * (FB + KD // 2)

(C_ANORM, C_CONVW, C_CONVB, C_RB, C_IB, C_LAM, C_KVN, C_BN, C_FN, C_BO, C_BQ, C_BKV, C_SCONV, C_SH) = \
    (0, 1, 5, 6, 7, 8, 9, 10, 11, 13, 14, 15, 16, 40)
NPROW = 48
N_PRM, N_FRM = 18, 10
NPB = 3
LROW = 36
NFROW = 40
F_W, F_B, F_S = 0, 3, 4


class Tally:

    def __init__(self, eng, sem):
        self.eng, self.sem, self.at = eng, sem, 0

    def mark(self, ins):
        ins.then_inc(self.sem, 1)
        self.at = self.at + 1

    def settle(self):
        self.eng.wait_ge(self.sem, self.at)


def wait(eng, sem, value):
    if not isinstance(value, int) or value > 0:
        eng.wait_ge(sem, value)


def build(nc, A):
    with ExitStack() as ctx:
        def sem(name):
            return ctx.enter_context(nc.semaphore(name))

        base = (nc.sbuf_base + 63) // 64 * 64
        top = [base]

        def at(name, shape, dt, offset):
            return nc.alloc_sbuf_tensor_at(name, shape, dt, offset=offset)

        def take(name, shape, dt):
            offset = top[0]
            top[0] += (int(np.prod(shape[1:])) * 4 + 31) // 32 * 32
            return at(name, shape, dt, offset)

        x = take("x", [P, KD, T], F32)
        reg_n = top[0]
        nhi = take("nhi", [P, KD, T], F32R)
        nlo = take("nlo", [P, KD, T], F32R)
        reg_h = top[0]
        hhi = take("hhi", [P, FB, T], F32R)
        hlo = take("hlo", [P, FB, T], F32R)
        raw = [take(f"raw{s}", [P, KD * P], F32) for s in range(2)]
        whi = [take(f"whi{s}", [P, KD * P], F32R) for s in range(2)]
        wlo = [take(f"wlo{s}", [P, KD * P], F32R) for s in range(2)]
        convin = take("convin", [P, 1120], F32)
        y = take("y", [P, T], F32)
        rstd = take("rstd", [P, T], F32)
        t1 = take("t1", [P, T], F32)
        t2 = take("t2", [P, T], F32)
        pcol = take("pcol", [P, KD, NPROW + 4], F32)
        lstash = pcol[:, :, C_SCONV:C_SCONV + LROW]
        fcol = take("fcol", [P, FT, NFROW], F32)
        fstash = take("fstash", [P, FT, 2 + 2 * DEC_B], F32)
        ident = take("ident", [P, P], F32)
        ones = take("ones", [P, P], F32)
        blockones = take("blockones", [P, P], F32)
        epst = take("epst", [P, 1], F32)
        qkn = take("qkn", [P, 2], F32)
        sp = take("sp", [P, 2, KD], F32)
        spt = take("spt", [P, 4, KD], F32)
        h0a = take("h0a", [P, DEC_B], F32)
        sinkb = take("sinkb", [P, HEADS], F32)
        sinks_s = take("sinks_s", [P, KV_HEADS], F32)
        stat = take("stat", [P, 8, 4 * NPB], F32)
        assert top[0] <= nc.sbuf_usable_end, top[0]

        z = at("z", [P, KD, T], F32, reg_h)
        xchi = at("xchi", [P, 2, T], F32R, reg_h + KD * T * 4)
        xclo = at("xclo", [P, 2, T], F32R, reg_h + (KD + 2) * T * 4)
        xrows = at("xrows", [P, 9, D], F32, reg_h)
        prow = xrows[NS:NS + NPROW, 8, :]
        frow = at("frow", [NFROW, D_FF], F32, reg_h + 9 * D * 4)
        qz = at("qz", [P, KD, T], F32, reg_h)
        kf = at("kf", [P, 2, T], F32, reg_h + KD * T * 4)
        vt = at("vt", [P, NB, 256], F32, reg_h + (KD + 2) * T * 4)
        tlast = at("tlast", [P, 2, T], F32, reg_n + (2 * KD - 2) * T * 4)
        top[0] = reg_n
        bias = take("bias", [P, HEADS, 2 * WIN], F32)
        sbias = take("sbias", [P, KV_HEADS, LS], F32)
        ck = take("ck", [P, DEC_B, 256], F32)
        kct = take("kct", [P, 2, DEC_B * WIN], F32)
        cv = take("cv", [P, DEC_B, 256], F32)
        vnew = take("vnew", [DEC_T, DEC_B, 256], F32)
        pb = [take("pb0", [P, 4, 2 * WIN], F32), take("pb1", [P, 4, 2 * WIN], F32),
              y[:, 0:8 * WIN].rearrange("p (j s) -> p j s", j=4)]
        pt = take("pt", [P, 2, 512], F32)
        kvrow = take("kvrow", [P, 3, 256], F32)
        assert top[0] <= reg_h
        yrows = at("yrows", [P, 9, D], F32, reg_n)
        fout = at("fout", [18, D_FF], F32, reg_h)
        lout = at("lout", [LROW, D], F32, reg_h + D_FF * 4)

        ps = ctx.enter_context(nc.psum_tensor("ps", [P, 8, 512], F32))

        raw_ready = [sem(f"raw_ready{s}") for s in range(2)]
        hi_ready = [sem(f"hi_ready{s}") for s in range(2)]
        lo_ready = [sem(f"lo_ready{s}") for s in range(2)]
        bank_ready = [sem(f"bank_ready{b}") for b in range(6)]
        bank_free = [sem(f"bank_free{b}") for b in range(6)]
        rows_in = [sem(f"rows_in{i}") for i in range(9)]
        const_ready = sem("const_ready")
        prm_in = sem("prm_in")
        frm_in = sem("frm_in")
        sq_dve = sem("sq_dve")
        tr_ready = sem("tr_ready")
        tr_act = sem("tr_act")
        tr_dve = sem("tr_dve")
        dve_seq = sem("dve_seq")
        pool_seq = sem("pool_seq")
        sq_done = sem("sq_done")
        sq_added = sem("sq_added")
        stat_ready = sem("stat_ready")
        stat_sqrt = sem("stat_sqrt")
        xn_mult = sem("xn_mult")
        xn_hi = sem("xn_hi")
        xn_lo = sem("xn_lo")
        xn_lo_pool = sem("xn_lo_pool")
        sp_exp = sem("sp_exp")
        sp_ready = sem("sp_ready")
        hist_ready = sem("hist_ready")
        conv_done = sem("conv_done")
        stash_done = sem("stash_done")
        gelu_done = sem("gelu_done")
        hhi_done = sem("hhi_done")
        hlo_done = sem("hlo_done")
        xc_hi = sem("xc_hi")
        xc_lo = sem("xc_lo")
        tanh_done = sem("tanh_done")
        a_ready = sem("a_ready")
        one_a2 = sem("one_a2")
        root_ready = sem("root_ready")
        scan_done = sem("scan_done")
        hlast_done = sem("hlast_done")
        z_ready = sem("z_ready")
        z_hi = sem("z_hi")
        z_lo = sem("z_lo")
        z_lo_pool = sem("z_lo_pool")
        fst_tr = sem("fst_tr")
        fst_cp = sem("fst_cp")
        states_out = sem("states_out")
        win_out = sem("win_out")
        y_out = sem("y_out")
        strip_in = sem("strip_in")
        strip_one = sem("strip_one")
        strip_mm = sem("strip_mm")
        strip_cp = sem("strip_cp")
        strip_out = sem("strip_out")
        ck_in = sem("ck_in")
        cv_in = sem("cv_in")
        bias_in = [sem(f"bias_in{g}") for g in range(KV_HEADS)]
        sbias_in = sem("sbias_in")
        sink_in = sem("sink_in")
        prep_dve = sem("prep_dve")
        vnew_in = sem("vnew_in")
        hsq = sem("hsq")
        hmean = sem("hmean")
        hroot = sem("hroot")
        hnorm = sem("hnorm")
        prep_tr = sem("prep_tr")
        prep_cp = sem("prep_cp")
        qs_ready = sem("qs_ready")
        sc_ready = sem("sc_ready")
        sc_read = sem("sc_read")
        max_ready = sem("max_ready")
        exp_done = sem("exp_done")
        inv_ready = sem("inv_ready")
        p_ready = sem("p_ready")
        pt_ready = sem("pt_ready")
        pt_copied = sem("pt_copied")
        o_ready = sem("o_ready")
        o_copied = sem("o_copied")
        qkv_ev = sem("qkv_ev")

        strip_dram = nc.dram_tensor("strip", [HEADS * P * FV], F32, kind="Internal").ap()
        strip_in_sb = at("strip_in_sb", [BUCKETS + 1, FV + HEADS], F32, reg_h + (KD + 2) * T * 4)
        ksq = at("ksq", [P, T], F32, reg_h + (KD + 2) * T * 4 + 4 * 960)
        strip_sb2 = at("strip_sb2", [HEADS, FV], F32, reg_h + (KD + 2) * T * 4 + 4 * (FV + HEADS))

        def chunk(c):
            return ds(CHUNKS[c][0], CHUNKS[c][1])

        def bank(b, c):
            return ps[:, b, 0:CHUNKS[c][1]]

        def sp_view(buf, hist):
            w = SEQ + hist
            return buf[:, 0:w], buf[:, w:w + DEC_B * (DEC_T + hist)].rearrange("p (b t) -> p b t", b=DEC_B)

        def gate_tiles(c, m):
            if m == 0:
                return t1[:, :], t2[:, :]
            if isinstance(c, int) and c == LRU_BLOCKS - 1:
                return tlast[:, 0, :], tlast[:, 1, :]
            return tuple(z[:, ds(2 * c + 2 + i, 1), :].rearrange("p o t -> p (o t)") for i in range(2))

        def requests(ap):
            return ap.rearrange("p (b t) -> p b t", b=DEC_B)

        def w_cols(w, col):
            return w.rearrange("(k p) n -> p k n", p=P)[:, :, ds(col, P)]

        setup = [("x", tt, half) for tt in range(3) for half in range(2)]
        setup += [("x", tt, half) for tt in range(3, 6) for half in range(2)]
        setup += [("p", half) for half in range(2)]
        setup += [("x", tt, half) for tt in range(6, 9) for half in range(2)]
        setup += [("f", half) for half in range(2)]
        SET_BANK = [0, 1, 2, 3, 4, 5] + [0, 1, 2, 3, 4, 5] + [0, 1] + [2, 1, 4, 5, 2, 1] + [6, 7]
        SET_END = [6, 14, 20]
        SQ_ACT = [4, 6, 6]
        NSET = len(setup)

        def sq_base(v):
            return 0 if v == 0 else 24 * v - 24 + sum(SQ_ACT)

        def lo_base(u):
            return 0 if u == 0 else 3 * KD + 3 * KD // 2 * (u - 1)

        def lo_base_pool(u):
            return 3 * KD // 2 * (u - 1)

        def norm_buffer(u, i):
            w = CHUNKS[i // KD][1]
            if u == 0 or i % 4 < 2:
                return y[:, ds((i % 2) * 384, w)]
            return convin[:, ds(8 + (i % 2) * 384, w)]

        def root_buffer(i):
            return rstd if i >= 3 and i % 2 == 1 else convin

        def job_out(job, bank_no):
            if job[0] == "p":
                h = job[1]
                return (ps[:, bank_no, 0:4 * NPROW].rearrange("p (k c) -> p k c", k=4), pcol[:, 4 * h:4 * h + 4, 0:NPROW])
            if job[0] == "f":
                h = job[1]
                return (ps[:, bank_no, 0:12 * NFROW].rearrange("p (k c) -> p k c", k=12),
                        fcol[:, 12 * h:12 * h + 12, :])
            _, tt, h = job
            w = P if tt < 8 else NS
            return (ps[:, bank_no, 0:4 * w].rearrange("p (k c) -> p k c", k=4),
                    x[:, 4 * h:4 * h + 4, tt * P:tt * P + w])

        ends = [(tt, half) for tt in range(9) for half in range(2)]
        TR_DVE_END, TR_ACT_END = [], []
        n_set_act, n_set_dve = (NSET + 1) // 2, NSET // 2
        for g in range(3):
            m = 6 * (g + 1)
            TR_ACT_END.append(n_set_act + (m + 1) // 2)
            TR_DVE_END.append(n_set_dve + m // 2)

        def end_out(m):
            tt, h = ends[m]
            w = P if tt < 8 else NS
            return ps[0:w, m % 8, :], yrows[0:w, tt, 512 * h:512 * h + 512]

        steps = [(a, e, b) for a in range(2) for e in range(2) for b in range(NB + 1)]
        NSTEP = len(steps)

        STATE0 = [0, 8, 14]

        def state_jobs(layer):
            jobs = []
            if layer == 0:
                for m in range(2):
                    b = 6 + len(jobs) % 2
                    outs = [(ps[0:LROW, b, i * P:(i + 1) * P], lstash[:, 4 * m + i, :]) for i in range(4)]
                    jobs.append((outs, ps[0:LROW, b, :], lout[:, m * 512:(m + 1) * 512]))
            for m in range(FT // 4):
                b = 6 + len(jobs) % 2
                outs = [(ps[0:18, b, i * P:(i + 1) * P], fstash[:, 4 * m + i, :]) for i in range(4)]
                jobs.append((outs, ps[0:18, b, :], fout[:, m * 512:(m + 1) * 512]))
            return jobs

        def prep_jobs():
            jobs = []
            for m in range(4):
                outs = []
                for q in range(4):
                    blk, a = 2 * m + q // 2, q % 2
                    src = (t1, t2)[a]
                    outs.append((ps[:, m, q * P:(q + 1) * P], src[:, blk * P:(blk + 1) * P]))
                jobs.append((outs, ps[:, m, :].rearrange("p (b c) -> p b c", b=2), vt[:, 2 * m:2 * m + 2, :]))
            outs = [(ps[:, 4, a * P:(a + 1) * P], kf[:, a, SEQ - WIN:SEQ]) for a in range(2)]
            jobs.append((outs, ps[:, 4, 0:256], kvrow[:, 0, :]))
            outs = [(ps[0:NS, 5, a * P:(a + 1) * P], kf[:, a, SEQ:T]) for a in range(2)]
            outs += [(ps[0:NS, 5, 256 + a * P:256 + (a + 1) * P], (t1, t2)[a][:, SEQ:T]) for a in range(2)]
            jobs.append((outs, ps[0:NS, 5, :].rearrange("p (b c) -> p b c", b=2), kvrow[0:NS, 1:3, :]))
            for m in range(4):
                outs = []
                for q in range(4):
                    r, a = 4 * (m % 2) + q, m // 2
                    outs.append((ps[:, (6 + m) % 8, q * P:(q + 1) * P], ck[:, r, a * P:(a + 1) * P]))
                jobs.append((outs, ps[:, (6 + m) % 8, :], kct[:, m // 2, 512 * (m % 2):512 * (m % 2) + 512]))
            return jobs

        block = ctx.enter_context(nc.Block())

        @block.sync
        def _(eng):
            def token_rows(tt):
                if tt < 8:
                    src, dst = A["x_prompt"][0, tt * P:(tt + 1) * P, :], xrows[:, tt, :]
                else:
                    src, dst = A["x_sample"].rearrange("b t d -> (b t) d"), xrows[0:NS, 8, :]
                eng.dma_start(dst, src).then_inc(rows_in[tt], 16)

            def parameter_rows():
                rows = [(0, A["a_norm"]), (1, A["a_conv_w"][0]), (5, A["a_conv_b"]), (6, A["a_gate_r_b"]),
                        (7, A["a_gate_i_b"]), (8, A["a_lambda"]), (9, A["kv_norm"].rearrange("(a d) -> a d", a=1)),
                        (10, A["b_norm"]), (11, A["f_norm"]), (13, A["b_o"]),
                        (16, A["state_lru_conv"][0].rearrange("b w d -> (b w) d")), (40, A["state_lru_h"][0])]
                count = 0
                for r, src in rows:
                    eng.dma_start(prow[r:r + src.shape[0], :], src).then_inc(prm_in, 16)
                    count += 1
                bq = A["b_q"].rearrange("o (a e j d) -> o a e j d", a=2, e=2, j=4)
                for e in range(2):
                    for a in range(2):
                        dst = prow[14:15, a * 512:a * 512 + 512].rearrange("o (j e d) -> o j e d", j=4, e=2)[:, :, e, :]
                        eng.dma_start(dst, bq[:, a, e, :, :]).then_inc(prm_in, 16)
                        count += 1
                for h in range(2):
                    eng.dma_start(prow[15:16, 512 * h:512 * h + 512], A["b_kv"].rearrange("(a d) -> a d", a=1))\
                       .then_inc(prm_in, 16)
                    count += 1
                assert count == N_PRM, count

            def load(n, s, src, cols):
                if not isinstance(n, int):
                    n = eng.snap(eng.to_reg(n))
                    eng.wait_ge(rows_in[0], 16)
                wait(eng, lo_ready[s], n)
                eng.dma_start(raw[s][:, 0:cols].rearrange("p (k n) -> p k n", n=P), src).then_inc(raw_ready[s], 16)

            w_in, w_out = A["a_w_in"][0], A["a_w_out"][0]

            def gate_w(w, c, m):
                return w[0][ds(c, 1), :, m * P:(m + 1) * P].rearrange("a (k p) n -> p (a k) n", p=P)

            def conv_loads(c):
                for s in range(2):
                    load(4 * c, s, w_cols(w_in, D + c * 256 + s * P), KD * P)

            def lru_loads(c):
                if not isinstance(c, int):
                    conv_loads(c)
                for s in range(2):
                    load(4 * c + 1, s, w_cols(w_in, c * 256 + s * P), KD * P)
                for m in range(2):
                    load(4 * c + 2 + m, 0, gate_w(A["a_gate_r_w"], c, m), 2 * P)
                    load(4 * c + 2 + m, 1, gate_w(A["a_gate_i_w"], c, m), 2 * P)

            for tt in range(6):
                token_rows(tt)
            parameter_rows()
            conv_loads(0)
            for tt in range(6, 9):
                token_rows(tt)
            count = 0
            for layer in range(2):
                o = 20 * layer
                for r, src in ((0, A["f_conv_w"][layer]), (3, A["f_conv_b"][layer:layer + 1, :]),
                               (4, A["state_ffn_conv"][layer].rearrange("b w d -> (b w) d"))):
                    eng.dma_start(frow[o + r:o + r + src.shape[0], :], src).then_inc(frm_in, 16)
                    count += 1
            with nc.allow_non_contiguous_dma(reason="64 single elements each"):
                for e in range(2):
                    for i, name in enumerate(("q_norm", "k_norm")):
                        src = A[name][0, :] if name == "q_norm" else A[name]
                        eng.dma_start(qkn[HD * e:HD * e + HD, i:i + 1], src.rearrange("(d o) -> d o", o=1))\
                           .then_inc(frm_in, 16)
                        count += 1
            assert count == N_FRM, count
            lru_loads(0)
            with nc.allow_non_contiguous_dma(reason="a few single elements"):
                eng.dma_start(sinkb[:, :], bass.AP(A["sinks"].tensor, 0, [[0, P], [1, HEADS]])).then_inc(sink_in, 16)
                for r in range(4):
                    for j in range(4):
                        p0 = 32 * r + DEC_T * j
                        src = bass.AP(A["sinks"].tensor, j, [[0, DEC_T], [4, KV_HEADS], [1, 1]])
                        eng.dma_start(sinks_s[p0:p0 + DEC_T, :].rearrange("p (g o) -> p g o", o=1), src)\
                           .then_inc(sink_in, 16)
            with eng.Fori(1, LRU_BLOCKS) as c:
                lru_loads(c)
            with eng.Fori(0, KD // 2) as i:
                for s in range(2):
                    load(N_OUT + i, s, w_cols(w_out, i * 256 + s * P), KD * P)

            def ffn(layer, n0):
                up, down = A["f_w_up"][layer], A["f_w_down"][layer]
                with eng.Fori(0, NFB) as b:
                    with eng.Fori(0, FB) as j:
                        for s in range(2):
                            load(n0 + b * (FB + KD // 2) + j, s, w_cols(up, s * D_FF + b * (FB * P) + j * P), KD * P)
                    with eng.Fori(0, KD // 2) as i:
                        for s in range(2):
                            src = down.rearrange("(k p) n -> p k n", p=P)[:, ds(b * FB, FB), ds(i * 256 + s * P, P)]
                            load(n0 + b * (FB + KD // 2) + FB + i, s, src, FB * P)

            ffn(0, N_F0)
            for m in range(2):
                for s in range(2):
                    load(N_KV + m, s, w_cols(A["w_kv"], (2 * m + s) * P), KD * P)
            wq = A["w_q"][0].rearrange("(k p) (a e j d) -> p k a e j d", p=P, a=2, e=2, j=4)
            for t in range(KD):
                a, j, n, s = t // 4, t % 4, N_Q + t // 2, t % 2
                eng.wait_ge(lo_ready[s], n)
                for e in range(2):
                    dst = raw[s][:, :].rearrange("p (k e d) -> p k e d", k=KD, e=2)[:, :, e, :]
                    eng.dma_start(dst, wq[:, :, a, e, j, :]).then_inc(raw_ready[s], 16)
            def attention_data():
                eng.wait_ge(bank_ready[5], N_O)
                eng.wait_ge(strip_out, 16)
                cache = {n: A[f"cache_{n}_win"].rearrange("r w h d -> w r (h d)") for n in "kv"}
                eng.dma_start(ck[:, :, :], cache["k"]).then_inc(ck_in, 16)
                for g in range(KV_HEADS):
                    src = bass.AP(strip_dram.tensor, WIN - 1 + 4 * g * P * FV, [[FV - 1, P], [P * FV, 4], [1, 2 * WIN]])
                    eng.dma_start(bias[:, 4 * g:4 * g + 4, :], src).then_inc(bias_in[g], 16)
                    if g == 0:
                        eng.dma_start(cv[:, :, :], cache["v"]).then_inc(cv_in, 16)
                        for r in range(4):
                            for j in range(4):
                                src = bass.AP(strip_dram.tensor, WIN - 1 + j * P * FV,
                                              [[FV - 1, DEC_T], [4 * P * FV, KV_HEADS], [1, LS]])
                                p0 = 32 * r + DEC_T * j
                                eng.dma_start(sbias[p0:p0 + DEC_T, :, :], src).then_inc(sbias_in, 16)
                eng.wait_ge(prep_dve, 3)
                eng.wait_ge(prep_cp, 3)
                for r in range(DEC_B):
                    eng.dma_start(vnew[:, r, :], kvrow[r * DEC_T:(r + 1) * DEC_T, 2, :]).then_inc(vnew_in, 16)
                for i, name in enumerate("kv"):
                    out = A[f"{name}_win_s"].rearrange("r w h d -> r w (h d)")
                    old = A[f"cache_{name}_win"].rearrange("r w h d -> r w (h d)")
                    eng.dma_start(out[:, 0:WIN - DEC_T, :], old[:, DEC_T:, :]).then_inc(win_out, 16)
                    for r in range(DEC_B):
                        eng.dma_start(out[r, WIN - DEC_T:, :], kvrow[r * DEC_T:(r + 1) * DEC_T, 1 + i, :])\
                           .then_inc(win_out, 16)
                eng.dma_start(A["k_win_p"][0].rearrange("w h d -> w (h d)"), kvrow[:, 0, :]).then_inc(win_out, 16)
                eng.dma_start(A["v_win_p"][0].rearrange("w h d -> w (h d)"), vt[:, NB - 1, :]).then_inc(win_out, 16)

            wo = A["w_o"][0].rearrange("(a e j d) n -> d a e j n", a=2, e=2, j=4)
            for t in range(KD):
                n, s = N_O + t // 2, t % 2
                if t == 2:
                    attention_data()
                eng.wait_ge(lo_ready[s], n)
                for e in range(2):
                    for a in range(2):
                        dst = raw[s][HD * e:HD * e + HD, a * 512:a * 512 + 512].rearrange("p (j n) -> p j n", j=4)
                        eng.dma_start(dst, wo[:, a, e, :, t * P:(t + 1) * P]).then_inc(raw_ready[s], 16)
            ffn(1, N_F1)

            for g in range(3):
                eng.wait_ge(tr_dve, TR_DVE_END[g])
                eng.wait_ge(tr_act, TR_ACT_END[g])
                if g < 2:
                    dst = A["y_prompt"][0, 384 * g:384 * g + 384, :].rearrange("(i p) d -> p i d", p=P)
                    eng.dma_start(dst, yrows[:, 3 * g:3 * g + 3, :]).then_inc(y_out, 16)
                else:
                    dst = A["y_prompt"][0, 768:1024, :].rearrange("(i p) d -> p i d", p=P)
                    eng.dma_start(dst, yrows[:, 6:8, :]).then_inc(y_out, 16)
                    eng.dma_start(A["y_sample"].rearrange("b t d -> (b t) d"), yrows[0:NS, 8, :])\
                       .then_inc(y_out, 16)
            eng.wait_ge(y_out, 16 * 4)

        def raw_count_at(n, phase):
            q, o = KD // 2, KD // 2
            if phase == "q":
                return 16 * (N_Q + 2 * (n - N_Q + 1))
            if phase == "o":
                return 16 * (N_Q + 2 * q + 4 * (n - N_O + 1))
            if phase == "f1":
                return 16 * (n + 1) + 16 * (q + 3 * o)
            return 16 * (n + 1)

        @block.tensor
        def _(pe):
            pe.wait_ge(const_ready, 4)

            def set_up(first, end):
                for m in range(first, end):
                    job, bk = setup[m], SET_BANK[m]
                    before_m = [i for i in range(m) if SET_BANK[i] == bk]
                    if before_m:
                        pe.wait_ge(tr_act if before_m[-1] % 2 == 0 else tr_dve, before_m[-1] // 2 + 1)
                    if job[0] == "p":
                        pe.wait_ge(prm_in, 16 * N_PRM)
                        for i in range(4):
                            k = 4 * job[1] + i
                            last = pe.transpose(ps[:, bk, i * NPROW:(i + 1) * NPROW], prow[:, k * P:(k + 1) * P],
                                                ident[NS:NS + NPROW, NS:NS + NPROW])
                    elif job[0] == "f":
                        pe.wait_ge(frm_in, 16 * N_FRM)
                        for i in range(12):
                            k = 12 * job[1] + i
                            last = pe.transpose(ps[:, bk, i * NFROW:(i + 1) * NFROW], frow[:, k * P:(k + 1) * P],
                                                ident[0:NFROW, 0:NFROW])
                    else:
                        _, tt, h = job
                        w = P if tt < 8 else NS
                        pe.wait_ge(rows_in[tt], 16)
                        for i in range(4):
                            k = 4 * h + i
                            last = pe.transpose(ps[:, bk, i * w:(i + 1) * w], xrows[0:w, tt, k * P:(k + 1) * P],
                                                ident[0:w, 0:w])
                    last.then_inc(tr_ready, 1)

            def piece(n, s, c, nk, mhi, mlo, before=None):
                wait(pe, bank_free[3 * s + c], n)
                out = bank(3 * s + c, c)
                for k in range(nk):
                    if before:
                        before(c, k)
                    w = ds(k * P, P)
                    pe.matmul(out, whi[s][:, w], mhi[:, k, chunk(c)], start=(k == 0), stop=False)
                    pe.matmul(out, whi[s][:, w], mlo[:, k, chunk(c)], start=False, stop=False)
                    last = pe.matmul(out, wlo[s][:, w], mhi[:, k, chunk(c)], start=False, stop=(k == nk - 1))
                last.then_inc(bank_ready[3 * s + c], 1)

            def unit(n, s, nk, mhi, mlo, before=None, stats_of=None):
                pe.wait_ge(hi_ready[s], n + 1)
                pe.wait_ge(lo_ready[s], n + 1)
                def stats_between(c, k):
                    if (c, k) == (1, nk - 2):
                        stats(stats_of, 0)
                for c in range(3):
                    piece(n, s, c, nk, mhi, mlo, before if stats_of is None else stats_between)

            def stats(v, c):
                if v == 0:
                    pe.wait_ge(sq_added, sum(SQ_ACT[:c + 1]))
                    pe.wait_ge(sq_dve, c + 1)
                else:
                    pe.wait_ge(sq_added, sq_base(v) + 22 + c)
                if c == 2:
                    pe.wait_ge(stat_sqrt, 3 * v + 1)
                out = bank(6 + c % 2, c)
                last = pe.matmul(out, ones[:, :], t2[:, chunk(c)], start=True, stop=(v > 0))
                if v == 0:
                    last = pe.matmul(out, ones[:, :], convin[:, ds(384, CHUNKS[c][1])], start=False, stop=True)
                last.then_inc(stat_ready, 1)

            def first_pair(n, u, v, slots=None):
                if v:
                    stats(v, 1)

                def first_piece(c, k):
                    if (c, k) == (0, KD - 2):
                        stats(0, 1)
                    if (c, k) == (1, KD // 2):
                        stats(0, 2)
                    normed(u)(c, k)

                for c in range(3):
                    for s in range(2):
                        if c == 0:
                            pe.wait_ge(hi_ready[s], n + 1)
                            pe.wait_ge(lo_ready[s], n + 1)
                        piece(n, s, c, KD, nhi, nlo,
                              None if s else first_piece if v == 0 and c < 2 else normed(u))
                        if (c, s) == (0, 1) and v:
                            stats(v, 2)
                        if slots:
                            slots(2 * c + s)
                        if (v, c, s) == (0, 0, 0):
                            set_up(SET_END[1], SET_END[2])
                        elif (v, c, s) == (0, 0, 1):
                            pe.wait_ge(tr_act, SET_END[2] // 2)
                            pe.wait_ge(tr_dve, SET_END[2] // 2)
                        elif (v, c, s) == (0, 1, 1):
                            pe.wait_ge(stat_sqrt, 3)
                            set_up(SET_END[2], NSET)

            def normed(u):
                def before(c, k):
                    if k % 2 == 0 and u == 0:
                        pe.wait_ge(xn_lo, 8 * c + k + 2)
                    elif k % 2 == 0:
                        pe.wait_ge(xn_lo, lo_base(u) + 4 * c + k // 2 + 1)
                        pe.wait_ge(xn_lo_pool, lo_base_pool(u) + 4 * c + k // 2 + 1)
                return before

            set_up(0, SET_END[1] - 2)
            stats(0, 0)
            set_up(SET_END[1] - 2, SET_END[1])
            pe.wait_ge(tr_act, SET_END[1] // 2)
            pe.wait_ge(tr_dve, SET_END[1] // 2)

            def lru_block(c, first=False):
                if first:
                    first_pair(0, 0, 0)
                else:
                    for s in range(2):
                        unit(4 * c, s, KD, nhi, nlo)
                for s in range(2):
                    unit(4 * c + 1, s, KD, nhi, nlo)
                pe.wait_ge(xc_lo, 2 * c + 2)
                for m in range(2):
                    for s in range(2):
                        unit(4 * c + 2 + m, s, 2, xchi, xclo)

            lru_block(0, first=True)
            with pe.Fori(1, LRU_BLOCKS) as c:
                lru_block(c)

            def z_split(base_count):
                def before(c, k):
                    pe.wait_ge(z_lo, base_count + k + 1)
                return before

            for ks in (range(KD - 2), range(KD - 2, KD)):
                for s in range(2):
                    if ks[0] == 0:
                        pe.wait_ge(hi_ready[s], N_OUT + 1)
                        pe.wait_ge(lo_ready[s], N_OUT + 1)
                    for c in range(3):
                        if ks[0] == 0:
                            pe.wait_ge(bank_free[3 * s + c], N_OUT)
                        for k in ks:
                            if k < KD - 2:
                                pe.wait_ge(z_lo_pool, k + 1)
                            else:
                                pe.wait_ge(z_lo, k - (KD - 2) + 1)
                            w, out = ds(k * P, P), bank(3 * s + c, c)
                            pe.matmul(out, whi[s][:, w], nhi[:, k, chunk(c)], start=(k == 0), stop=False)
                            pe.matmul(out, whi[s][:, w], nlo[:, k, chunk(c)], start=False, stop=False)
                            last = pe.matmul(out, wlo[s][:, w], nhi[:, k, chunk(c)], start=False, stop=(k == KD - 1))
                        if ks[0] > 0:
                            last.then_inc(bank_ready[3 * s + c], 1)
            with pe.Fori(1, KD // 2 - 1) as i:
                for s in range(2):
                    unit(N_OUT + i, s, KD, nhi, nlo)
            for s in range(2):
                unit(N_F0 - 1, s, KD, nhi, nlo, stats_of=1 if s == 1 else None)

            def ffn(layer, n0, u, v):
                def block_(b, first, last):
                    nb = n0 + b * (FB + KD // 2)
                    f1 = layer * FT + b * FB + FB
                    if first:
                        first_pair(nb, u, v)
                    with pe.Fori(1 if first else 0, FB) as j:
                        unit(nb + j, 0, KD, nhi, nlo)
                        unit(nb + j, 1, KD, nhi, nlo)

                    def hidden(c, k):
                        if c == 0 and k == 0:
                            pe.wait_ge(hlo_done, 3 * f1 - 3)
                        if k == FB - 1:
                            pe.wait_ge(hlo_done, 3 * f1 - 2 + c)
                    with pe.Fori(0, KD // 2 - last) as i:
                        for s in range(2):
                            unit(nb + FB + i, s, FB, hhi, hlo, hidden if s == 0 else None)
                    if last:
                        for s in range(2):
                            unit(nb + FB + KD // 2 - 1, s, FB, hhi, hlo, stats_of=2 if layer == 0 and s == 1 else None)

                block_(0, True, False)
                with pe.Fori(1, NFB - 1) as b:
                    block_(b, False, False)
                block_(NFB - 1, False, True)

            def state_job(layer, m):
                if m == 0:
                    pe.wait_ge(stash_done, KD + (layer + 1) * FT)
                    if layer == 0:
                        pe.wait_ge(hlast_done, KD)
                if m >= 2:
                    pe.wait_ge(fst_cp, STATE0[layer] + m - 1)
                for o, t in state_jobs(layer)[m][0]:
                    last = pe.transpose(o, t, ident[:, :])
                last.then_inc(fst_tr, 1)

            ffn(0, N_F0, 1, 1)
            def head_stat(i, c):
                pe.wait_ge(hsq, i + 1)
                if 3 * i + c >= 2:
                    pe.wait_ge(hroot, 3 * i + c - 1)
                src = ksq if i == 1 else y
                pe.matmul(bank(6 + (3 * i + c) % 2, c), blockones[:, :], src[:, chunk(c)], start=True, stop=True)\
                  .then_inc(hmean, 1)

            def head_stats(i):
                for c in range(3):
                    head_stat(i, c)

            def kv_slots(q):
                if q == 3:
                    pe.wait_ge(strip_in, 32)
                    pe.wait_ge(strip_one, 1)
                    pe.wait_ge(stat_sqrt, 8)
                    pe.matmul(ps[0:HEADS, 7, 0:FV], strip_in_sb[:, FV:FV + HEADS], strip_in_sb[:, 0:FV], start=True,
                              stop=True).then_inc(strip_mm, 1)

            first_pair(N_KV, 2, 2, kv_slots)
            pe.wait_ge(stat_sqrt, 9)
            head_stat(0, 0)
            pe.wait_ge(strip_cp, 1)
            head_stat(0, 1)
            for c in range(3):
                for s in range(2):
                    if c == 0:
                        pe.wait_ge(hi_ready[s], N_KV + 2)
                        pe.wait_ge(lo_ready[s], N_KV + 2)
                    piece(N_KV + 1, s, c, KD, nhi, nlo)
                    q = 2 * c + s
                    if q == 0:
                        head_stat(0, 2)
                        head_stat(1, 0)
                    elif q == 1:
                        head_stat(1, 1)
                    elif q == 2:
                        head_stat(1, 2)
                    else:
                        if q == 3:
                            pe.wait_ge(hroot, 6)
                        state_job(0, 2 * (q - 3))
                        state_job(0, 2 * (q - 3) + 1)

            def q_slots(q):
                if q == 0:
                    state_job(0, 6)
                    state_job(0, 7)

            first_pair(N_Q, 3, None, q_slots)
            pe.wait_ge(fst_cp, STATE0[1])
            head_stats(2)
            for t in range(2, KD - 1):
                unit(N_Q + t // 2, t % 2, KD, nhi, nlo)
                head_stats(2 + t - 1)
            unit(N_O - 1, 1, KD, nhi, nlo)

            jobs = prep_jobs()

            def prep_job(m):
                for o, i in jobs[m][0]:
                    last = pe.transpose(o, i, ident[0:i.shape[0], 0:i.shape[0]])
                last.then_inc(prep_tr, 1)

            for m in range(3):
                pe.wait_ge(bank_free[m], N_O)
                prep_job(m)
            head_stats(2 + KD - 2)
            for m in range(3, 6):
                pe.wait_ge(bank_free[m], N_O)
                if m == 4:
                    pe.wait_ge(hnorm, 2)
                prep_job(m)
            head_stats(2 + KD - 1)
            pe.wait_ge(ck_in, 16)
            pe.wait_ge(hroot, 3 * (2 + KD))
            for m in range(6, len(jobs)):
                if m >= 8:
                    pe.wait_ge(prep_dve if (m - 8) % 2 else prep_cp, (m - 8) // 2 + 1)
                prep_job(m)
            pe.wait_ge(prep_cp, len(jobs) // 2)
            pe.wait_ge(prep_dve, len(jobs) // 2)
            pe.wait_ge(hnorm, 2 + KD // 2)

            def scores(i):
                a, e, b = steps[i]
                h0 = HD * e
                if i == NSTEP // 2:
                    pe.wait_ge(hnorm, 2 + KD)
                if b == NB:
                    pe.wait_ge(qs_ready, a + 1)
                if i >= 2:
                    pe.wait_ge(sc_read, i - 1)
                if b < NB:
                    k0 = 0 if b > 0 else WIN
                    for j in range(4):
                        out = ps[:, 2 * (i % 2) + j // 2, (j % 2) * 256 + k0:(j % 2) * 256 + 256]
                        last = pe.matmul(out, qz[h0:h0 + HD, 4 * a + j, b * WIN:(b + 1) * WIN],
                                         kf[h0:h0 + HD, a, (b - 1) * WIN + k0:(b + 1) * WIN], start=True, stop=True)
                else:
                    for r in range(DEC_B):
                        new = ds(SEQ + r * DEC_T, DEC_T)
                        q = convin[h0:h0 + HD, ds(256 * a + 32 * r, 32)]
                        o0 = 32 * (r % 4)
                        c0 = LS * (r // 4)
                        pe.matmul(ps[o0:o0 + 32, 2 * (i % 2), c0:c0 + WIN], q, kct[h0:h0 + HD, a, r * WIN:(r + 1) * WIN],
                                  start=True, stop=True)
                        last = pe.matmul(ps[o0:o0 + 32, 2 * (i % 2), c0 + WIN:c0 + LS], q, kf[h0:h0 + HD, a, new],
                                         start=True, stop=True)
                last.then_inc(sc_ready, 1)

            def transposes(i):
                a, e, b = steps[i]
                pe.wait_ge(p_ready, i + 1)
                if i >= 1:
                    pe.wait_ge(pt_copied, i)
                if b < NB:
                    for h in range(0 if b > 0 else 1, 2):
                        for j in range(4):
                            last = pe.transpose(ps[:, 4 + h, j * P:(j + 1) * P], pb[i % NPB][:, j, h * P:(h + 1) * P],
                                                ident[:, :])
                else:
                    flat = pb[i % NPB][:, :, :].rearrange("p a b -> p (a b)")
                    for h in range(2):
                        pe.transpose(ps[:, 4, h * P:(h + 1) * P], flat[:, h * LS:h * LS + WIN], ident[:, :])
                        last = pe.transpose(ps[0:DEC_T, 5, h * P:(h + 1) * P], flat[:, h * LS + WIN:(h + 1) * LS],
                                            ident[:, :])
                last.then_inc(pt_ready, 1)

            def values(i):
                a, e, b = steps[i]
                h0, g = HD * e, 2 * a + e
                out = 6 + i % 2
                pe.wait_ge(pt_copied, i + 1)
                if i >= 2:
                    pe.wait_ge(o_copied, i - 1)
                col = ds(g * HD, HD)
                if b < NB:
                    for h in range(0 if b > 0 else 1, 2):
                        last = pe.matmul(ps[h0:h0 + HD, out, :], vt[:, b - 1 + h, col], pt[:, h, :],
                                         start=(h == 0 or b == 0), stop=(h == 1))
                else:
                    pe.wait_ge(cv_in, 16)
                    pe.wait_ge(vnew_in, 16 * DEC_B)
                    for r in range(DEC_B):
                        c0 = 32 * r
                        pe.matmul(ps[h0:h0 + HD, out, c0:c0 + 32], cv[:, r, col], pt[:, 0, c0:c0 + 32],
                                  start=True, stop=False)
                        last = pe.matmul(ps[h0:h0 + HD, out, c0:c0 + 32], vnew[:, r, col], pt[0:DEC_T, 1, c0:c0 + 32],
                                         start=False, stop=True)
                last.then_inc(o_ready, 1)

            scores(0)
            scores(1)
            for i in range(NSTEP):
                if i + 2 < NSTEP:
                    scores(i + 2)
                if i >= 1:
                    values(i - 1)
                transposes(i)
            values(NSTEP - 1)
            pe.wait_ge(sc_read, NSTEP)
            pe.wait_ge(pt_copied, NSTEP)
            pe.wait_ge(o_copied, NSTEP)

            unit(N_O, 0, KD, nhi, nlo, z_split(2))
            unit(N_O, 1, KD, nhi, nlo)
            with pe.Fori(1, KD // 2 - 1) as i:
                for s in range(2):
                    unit(N_O + i, s, KD, nhi, nlo)
            for s in range(2):
                unit(N_F1 - 1, s, KD, nhi, nlo, stats_of=3 if s == 1 else None)
            ffn(1, N_F1, 4, 3)
            for m in range(len(state_jobs(1))):
                state_job(1, m)
            pe.wait_ge(fst_cp, STATE0[2])

            for b in range(6):
                pe.wait_ge(bank_free[b], N_END)
            for m, (tt, h) in enumerate(ends):
                if m >= 8:
                    pe.wait_ge(tr_act if m % 2 == 0 else tr_dve,
                               (n_set_act if m % 2 == 0 else n_set_dve) + (m - 8) // 2 + 1)
                w = P if tt < 8 else NS
                for i in range(4):
                    last = pe.transpose(ps[0:w, m % 8, i * P:(i + 1) * P], x[:, 4 * h + i, tt * P:tt * P + w],
                                        ident[:, :])
                last.then_inc(tr_ready, 1)

        @block.scalar
        def _(act):
            def set_up(first, end):
                for m in range(first, end, 2):
                    act.wait_ge(tr_ready, m + 1)
                    view, dst = job_out(setup[m], SET_BANK[m])
                    act.activation(dst, view, ACT.Copy).then_inc(tr_act, 1)

            def prep(n, s, cols, phase=""):
                act.wait_ge(raw_ready[s], raw_count_at(n, phase))
                wait(act, bank_ready[3 * s + 2], n)
                act.activation(whi[s][:, 0:cols], raw[s][:, 0:cols], ACT.Copy).then_inc(hi_ready[s], 1)

            act.wait_ge(const_ready, 4)

            def apart():
                act.wait_ge(const_ready, 4)

            def square(v, k, c):
                act.wait_ge(sq_added, sq_base(v) + 3 * k + c - 2)
                act.activation(t1[:, chunk(c)], x[:, k, chunk(c)], ACT.Square).then_inc(sq_done, 1)

            def root(v, c):
                act.wait_ge(stat_ready, 3 * v + c + 1)
                act.activation(rstd[:, chunk(c)], bank(6 + c % 2, c), ACT.Sqrt, bias=epst[:, 0:1])\
                   .then_inc(stat_sqrt, 1)

            def norm_hi(u, v, chunks, between=None):
                for c in chunks:
                    for k in range(KD):
                        act.wait_ge(xn_mult, 24 * u + 8 * c + k + 1)
                        act.activation(nhi[:, k, chunk(c)], norm_buffer(u, 8 * c + k), ACT.Copy).then_inc(xn_hi, 1)
                        if between:
                            between(k)
                        if k == (3 if v else 5) and c < 2 and v is not None and (v, c) != (0, 0):
                            root(v, c + 1)

                if u > 0 and chunks[-1] == 2:
                    act.wait_ge(xn_lo, lo_base(u + 1))
                    act.wait_ge(xn_lo_pool, lo_base_pool(u + 1))

            def squares_in(c, ks):
                act.wait_ge(tr_act, SET_END[c] // 2)
                act.wait_ge(tr_dve, SET_END[c] // 2)
                for k in ks:
                    i = sum(SQ_ACT[:c]) + k
                    wait(act, sq_added, i - 1 if i >= 2 else 0)
                    act.activation(t1[:, ds((i % 2) * 384, CHUNKS[c][1])], x[:, k, chunk(c)], ACT.Square)\
                       .then_inc(sq_done, 1)

            set_up(0, SET_END[0])
            squares_in(0, range(SQ_ACT[0]))
            set_up(SET_END[0], SET_END[1] - 2)
            root(0, 0)
            set_up(SET_END[1] - 2, SET_END[1])

            def first_chunk_in(k):
                if k == 0:
                    prep(0, 0, KD * P)
                if k < SQ_ACT[1]:
                    squares_in(1, [k])
                if k == SQ_ACT[1]:
                    prep(0, 1, KD * P)
                    root(0, 1)

            norm_hi(0, 0, [0], first_chunk_in)
            set_up(SET_END[1], SET_END[2])
            norm_hi(0, 0, [1], lambda k: squares_in(2, range(SQ_ACT[2])) if k == 3 else None)
            norm_hi(0, 0, [2])
            set_up(SET_END[2], NSET)
            act.wait_ge(sp_ready, 1)
            act.activation(spt[:, 1, :], spt[:, 0, :], ACT.Exp, scale=-1.0).then_inc(sp_exp, 1)

            def evac_conv(s, n, hist, convs, stashes):
                gp, gs = sp_view(convin, hist)
                wait(act, conv_done, convs)
                wait(act, stash_done, stashes)
                for c in range(3):
                    act.wait_ge(bank_ready[3 * s + c], n + 1)
                    lo, w = CHUNKS[c]
                    b = 3 * s + c
                    if c == 2:
                        act.activation(gs[:, :, hist:], requests(ps[:, b, SEQ - lo:w]), ACT.Copy)
                        w = SEQ - lo
                    act.activation(gp[:, hist + lo:hist + lo + w], ps[:, b, 0:w], ACT.Copy).then_inc(bank_free[b], 1)

            def lru_block(c, last):
                for s in range(2):
                    n, kt = 4 * c, 2 * c + s
                    evac_conv(s, n, 3, 2 * kt, kt)
                    prep(n + 1, s, KD * P)
                    act.wait_ge(conv_done, 2 * kt + 2)
                    act.activation(xchi[:, s, :], y[:, :], ACT.Copy).then_inc(xc_hi, 1)
                wait(act, hlast_done, 2 * c)
                wait(act, z_ready, 2 * c)
                for s in range(2):
                    n = 4 * c + 1
                    for ch in range(3):
                        b = 3 * s + ch
                        act.wait_ge(bank_ready[b], n + 1)
                        apart()
                        act.activation(z[:, ds(2 * c + s, 1), chunk(ch)], bank(b, ch).rearrange("p (o t) -> p o t", o=1),
                                       ACT.Gelu_apprx_tanh).then_inc(bank_free[b], 1)
                        if ch == 1:
                            prep(n + 1, s, 2 * P)
                if last:
                    act.wait_ge(bank_ready[5], 4 * c + 2)
                    for k in range(KD - 2):
                        act.wait_ge(z_ready, k + 1)
                        act.activation(nhi[:, k, :], z[:, k, :], ACT.Copy).then_inc(z_hi, 1)
                for m in range(2):
                    n, kt = 4 * c + 2 + m, 2 * c + m
                    for s, t, col in zip(range(2), gate_tiles(c, m), (C_RB, C_IB)):
                        for ch in range(3):
                            b = 3 * s + ch
                            apart()
                            act.wait_ge(bank_ready[b], n + 1)
                            act.activation(t[:, chunk(ch)], bank(b, ch), ACT.Sigmoid,
                                           bias=pcol[:, ds(kt, 1), col]).then_inc(bank_free[b], 1)
                            if ch == 1:
                                prep(n + 1, s, 2 * P if m == 0 else KD * P)
                for m in range(2):
                    n, kt = 4 * c + 2 + m, 2 * c + m
                    t = gate_tiles(c, m)[0]
                    act.wait_ge(bank_free[2], n + 1)
                    apart()
                    act.activation(rstd[:, :], t, ACT.Tanh, scale=sp[:, 0, ds(kt, 1)]).then_inc(tanh_done, 1)
                    apart()
                    act.wait_ge(tanh_done, kt + 1)
                    act.activation(t, t, ACT.Exp, scale=sp[:, 1, ds(kt, 1)]).then_inc(a_ready, 1)
                    act.wait_ge(one_a2, kt + 1)
                    act.activation(y[:, :], y[:, :], ACT.Sqrt).then_inc(root_ready, 1)

            lru_block(0, False)
            with act.Fori(1, LRU_BLOCKS - 1) as c:
                lru_block(c, False)
            lru_block(LRU_BLOCKS - 1, True)
            for k in range(KD - 2, KD):
                act.wait_ge(z_ready, k + 1)
                act.activation(nhi[:, k, :], z[:, k, :], ACT.Copy).then_inc(z_hi, 1)

            def residual(n, i, v, last_cols, phase, last=False, u=None):
                for s in range(2):
                    for c in range(3):
                        if last and s == 1 and c == 1:
                            root(v, 0)
                        if last and s == 1 and c == 2:
                            norm_hi(u, v, [0], lambda k: prep(n + 1, 1, last_cols, phase) if k == 5 else None)
                        act.wait_ge(bank_free[3 * s + c], n + 1)
                        act.wait_ge(sq_added, sq_base(v) + 6 * i + 3 * s + c - 2)
                        apart()
                        act.activation(t1[:, chunk(c)].rearrange("p (o t) -> p o t", o=1),
                                       x[:, ds(2 * i + s, 1), chunk(c)], ACT.Square).then_inc(sq_done, 1)
                    if not (last and s == 1):
                        prep(n + 1, s, last_cols, phase)

            with act.Fori(0, KD // 2 - 1) as i:
                residual(N_OUT + i, i, 1, KD * P, "")
            residual(N_F0 - 1, KD // 2 - 1, 1, KD * P, "", last=True, u=1)
            norm_hi(1, 1, [1, 2])

            def ffn(layer, n0, v, phase):
                def block_(b, last):
                    nb = n0 + b * (FB + KD // 2)

                    def tile(j, next_cols):
                        n = nb + j
                        f = layer * FT + b * FB + j
                        evac_conv(0, n, 2, 2 * (KD + f), KD + f)
                        prep(n + 1, 0, next_cols, phase)
                        act.wait_ge(conv_done, 2 * (KD + f) + 2)
                        act.activation(y[:, :], y[:, :], ACT.Gelu_apprx_tanh).then_inc(gelu_done, 1)
                        for c in range(3):
                            act.wait_ge(bank_free[3 + c], n + 1)
                            apart()
                            act.activation(hhi[:, ds(j, 1), chunk(c)], y[:, chunk(c)].rearrange("p (o t) -> p o t", o=1),
                                           ACT.Copy).then_inc(hhi_done, 1)
                        prep(n + 1, 1, next_cols, phase)

                    with act.Fori(0, FB - 1) as j:
                        tile(j, KD * P)
                    tile(FB - 1, FB * P)
                    nd = nb + FB
                    if last and layer == 0:
                        with act.Fori(0, KD // 2 - 1) as i:
                            residual(nd + i, i, v, FB * P, phase)
                        residual(nd + KD // 2 - 1, KD // 2 - 1, v, KD * P, "", last=True, u=2)
                    else:
                        with act.Fori(0, KD // 2 - 1) as i:
                            for s in range(2):
                                prep(nd + i + 1, s, FB * P, phase)
                        if not last:
                            for s in range(2):
                                prep(nd + KD // 2, s, KD * P, phase)

                with act.Fori(0, NFB - 1) as b:
                    block_(b, False)
                block_(NFB - 1, True)

            def state_copy(layer, m):
                _, view, dst = state_jobs(layer)[m]
                act.wait_ge(fst_tr, STATE0[layer] + m + 1)
                act.activation(dst, view, ACT.Copy).then_inc(fst_cp, 1)

            def states_to_dram(layer):
                act.wait_ge(fst_cp, STATE0[layer + 1])
                act.dma_start(A["ffn_conv_p"][layer, 0], fout[0:2, :]).then_inc(states_out, 16)
                act.dma_start(A["ffn_conv_s"][layer].rearrange("b w d -> (b w) d"), fout[2:18, :])\
                   .then_inc(states_out, 16)
                if layer == 0:
                    for dst, lo, hi in ((A["lru_conv_p"][0, 0], 32, 35),
                                        (A["lru_conv_s"][0].rearrange("b w d -> (b w) d"), 0, 24),
                                        (A["lru_h_p"][0], 35, 36), (A["lru_h_s"][0], 24, 32)):
                        act.dma_start(dst, lout[lo:hi, :]).then_inc(states_out, 16)

            ffn(0, N_F0, 2, "")

            norm_hi(2, 2, [1, 2])

            def head_roots(i):
                for c in range(3):
                    act.wait_ge(hmean, 3 * i + c + 1)
                    if c == 0:
                        wait(act, hnorm, i if i < 3 else i - 1)
                    act.activation(root_buffer(i)[:, chunk(c)], bank(6 + (3 * i + c) % 2, c), ACT.Sqrt, bias=epst[:, 0:1])\
                       .then_inc(hroot, 1)

            def kv_out(m, s, c):
                b = 3 * s + c
                dst = kf[:, s, chunk(c)] if m == 0 else (t1, t2)[s][:, chunk(c)]
                act.wait_ge(bank_ready[b], N_KV + m + 1)
                act.activation(dst, bank(b, c), ACT.Identity, bias=pcol[:, 2 * m + s, C_BKV:C_BKV + 1])\
                   .then_inc(bank_free[b], 1)

            act.wait_ge(strip_mm, 1)
            act.activation(strip_sb2[:, :], ps[0:HEADS, 7, 0:FV], ACT.Copy).then_inc(strip_cp, 1)
            for s in range(2):
                for c in range(3):
                    kv_out(0, s, c)
                prep(N_KV + 1, s, KD * P)
                act.wait_ge(bank_free[3 * s + 2], N_KV + 1)
                if s == 0:
                    act.wait_ge(xn_lo, lo_base(3))
                    act.wait_ge(xn_lo_pool, lo_base_pool(3))
                act.activation((y, ksq)[s][:, :], kf[:, s, :], ACT.Square).then_inc(hsq, 1)
            act.wait_ge(strip_cp, 1)
            src = strip_sb2[:, :].rearrange("h (o v) -> h o v", o=1).broadcast_to([HEADS, P, FV])
            act.dma_start(strip_dram.rearrange("(h r v) -> h r v", h=HEADS, r=P), src).then_inc(strip_out, 16)
            head_roots(0)
            head_roots(1)

            def first_chunk(k):
                if k == 1:
                    for s in range(2):
                        kv_out(1, s, 1)
                elif k == 3:
                    state_copy(0, 0)
                    state_copy(0, 1)
                elif k == 5:
                    kv_out(1, 0, 2)
                    prep(N_Q, 0, KD * P, "q")
                elif k == 7:
                    state_copy(0, 2)
                    state_copy(0, 3)

            for s in range(2):
                kv_out(1, s, 0)
            norm_hi(3, None, [0], first_chunk)
            kv_out(1, 1, 2)
            prep(N_Q, 1, KD * P, "q")
            state_copy(0, 4)
            state_copy(0, 5)

            def second_chunk(k):
                if k == 3:
                    state_copy(0, 6)
                    state_copy(0, 7)

            norm_hi(3, None, [1], second_chunk)
            norm_hi(3, None, [2])
            states_to_dram(0)
            act.wait_ge(states_out, 16 * 6)
            jobs = prep_jobs()

            def prep_out(ms):
                for m in ms:
                    if m % 2 == 0:
                        _, view, dst = jobs[m]
                        act.wait_ge(prep_tr, m + 1)
                        act.activation(dst, view, ACT.Copy).then_inc(prep_cp, 1)

            for t in range(KD):
                n, s = N_Q + t // 2, t % 2
                for c in range(3):
                    b = 3 * s + c
                    act.wait_ge(bank_ready[b], n + 1)
                    act.activation(qz[:, t, chunk(c)], bank(b, c), ACT.Identity, bias=pcol[:, t, C_BQ:C_BQ + 1])\
                       .then_inc(bank_free[b], 1)
                act.wait_ge(bank_free[3 * s + 2], n + 1)
                if t == KD - 1:
                    head_roots(2 + t - 1)
                act.wait_ge(hmean, 3 * (2 + t))
                act.activation(y[:, :], qz[:, t, :], ACT.Square).then_inc(hsq, 1)
                prep(n + 1, s, KD * P, "q" if t < KD - 2 else "o")
                if t < KD - 2:
                    head_roots(2 + t)
            act.wait_ge(strip_out, 16)
            head_roots(2 + KD - 1)
            prep_out(range(len(jobs)))

            def exps(i):
                a, e, b = steps[i]
                st = stat[:, :, 4 * (i % NPB):4 * (i % NPB) + 4]
                act.wait_ge(max_ready, i + 1)
                if b < NB:
                    k0 = 0 if b > 0 else WIN
                    for j in range(4):
                        w = pb[i % NPB][:, j, k0:]
                        act.activation(w, w, ACT.Exp, bias=st[:, 1, j:j + 1], accum_out=st[:, 2, j:j + 1])
                else:
                    flat = pb[i % NPB][:, :, :].rearrange("p a b -> p (a b)")
                    for h in range(2):
                        w = flat[:, h * LS:(h + 1) * LS]
                        act.activation(w, w, ACT.Exp, bias=st[:, 1, h:h + 1], accum_out=st[:, 2, h:h + 1])
                m = 4 if b < NB else 2
                act.activation(st[:, 3, 0:m], st[:, 4, 0:m], ACT.Exp).then_inc(exp_done, 1)

            exps(0)
            for i in range(NSTEP):
                a, e, b = steps[i]
                if i + 1 < NSTEP:
                    exps(i + 1)
                act.wait_ge(pt_ready, i + 1)
                if i >= 1:
                    act.wait_ge(o_ready, i)
                if b < NB:
                    if b > 0:
                        act.activation(pt[:, 0, :], ps[:, 4, :], ACT.Copy)
                    act.activation(pt[:, 1, :], ps[:, 5, :], ACT.Copy).then_inc(pt_copied, 1)
                else:
                    act.activation(pt[:, 0, 0:256], ps[:, 4, 0:256], ACT.Copy)
                    act.activation(pt[0:DEC_T, 1, 0:256], ps[0:DEC_T, 5, 0:256], ACT.Copy).then_inc(pt_copied, 1)
            act.wait_ge(win_out, 16 * (4 + 2 * DEC_B))
            for k in range(KD):
                act.wait_ge(o_copied, NSTEP)
                act.activation(nhi[:, k, :], qz[:, k, :], ACT.Copy).then_inc(z_hi, 1)
            with act.Fori(0, KD // 2 - 1) as i:
                residual(N_O + i, i, 3, KD * P, "o")
            residual(N_O + KD // 2 - 1, KD // 2 - 1, 3, KD * P, "f1", last=True, u=4)
            norm_hi(4, 3, [1, 2])
            ffn(1, N_F1, 4, "f1")
            for m in range(len(state_jobs(1))):
                state_copy(1, m)
            states_to_dram(1)

            for m in range(len(ends)):
                if m % 2 == 0:
                    act.wait_ge(tr_ready, NSET + m + 1)
                    view, dst = end_out(m)
                    act.activation(dst, view, ACT.Copy).then_inc(tr_act, 1)
            act.wait_ge(states_out, 16 * 8)

        @block.vector
        def _(dve):
            seq = Tally(dve, dve_seq)

            dve.memset(ones[:, :], 1.0 / D).then_inc(const_ready, 1)
            dve.memset(epst[:, :], EPS).then_inc(const_ready, 1)
            seq.mark(dve.memset(blockones[:, :], 0.0))
            seq.settle()
            dve.memset(blockones[0:HD, 0:HD], 1.0 / HD)
            dve.memset(blockones[HD:P, HD:P], 1.0 / HD).then_inc(const_ready, 1)
            def set_up(first, end):
                for m in range(first + 1, end, 2):
                    dve.wait_ge(tr_ready, m + 1)
                    view, dst = job_out(setup[m], SET_BANK[m])
                    dve.tensor_copy(dst, view).then_inc(tr_dve, 1)

            def prep(n, s, cols):
                dve.wait_ge(hi_ready[s], n + 1)
                dve.tensor_tensor(wlo[s][:, 0:cols], raw[s][:, 0:cols], whi[s][:, 0:cols].bitcast(F32), ALU.subtract)\
                   .then_inc(lo_ready[s], 1)

            def recip(v, c):
                dve.wait_ge(stat_sqrt, 3 * v + c + 1)
                seq.mark(dve.reciprocal(rstd[:, chunk(c)], rstd[:, chunk(c)]))

            def norm(u, gain, v, chunks, between=None):
                if len(chunks) > 1:
                    for c in chunks:
                        norm(u, gain, v, [c], between)
                    return
                if v and chunks[0] > 0:
                    recip(v, chunks[0])
                c = chunks[0]
                for j in range(KD + 1):
                    i = 8 * c + j
                    if j < KD:
                        if j == 0 and v is not None:
                            seq.settle()
                        if u == 0 and i >= 2:
                            dve.wait_ge(xn_lo, i - 1)
                        elif u > 0 and i >= 4 and i % 2 == 0:
                            dve.wait_ge(xn_lo, lo_base(u) + i // 2 - 1)
                        elif u > 0 and i >= 4:
                            dve.wait_ge(xn_lo_pool, lo_base_pool(u) + i // 2 - 1)
                        dve.scalar_tensor_tensor(norm_buffer(u, i), x[:, j, chunk(c)],
                                                 pcol[:, j, gain:gain + 1], rstd[:, chunk(c)], ALU.mult, ALU.mult)\
                           .then_inc(xn_mult, 1)
                    if j >= 1:
                        k = j - 1
                        if u == 0 or k % 2 == 0:
                            dve.wait_ge(xn_mult, 24 * u + i)
                            dve.wait_ge(xn_hi, 24 * u + i)
                            dve.tensor_tensor(nlo[:, k, chunk(c)], norm_buffer(u, i - 1),
                                              nhi[:, k, chunk(c)].bitcast(F32), ALU.subtract).then_inc(xn_lo, 1)
                        if between:
                            between(k)

            def squares_in(c):
                dve.wait_ge(tr_act, SET_END[c] // 2)
                dve.wait_ge(tr_dve, SET_END[c] // 2)
                wait(dve, stat_ready, c)
                w = CHUNKS[c][1]
                part, total = convin[:, 0:w], convin[:, 384:384 + w]
                for k in range(SQ_ACT[c], KD):
                    seq.mark(dve.tensor_tensor(part if k > SQ_ACT[c] else total, x[:, k, chunk(c)], x[:, k, chunk(c)], ALU.mult))
                    seq.settle()
                    if k > SQ_ACT[c]:
                        ins = dve.tensor_tensor(total, total, part, ALU.add)
                        if k < KD - 1:
                            seq.mark(ins)
                            seq.settle()
                        else:
                            ins.then_inc(sq_dve, 1)

            set_up(0, SET_END[0])
            squares_in(0)
            set_up(SET_END[0], SET_END[1])
            recip(0, 0)

            def first_chunk_in(k):
                if k == 0:
                    prep(0, 0, KD * P)
                elif k == 2:
                    squares_in(1)
                elif k == KD - 1:
                    prep(0, 1, KD * P)

            dve.wait_ge(tr_act, SET_END[1] // 2)
            dve.wait_ge(tr_dve, SET_END[1] // 2)
            norm(0, C_ANORM, 0, [0], first_chunk_in)
            recip(0, 1)
            set_up(SET_END[1], SET_END[2])
            norm(0, C_ANORM, 0, [1], lambda k: squares_in(2) if k == 3 else None)
            recip(0, 2)
            norm(0, C_ANORM, 0, [2])
            set_up(SET_END[2], NSET)
            dve.wait_ge(sq_dve, 3)
            seq.mark(dve.memset(convin[:, 0:CONV_W - 1], 0.0))

            lam = pcol[:, :, C_LAM]
            seq.mark(dve.tensor_scalar(spt[:, 2, :], lam, -1.0, 0.0, ALU.mult, ALU.max))
            seq.mark(dve.tensor_scalar(spt[:, 3, :], lam, 0.0, None, ALU.max))
            seq.settle()
            dve.tensor_tensor(spt[:, 0, :], spt[:, 2, :], spt[:, 3, :], ALU.add).then_inc(sp_ready, 1)
            dve.wait_ge(sp_exp, 1)
            seq.mark(dve.tensor_scalar(spt[:, 0, :], spt[:, 1, :], 2.0, None, ALU.add))
            seq.settle()
            seq.mark(dve.reciprocal(spt[:, 0, :], spt[:, 0, :]))
            seq.settle()
            seq.mark(dve.tensor_tensor(spt[:, 0, :], spt[:, 0, :], spt[:, 1, :], ALU.mult))
            seq.settle()
            seq.mark(dve.tensor_tensor(spt[:, 1, :], spt[:, 0, :], spt[:, 0, :], ALU.mult))
            seq.settle()
            terms = 9
            seq.mark(dve.tensor_scalar(spt[:, 3, :], spt[:, 1, :], 1.0 / (2 * terms + 1), 1.0 / (2 * terms - 1),
                                       ALU.mult, ALU.add))
            seq.settle()
            for i in range(terms - 2, -1, -1):
                seq.mark(dve.tensor_tensor(spt[:, 3, :], spt[:, 3, :], spt[:, 1, :], ALU.mult))
                seq.settle()
                seq.mark(dve.tensor_scalar(spt[:, 3, :], spt[:, 3, :], 1.0 / (2 * i + 1), None, ALU.add))
                seq.settle()
            seq.mark(dve.tensor_tensor(spt[:, 3, :], spt[:, 3, :], spt[:, 0, :], ALU.mult))
            seq.settle()
            seq.mark(dve.scalar_tensor_tensor(spt[:, 3, :], spt[:, 3, :], 2.0, spt[:, 2, :], ALU.mult, ALU.add))
            seq.settle()
            seq.mark(dve.tensor_scalar(sp[:, 0, :], spt[:, 3, :], C_GATE, None, ALU.mult))
            seq.mark(dve.tensor_scalar(sp[:, 1, :], spt[:, 3, :], -C_GATE, None, ALU.mult))
            seq.settle()


            def conv(taps, hist, w, b, hists, free_banks, n, before):
                gp, gs = sp_view(convin, hist)
                before()
                for bk in free_banks:
                    dve.wait_ge(bank_free[bk], n + 1)
                dve.wait_ge(hist_ready, hists)
                yp, ys = y[:, 0:SEQ], requests(y[:, SEQ:T])
                for i in range(taps):
                    t = taps - 1 - i
                    for o, g, m in ((yp, gp[:, t:t + SEQ], "p"), (ys, gs[:, :, t:t + DEC_T], "s")):
                        if i == 0:
                            ins = dve.tensor_scalar(o, g, w(t), b, ALU.mult, ALU.add)
                        else:
                            ins = dve.scalar_tensor_tensor(o, g, w(t), o, ALU.mult, ALU.add)
                        if i < taps - 1:
                            seq.mark(ins)
                        else:
                            ins.then_inc(conv_done, 1)
                    if i < taps - 1:
                        seq.settle()

            def lru_block(c, last, start):
                seq.at = start
                for s in range(2):
                    n, kt = 4 * c, 2 * c + s
                    wait(dve, xc_lo, kt)
                    conv(CONV_W, 3, lambda t: pcol[:, ds(kt, 1), C_CONVW + t], pcol[:, ds(kt, 1), C_CONVB], kt + 1,
                         (3 * s, 3 * s + 1, 3 * s + 2), n, lambda: prep(n + 1, s, KD * P))
                    dve.wait_ge(xc_hi, kt + 1)
                    dve.tensor_tensor(xclo[:, s, :], y[:, :], xchi[:, s, :].bitcast(F32), ALU.subtract)\
                       .then_inc(xc_lo, 1)
                for s in range(2):
                    prep(4 * c + 2, s, 2 * P)
                for m in range(2):
                    for s in range(2):
                        prep(4 * c + 3 + m, s, 2 * P if m == 0 else KD * P)
                for m in range(2):
                    n, kt = 4 * c + 2 + m, 2 * c + m
                    ta, tb = gate_tiles(c, m)
                    dve.wait_ge(xc_lo, 2 * c + 2)
                    seq.mark(dve.tensor_tensor(y[:, :], xchi[:, m, :].bitcast(F32), xclo[:, m, :].bitcast(F32), ALU.add))
                    seq.settle()
                    dve.wait_ge(bank_free[5], n + 1)
                    seq.mark(dve.tensor_tensor(tb, tb, y[:, :], ALU.mult))
                    seq.settle()
                    dve.wait_ge(a_ready, kt + 1)
                    seq.mark(dve.tensor_tensor(y[:, :], ta, ta, ALU.mult))
                    seq.settle()
                    dve.scalar_tensor_tensor(y[:, :], y[:, :], 1.0, rstd[:, :], ALU.add, ALU.mult).then_inc(one_a2, 1)
                    first1, first2 = (requests(t[:, SEQ:T])[:, :, 0] for t in (ta, tb))
                    h0 = pcol[:, ds(kt, 1), C_SH:C_SH + DEC_B].rearrange("p o b -> p (o b)")
                    seq.mark(dve.tensor_tensor(h0a[:, :], first1, h0, ALU.mult))
                    seq.settle()
                    seq.mark(dve.tensor_scalar(first1, first1, 0.0, None, ALU.mult))
                    dve.wait_ge(root_ready, kt + 1)
                    seq.mark(dve.tensor_tensor(tb, tb, y[:, :], ALU.mult))
                    seq.settle()
                    seq.mark(dve.tensor_tensor(first2, first2, h0a[:, :], ALU.add))
                    seq.settle()
                    dve.tensor_tensor_scan(tb, ta, tb, 0.0, ALU.mult, ALU.add).then_inc(scan_done, 1)
                    if last:
                        dve.wait_ge(scan_done, kt + 1)
                        dve.wait_ge(z_ready, kt)
                        zt = z[:, ds(kt, 1), :].rearrange("p o t -> p (o t)")
                        dve.tensor_tensor(zt, zt, tb, ALU.mult).then_inc(z_ready, 1)

            start = seq.at
            per = 2 * 2 * (CONV_W - 1) + 2 * 7
            lru_block(0, False, start)
            with dve.Fori(1, LRU_BLOCKS - 1) as c:
                lru_block(c, False, start + c * per)
            lru_block(LRU_BLOCKS - 1, True, start + (LRU_BLOCKS - 1) * per)
            assert seq.at == start + LRU_BLOCKS * per, (seq.at, start, per)
            for k in range(KD - 2, KD):
                dve.wait_ge(z_ready, k + 1)
                dve.wait_ge(z_hi, k + 1)
                dve.wait_ge(hlast_done, KD)
                dve.tensor_tensor(nlo[:, k, :], z[:, k, :], nhi[:, k, :].bitcast(F32), ALU.subtract).then_inc(z_lo, 1)

            def residual(n, i, next_cols, bias_col=None, last=False, v=None, u=None, gain=None):
                for s in range(2):
                    for c in range(3):
                        if v is not None and s == 1 and c == 2:
                            recip(v, 0)
                            if v == 3:
                                dve.wait_ge(hnorm, 2 + KD)
                            else:
                                dve.wait_ge(conv_done, 2 * (KD + (v - 1) * FT))
                                dve.wait_ge(stash_done, KD + (v - 1) * FT)
                            norm(u, gain, v, [0], lambda k: prep(n + 1, 1, next_cols) if k == KD - 1 else None)
                        b = 3 * s + c
                        dve.wait_ge(bank_ready[b], n + 1)
                        xt = x[:, ds(2 * i + s, 1), chunk(c)].rearrange("p o t -> p (o t)")
                        if bias_col is None:
                            ins = dve.tensor_tensor(xt, bank(b, c), xt, ALU.add)
                        else:
                            ins = dve.scalar_tensor_tensor(xt, bank(b, c), pcol[:, ds(2 * i + s, 1), bias_col], xt,
                                                           ALU.add, ALU.add)
                        ins.then_inc(bank_free[b], 1)
                    if not last and not (v is not None and s == 1):
                        prep(n + 1, s, next_cols)

            with dve.Fori(0, KD // 2 - 1) as i:
                residual(N_OUT + i, i, KD * P)
            residual(N_F0 - 1, KD // 2 - 1, KD * P, v=1, u=1, gain=C_FN)
            norm(1, C_FN, 1, [1, 2])

            FT_MARKS = 2 * (FFN_W - 1)

            def ffn(layer, n0):
                start = seq.at

                def block_(b):
                    nb = n0 + b * (FB + KD // 2)

                    def tile(j, next_cols):
                        n = nb + j
                        f = b * FB + j
                        g = layer * FT + f
                        seq.at = start + f * FT_MARKS
                        col = 20 * layer
                        conv(FFN_W, 2, lambda t: fcol[:, ds(f, 1), col + F_W + t], fcol[:, ds(f, 1), col + F_B],
                             KD + g + 1, (0, 1, 2), n, lambda: prep(n + 1, 0, next_cols))
                        dve.wait_ge(gelu_done, g + 1)
                        for c in range(3):
                            dve.wait_ge(bank_ready[3 + c], n + 1)
                            dve.tensor_tensor(y[:, chunk(c)], bank(3 + c, c), y[:, chunk(c)], ALU.mult)\
                               .then_inc(bank_free[3 + c], 1)
                        for c in range(3):
                            dve.wait_ge(bank_free[3 + c], n + 1)
                            dve.wait_ge(hhi_done, 3 * g + c + 1)
                            ht = hhi[:, ds(j, 1), chunk(c)].rearrange("p o t -> p (o t)").bitcast(F32)
                            lt = hlo[:, ds(j, 1), chunk(c)].rearrange("p o t -> p (o t)")
                            dve.tensor_tensor(lt, y[:, chunk(c)], ht, ALU.subtract).then_inc(hlo_done, 1)
                        prep(n + 1, 1, next_cols)
                        dve.wait_ge(const_ready, 4)
                        dve.wait_ge(hlo_done, 3 * g + 3)

                    with dve.Fori(0, FB - 1) as j:
                        tile(j, KD * P)
                    tile(FB - 1, FB * P)
                    nd = nb + FB
                    with dve.Fori(0, KD // 2 - 1) as i:
                        residual(nd + i, i, FB * P)
                    return nd + KD // 2 - 1

                with dve.Fori(0, NFB - 1) as b:
                    residual(block_(b), KD // 2 - 1, KD * P)
                nd = block_(NFB - 1)
                seq.at = start + FT * FT_MARKS
                residual(nd, KD // 2 - 1, KD * P, last=(layer == 1), v=2 if layer == 0 else None, u=2,
                         gain=C_KVN)

            ffn(0, N_F0)
            dve.memset(strip_in_sb[BUCKETS:BUCKETS + 1, FV:FV + HEADS], 1.0).then_inc(strip_one, 1)
            norm(2, C_KVN, 2, [1, 2])

            def head_norm(i, tile_, gain):
                root = root_buffer(i)
                for c in range(3):
                    dve.wait_ge(hroot, 3 * i + c + 1)
                    seq.mark(dve.reciprocal(root[:, chunk(c)], root[:, chunk(c)]))
                seq.settle()
                dve.scalar_tensor_tensor(tile_, tile_, qkn[:, gain:gain + 1], root[:, 0:T], ALU.mult, ALU.mult)\
                   .then_inc(hnorm, 1)

            for s in range(2):
                prep(N_KV + 1, s, KD * P)
            for s in range(2):
                head_norm(s, kf[:, s, :], 1)
            dve.wait_ge(hmean, 3)
            dve.wait_ge(hnorm, 2)
            for c in range(3):
                for s in range(2):
                    dve.wait_ge(bank_ready[3 * s + c], N_Q)
                norm(3, C_BN, None, [c], lambda k: prep(N_Q, 0, KD * P) if (c, k) == (0, 6) else None)
                if c == 0:
                    prep(N_Q, 1, KD * P)
            jobs = prep_jobs()
            for t in range(KD):
                if t == KD - 1:
                    head_norm(2 + t - 1, qz[:, t - 1, :], 0)
                prep(N_Q + t // 2 + 1, t % 2, KD * P)
                if t < KD - 2:
                    head_norm(2 + t, qz[:, t, :], 0)
            dve.wait_ge(strip_out, 16)
            for m in range(1, len(jobs), 2):
                _, view, dst = jobs[m]
                dve.wait_ge(prep_tr, m + 1)
                dve.tensor_copy(dst, view).then_inc(prep_dve, 1)

            def before_exp(i):
                a, e, b = steps[i]
                g = 2 * a + e
                st = stat[:, :, 4 * (i % NPB):4 * (i % NPB) + 4]
                dve.wait_ge(sc_ready, i + 1)
                if i >= NPB:
                    dve.wait_ge(pt_ready, i - NPB + 1)
                if i % (NB + 1) == 0:
                    dve.wait_ge(bias_in[g], 16)
                if i == NB:
                    dve.wait_ge(sbias_in, 16 * 16)
                if i == 2:
                    dve.wait_ge(hmean, 3 * (2 + KD))
                if b < NB:
                    m, k0 = 4, (0 if b > 0 else WIN)
                    sc = ps[:, 2 * (i % 2):2 * (i % 2) + 2, :].rearrange("p a (j s) -> p (a j) s", j=2)[:, :, k0:]
                    w = pb[i % NPB][:, :, k0:]
                    bs = bias[:, 4 * g:4 * g + 4, k0:]
                    sk = sinkb[:, 4 * g:4 * g + 4]
                    dve.scalar_tensor_tensor(w, sc, SCALE, bs, ALU.mult, ALU.add).then_inc(sc_read, 1)
                else:
                    m = 2
                    w = pb[i % NPB][:, :, :].rearrange("p a b -> p (a b)")[:, 0:2 * LS].rearrange("p (h s) -> p h s", h=2)
                    for h in range(2):
                        ins = dve.scalar_tensor_tensor(w[:, h, :], ps[:, 2 * (i % 2), h * LS:(h + 1) * LS], SCALE,
                                                       sbias[:, g, :], ALU.mult, ALU.add)
                    ins.then_inc(sc_read, 1)
                dve.wait_ge(sc_read, i + 1)
                seq.mark(dve.tensor_reduce(st[:, 0, 0:m], w, AX_X, ALU.max))
                if i >= 1:
                    after_exp(i - 1)
                seq.settle()
                if b < NB:
                    seq.mark(dve.tensor_tensor(st[:, 0, 0:m], st[:, 0, 0:m], sk, ALU.max))
                    seq.settle()
                    seq.mark(dve.tensor_tensor(st[:, 4, 0:m], sk, st[:, 0, 0:m], ALU.subtract))
                else:
                    seq.mark(dve.tensor_scalar(st[:, 0, 0:m], st[:, 0, 0:m], sinks_s[:, g:g + 1], None, ALU.max))
                    seq.settle()
                    seq.mark(dve.tensor_scalar(st[:, 4, 0:m], st[:, 0, 0:m], -1.0, sinks_s[:, g:g + 1], ALU.mult,
                                               ALU.add))
                dve.tensor_scalar(st[:, 1, 0:m], st[:, 0, 0:m], -1.0, None, ALU.mult).then_inc(max_ready, 1)

            def after_exp(i):
                a, e, b = steps[i]
                st = stat[:, :, 4 * (i % NPB):4 * (i % NPB) + 4]
                m = 4 if b < NB else 2
                dve.wait_ge(exp_done, i + 1)
                seq.mark(dve.tensor_tensor(st[:, 5, 0:m], st[:, 2, 0:m], st[:, 3, 0:m], ALU.add))
                seq.settle()
                dve.reciprocal(st[:, 6, 0:m], st[:, 5, 0:m]).then_inc(inv_ready, 1)

            def take_out(i):
                a, e, b = steps[i]
                h0 = HD * e
                dve.wait_ge(o_ready, i + 1)
                src = ps[h0:h0 + HD, 6 + i % 2, :]
                if b < NB:
                    dst = qz[h0:h0 + HD, 4 * a:4 * a + 4, b * WIN:(b + 1) * WIN]
                    dve.tensor_copy(dst, src.rearrange("p (j q) -> p j q", j=4)).then_inc(o_copied, 1)
                else:
                    dst = qz[h0:h0 + HD, 4 * a:4 * a + 4, SEQ:T].rearrange("p j (r t) -> p j r t", r=DEC_B)
                    dve.tensor_copy(dst, src[:, 0:32 * DEC_B].rearrange("p (r j t) -> p j r t", r=DEC_B, j=4))\
                       .then_inc(o_copied, 1)

            def request_queries(a):
                src = qz[:, 4 * a:4 * a + 4, SEQ:T].rearrange("p j (r t) -> p r j t", r=DEC_B)
                dst = convin[:, 256 * a:256 * a + 256].rearrange("p (r j t) -> p r j t", r=DEC_B, j=4)
                dve.tensor_copy(dst, src).then_inc(qs_ready, 1)

            dve.wait_ge(hnorm, 1 + KD)
            request_queries(0)
            dve.wait_ge(sink_in, 16 * 17)

            def last_query_tile(i):
                t = 2 + KD - 1
                if i < 3:
                    dve.wait_ge(hroot, 3 * t + i + 1)
                    seq.mark(dve.reciprocal(root_buffer(t)[:, chunk(i)], root_buffer(t)[:, chunk(i)]))
                elif i == 3:
                    seq.settle()
                    dve.scalar_tensor_tensor(qz[:, KD - 1, :], qz[:, KD - 1, :], qkn[:, 0:1], root_buffer(t)[:, 0:T],
                                             ALU.mult, ALU.mult).then_inc(hnorm, 1)
                elif i == 4:
                    dve.wait_ge(hnorm, 2 + KD)
                    request_queries(1)

            before_exp(0)
            for i in range(NSTEP):
                if i + 1 < NSTEP:
                    before_exp(i + 1)
                else:
                    after_exp(i)
                if i >= 1:
                    last_query_tile(i - 1)
                if i >= 2:
                    take_out(i - 2)
            take_out(NSTEP - 2)
            take_out(NSTEP - 1)
            for k in range(KD):
                dve.wait_ge(z_hi, KD + k + 1)
                dve.tensor_tensor(nlo[:, k, :], qz[:, k, :], nhi[:, k, :].bitcast(F32), ALU.subtract).then_inc(z_lo, 1)
            with dve.Fori(0, KD // 2 - 1) as i:
                residual(N_O + i, i, KD * P, bias_col=C_BO)
            residual(N_F1 - 1, KD // 2 - 1, KD * P, bias_col=C_BO, v=3, u=4, gain=C_FN + 1)
            norm(4, C_FN + 1, 3, [1, 2])
            ffn(1, N_F1)
            for m in range(len(ends)):
                if m % 2 == 1:
                    dve.wait_ge(tr_ready, NSET + m + 1)
                    view, dst = end_out(m)
                    dve.tensor_copy(dst, view).then_inc(tr_dve, 1)

        @block.gpsimd
        def _(pool):
            seq = Tally(pool, pool_seq)
            seq.mark(pool.memset(ident[:, :], 0.0))
            seq.settle()
            pool.affine_select(out=ident[:, :], in_=ident[:, :], compare_op=ALU.not_equal, fill=1.0, base=0,
                               pattern=[[-1, P]], channel_multiplier=1).then_inc(const_ready, 1)

            def add(v, k, c):
                pool.wait_ge(sq_done, sq_base(v) + 3 * k + c + 1)
                pool.wait_ge(sq_added, sq_base(v) + 3 * k + c - 2)
                pool.tensor_tensor(t2[:, chunk(c)], t2[:, chunk(c)], t1[:, chunk(c)], ALU.add).then_inc(sq_added, 1)

            def norm_lo(u, c):
                for k in range(1, KD, 2):
                    pool.wait_ge(xn_mult, 24 * u + 8 * c + k + 1)
                    pool.wait_ge(xn_hi, 24 * u + 8 * c + k + 1)
                    pool.tensor_tensor(nlo[:, k, chunk(c)], norm_buffer(u, 8 * c + k),
                                       nhi[:, k, chunk(c)].bitcast(F32), ALU.subtract).then_inc(xn_lo_pool, 1)

            def bias_table():
                pool.dma_start(strip_in_sb[0:BUCKETS, FV:FV + HEADS], A["rel_bias"]).then_inc(strip_in, 16)
                pool.dma_start(strip_in_sb[:, 0:FV], A["onehot"]).then_inc(strip_in, 16)

            def sum_squares(v, u):
                for c in range(3):
                    seq.mark(pool.memset(t2[:, chunk(c)], 0.0))
                seq.settle()
                with pool.Fori(0, KD - 1) as k:
                    for c in range(3):
                        add(v, k, c)
                add(v, KD - 1, 0)
                add(v, KD - 1, 1)
                norm_lo(u, 0)
                add(v, KD - 1, 2)
                if v == 2:
                    bias_table()
                norm_lo(u, 1)
                norm_lo(u, 2)

            for i, (c, k) in enumerate((c, k) for c in range(3) for k in range(SQ_ACT[c])):
                t = t1[:, ds((i % 2) * 384, CHUNKS[c][1])]
                pool.wait_ge(sq_done, i + 1)
                if k == 0:
                    pool.tensor_copy(t2[:, chunk(c)], t).then_inc(sq_added, 1)
                else:
                    pool.wait_ge(sq_added, i)
                    pool.tensor_tensor(t2[:, chunk(c)], t2[:, chunk(c)], t, ALU.add).then_inc(sq_added, 1)
            pool.wait_ge(tr_act, n_set_act)
            pool.wait_ge(tr_dve, n_set_dve)

            def history(hist, src, convs, stashes):
                _, gs = sp_view(convin, hist)
                wait(pool, conv_done, convs)
                wait(pool, stash_done, stashes)
                pool.tensor_copy(gs[:, :, 0:hist], src.rearrange("p o (b w) -> p (o b) w", b=DEC_B))\
                    .then_inc(hist_ready, 1)

            def new_state(hist, dst_p, dst_s, b, n):
                gp, gs = sp_view(convin, hist)
                pool.wait_ge(bank_free[b], n + 1)
                pool.tensor_copy(dst_p, gp[:, SEQ:SEQ + hist].rearrange("p (o w) -> p o w", o=1))
                pool.tensor_copy(dst_s.rearrange("p o (b w) -> p (o b) w", b=DEC_B), gs[:, :, DEC_T:])\
                    .then_inc(stash_done, 1)

            def lru_block(c, last):
                for s in range(2):
                    kt = 2 * c + s
                    history(3, pcol[:, ds(kt, 1), C_SCONV:C_SCONV + 24], 2 * kt, kt)
                    pool.wait_ge(hist_ready, kt + 1)
                    new_state(3, lstash[:, ds(kt, 1), 32:35], lstash[:, ds(kt, 1), 0:24], 3 * s + 2, 4 * c)
                if last:
                    for k in range(KD - 2):
                        pool.wait_ge(z_hi, k + 1)
                        pool.tensor_tensor(nlo[:, k, :], z[:, k, :], nhi[:, k, :].bitcast(F32), ALU.subtract)\
                            .then_inc(z_lo_pool, 1)
                for m in range(2):
                    kt = 2 * c + m
                    h = gate_tiles(c, m)[1]
                    pool.wait_ge(scan_done, kt + 1)
                    if not last:
                        zt = z[:, ds(kt, 1), :].rearrange("p o t -> p (o t)")
                        pool.tensor_tensor(zt, zt, h, ALU.mult).then_inc(z_ready, 1)
                    pool.tensor_copy(lstash[:, ds(kt, 1), 35:36], h[:, SEQ - 1:SEQ].rearrange("p (o t) -> p o t", o=1))
                    pool.tensor_copy(lstash[:, ds(kt, 1), 24:32].rearrange("p o b -> p (o b)"),
                                     requests(h[:, SEQ:T])[:, :, DEC_T - 1]).then_inc(hlast_done, 1)

            lru_block(0, False)
            with pool.Fori(1, LRU_BLOCKS - 1) as c:
                lru_block(c, False)
            lru_block(LRU_BLOCKS - 1, True)

            def ffn(layer):
                base = layer * FT
                with pool.Fori(0, FT) as f:
                    g = base + f
                    history(2, fcol[:, ds(f, 1), 20 * layer + F_S:20 * layer + F_S + 16], 2 * (KD + g), KD + g)
                    _, gs = sp_view(convin, 2)
                    gp, _ = sp_view(convin, 2)
                    pool.wait_ge(conv_done, 2 * (KD + g) + 2)
                    pool.tensor_copy(fstash[:, ds(f, 1), 0:2], gp[:, SEQ:SEQ + 2].rearrange("p (o w) -> p o w", o=1))
                    pool.tensor_copy(fstash[:, ds(f, 1), 2:18].rearrange("p o (b w) -> p (o b) w", b=DEC_B),
                                     gs[:, :, DEC_T:]).then_inc(stash_done, 1)

            pool.wait_ge(z_ready, KD)
            pool.wait_ge(hlast_done, KD)
            sum_squares(1, 1)
            ffn(0)
            sum_squares(2, 2)
            for c in range(3):
                norm_lo(3, c)
            for i in range(NSTEP):
                a, e, b = steps[i]
                m = 4 if b < NB else 2
                inv = stat[:, 6, 4 * (i % NPB):4 * (i % NPB) + m].rearrange("p (j o) -> p j o", o=1)
                if b < NB:
                    w = pb[i % NPB][:, :, (0 if b > 0 else WIN):]
                else:
                    w = pb[i % NPB][:, :, :].rearrange("p a b -> p (a b)")[:, 0:2 * LS].rearrange("p (h s) -> p h s", h=2)
                pool.wait_ge(inv_ready, i + 1)
                pool.tensor_tensor(w, w, inv.broadcast_to([P, m, w.shape[2]]), ALU.mult).then_inc(p_ready, 1)
            pool.wait_ge(z_hi, KD + 1)
            pool.wait_ge(o_copied, NSTEP)
            sum_squares(3, 4)
            pool.memset(convin[:, 0:FFN_W - 1], 0.0)
            pool.wait_ge(fst_cp, STATE0[1])
            ffn(1)


def onehot_strip():
    dist = (2 * WIN - 1) - np.arange(FV)
    exact = BUCKETS // 2
    d = np.maximum(dist, 0)
    df = np.maximum(d, 1).astype(np.float32)
    large = exact + (np.log(df / exact) / np.float32(np.log(WIN / exact)) * (BUCKETS - exact)).astype(np.int32)
    bucket = np.where(d < exact, d, np.minimum(large, BUCKETS - 1))
    valid = (dist >= 0) & (dist < WIN)
    rows = np.zeros((BUCKETS + 1, FV), np.float32)
    rows[bucket[valid], np.arange(FV)[valid]] = 1.0
    rows[BUCKETS, ~valid] = NEG
    return rows


_OUTS = [("y_prompt", (1, SEQ, D)), ("y_sample", (DEC_B, DEC_T, D)), ("lru_h_p", (1, 1, D)),
         ("lru_conv_p", (1, 1, CONV_W - 1, D)), ("ffn_conv_p", (2, 1, FFN_W - 1, D_FF)),
         ("k_win_p", (1, WIN, KV_HEADS, HD)), ("v_win_p", (1, WIN, KV_HEADS, HD)), ("lru_h_s", (1, DEC_B, D)),
         ("lru_conv_s", (1, DEC_B, CONV_W - 1, D)), ("ffn_conv_s", (2, DEC_B, FFN_W - 1, D_FF)),
         ("k_win_s", (DEC_B, WIN, KV_HEADS, HD)), ("v_win_s", (DEC_B, WIN, KV_HEADS, HD))]


def kernel(**inputs):
    import numpy as _np
    import concourse.bacc as _bacc
    from concourse import mybir as _mybir
    from concourse.bass_utils import run_bass_kernel_spmd as _run

    nc = _bacc.Bacc("TRN2", target_bir_lowering=False, num_devices=1)
    arrays, A = {}, {}
    for name, a in [*inputs.items(), ("onehot", onehot_strip())]:
        a = _np.ascontiguousarray(a)
        arrays[f"in_{name}"] = a
        A[name] = nc.dram_tensor(f"in_{name}", a.shape, _mybir.dt.from_np(a.dtype), kind="ExternalInput").ap()
    for name, shape in _OUTS:
        A[name] = nc.dram_tensor(f"out_{name}", shape, _mybir.dt.float32, kind="ExternalOutput").ap()
    build(nc, A)
    r = _run(nc, [arrays], core_ids=[0])
    return tuple(r.results[0][f"out_{name}"] for name, _ in _OUTS)
```
